# Optimizing a Trainium2 kernel written in Bass

```python
import math
import jax, jax.numpy as jnp
from jax import lax
import numpy as np

D_MODEL = 1024
BATCH = 1
SEQ = 512
DEPTH = 2

N_EVEN = (DEPTH + 1) // 2
N_ODD = DEPTH // 2
D_FF = 2816
MIX_WIDTH = D_MODEL
HALF = MIX_WIDTH // 2
CONV_WIDTH = 4
RG_WIDTH = HALF
RG_BLOCKS = 8
RG_BLK = RG_WIDTH // RG_BLOCKS
RG_C = 8.0
ML_HEADS = 4
ML_DH = HALF // ML_HEADS
ML_CHUNK = 64
ML_NORM_EPS = 1e-6
RK_WIDTH = HALF
RK_HEADS = 8
RK_DH = RK_WIDTH // RK_HEADS
RK_DECAY_LORA = 32
RK_A_LORA = 32
RK_G_LORA = 64
RK_NORM_EPS = 64e-5
GLA_HEADS = 4
GLA_DK = 64
GLA_DV = HALF // GLA_HEADS
GLA_GATE_LORA = 16
GLA_TAU = 16.0
GLA_CHUNK = 64
GLA_NORM_EPS = 1e-5
DEEPNORM_ALPHA = (2.0 * DEPTH) ** 0.25
DEEPNORM_BETA = (8.0 * DEPTH) ** -0.25
LN_EPS = 1e-5

EVEN_SIZES = (RG_WIDTH, RG_WIDTH, 2 * HALF, HALF, HALF, 2 * ML_HEADS)
EVEN_IN = sum(EVEN_SIZES)
RK_SIZES = (RK_WIDTH, RK_WIDTH, RK_WIDTH, RK_DECAY_LORA, RK_A_LORA, RK_G_LORA)
RK_IN = sum(RK_SIZES)
GLA_SIZES = (GLA_HEADS * GLA_DK, GLA_HEADS * GLA_DK, HALF, GLA_GATE_LORA, HALF)
GLA_IN = sum(GLA_SIZES)
ODD_IN = RK_IN + GLA_IN


def split_cols(p, sizes):
    return jnp.split(p, [int(s) for s in np.cumsum(sizes)[:-1]], axis=-1)

def layer_norm(x, g, b):
    xf = x.astype(jnp.float32)
    mu = jnp.mean(xf, -1, keepdims=True)
    var = jnp.mean(jnp.square(xf - mu), -1, keepdims=True)
    return ((xf - mu) * lax.rsqrt(var + LN_EPS) * g + b).astype(x.dtype)

def head_norm(h, g, b, eps):
    mu = jnp.mean(h, -1, keepdims=True)
    var = jnp.mean(jnp.square(h - mu), -1, keepdims=True)
    hn = ((h - mu) * lax.rsqrt(var + eps)).reshape(h.shape[0], h.shape[1], -1)
    hn = hn * g
    if b is not None:
        hn = hn + b
    return hn

def swiglu_ffn(x, wi, wo):
    gate, up = jnp.split(x @ wi, 2, axis=-1)
    return (jax.nn.silu(gate) * up) @ wo

def causal_depthwise_conv(t, w, b):
    S = t.shape[1]
    width = w.shape[0]
    tp = jnp.pad(t, ((0, 0), (width - 1, 0), (0, 0)))
    out = b
    for j in range(width):
        out = out + w[j] * tp[:, j:j + S]
    return out

def token_shift(t, mu):
    prev = jnp.pad(t, ((0, 0), (1, 0), (0, 0)))[:, :-1]
    return t + mu * (prev - t)

def linear_scan(a, b):
    def combine(l, r):
        a_l, b_l = l
        a_r, b_r = r
        return a_l * a_r, a_r * b_l + b_r
    _, h = lax.associative_scan(combine, (a, b), axis=1)
    return h

def to_chunks(t, c):
    B, S = t.shape[:2]
    t = t.reshape(B, S // c, c, *t.shape[2:])
    return jnp.moveaxis(jnp.moveaxis(t, 1, 0), 3, 2)

def from_chunks(t):
    t = jnp.moveaxis(jnp.moveaxis(t, 2, 3), 0, 1)
    return t.reshape(t.shape[0], t.shape[1] * t.shape[2], *t.shape[3:])

def rg_lru_mixer(xr, xg, conv_w, conv_b, wa, wx, ba, bx, lam):
    B, S, W = xr.shape
    u = causal_depthwise_conv(xr, conv_w, conv_b)
    ub = u.reshape(B, S, RG_BLOCKS, RG_BLK)
    r = jax.nn.sigmoid(jnp.einsum('bsnc,ncd->bsnd', ub, wa).reshape(B, S, W) + ba)
    i = jax.nn.sigmoid(jnp.einsum('bsnc,ncd->bsnd', ub, wx).reshape(B, S, W) + bx)
    log_a = -RG_C * r * jax.nn.softplus(-lam)
    a = jnp.exp(log_a)
    b = jnp.sqrt(-jnp.expm1(2.0 * log_a)) * (i * u)
    h = linear_scan(a, b)
    return h * jax.nn.gelu(xg)

def mlstm_mixer(qk, v, o, if_pre, conv_w, conv_b, i_bias, f_bias, norm_g):
    B, S, _ = v.shape
    qk = jax.nn.silu(causal_depthwise_conv(qk, conv_w, conv_b))
    q, k = jnp.split(qk, 2, axis=-1)
    q = q.reshape(B, S, ML_HEADS, ML_DH) * (ML_DH ** -0.5)
    k = k.reshape(B, S, ML_HEADS, ML_DH)
    v = v.reshape(B, S, ML_HEADS, ML_DH)
    i_pre = if_pre[..., :ML_HEADS] + i_bias
    log_f = jax.nn.log_sigmoid(if_pre[..., ML_HEADS:] + f_bias)
    causal = jnp.tril(jnp.ones((ML_CHUNK, ML_CHUNK), bool))

    def step(carry, inp):
        c_st, n_st, m = carry
        qc, kc, vc, ic, fc = inp
        bcum = jnp.cumsum(fc, axis=-1)
        d = jnp.where(causal, bcum[..., :, None] - bcum[..., None, :] + ic[..., None, :], -jnp.inf)
        inter = bcum + m[..., None]
        m_t = jnp.maximum(inter, jnp.max(d, -1))
        w_intra = jnp.exp(d - m_t[..., None])
        w_inter = jnp.exp(inter - m_t)
        s = jnp.einsum('bhid,bhjd->bhij', qc, kc) * w_intra
        num = jnp.einsum('bhij,bhje->bhie', s, vc) + w_inter[..., None] * jnp.einsum('bhid,bhde->bhie', qc, c_st)
        den = jnp.sum(s, -1) + w_inter * jnp.einsum('bhid,bhd->bhi', qc, n_st)
        h = num / jnp.maximum(jnp.abs(den), jnp.exp(-m_t))[..., None]
        b_last = bcum[..., -1]
        g = b_last[..., None] - bcum + ic
        m_new = jnp.maximum(b_last + m, jnp.max(g, -1))
        wk = jnp.exp(g - m_new[..., None])
        decay = jnp.exp(b_last + m - m_new)
        c_st = decay[..., None, None] * c_st + jnp.einsum('bhc,bhcd,bhce->bhde', wk, kc, vc)
        n_st = decay[..., None] * n_st + jnp.einsum('bhc,bhcd->bhd', wk, kc)
        return (c_st, n_st, m_new), h

    init = (jnp.zeros((B, ML_HEADS, ML_DH, ML_DH), jnp.float32),
            jnp.zeros((B, ML_HEADS, ML_DH), jnp.float32),
            jnp.zeros((B, ML_HEADS), jnp.float32))
    xs = (to_chunks(q, ML_CHUNK), to_chunks(k, ML_CHUNK), to_chunks(v, ML_CHUNK),
          to_chunks(i_pre, ML_CHUNK), to_chunks(log_f, ML_CHUNK))
    _, h = lax.scan(step, init, xs)
    h = from_chunks(h)
    return head_norm(h, norm_g, None, ML_NORM_EPS) * jax.nn.sigmoid(o)

def rwkv7_mixer(p, mu, w0, wB, a0, aB, gB, k_k, k_a, r_k, ln_g, ln_b):
    B, S, _ = p.shape
    p = token_shift(p, mu)
    r, k, v, wd, ad, gd = split_cols(p, RK_SIZES)
    w_raw = -jax.nn.softplus(-(w0 + jnp.tanh(wd) @ wB)) - 0.5
    decay = jnp.exp(-jnp.exp(w_raw))
    a = jax.nn.sigmoid(a0 + ad @ aB)
    g = jax.nn.sigmoid(gd) @ gB
    heads = lambda t: t.reshape(B, S, RK_HEADS, RK_DH)
    kk = heads(k * k_k)
    kk = kk / jnp.maximum(jnp.sqrt(jnp.sum(kk * kk, -1, keepdims=True)), 1e-12)
    k = k * (1.0 + (a - 1.0) * k_a)
    r, k, v, decay, a = heads(r), heads(k), heads(v), heads(decay), heads(a)

    def step(state, inp):
        r_t, w_t, k_t, v_t, kk_t, a_t = inp
        sa = jnp.einsum('bhij,bhj->bhi', state, -kk_t)
        state = (state * w_t[:, :, None, :] + sa[..., None] * (kk_t * a_t)[:, :, None, :]
                 + v_t[..., None] * k_t[:, :, None, :])
        return state, jnp.einsum('bhij,bhj->bhi', state, r_t)

    tm = lambda t: jnp.moveaxis(t, 1, 0)
    init = jnp.zeros((B, RK_HEADS, RK_DH, RK_DH), jnp.float32)
    _, y = lax.scan(step, init, (tm(r), tm(decay), tm(k), tm(v), tm(kk), tm(a)))
    y = head_norm(jnp.moveaxis(y, 0, 1), ln_g, ln_b, RK_NORM_EPS)
    bonus = (jnp.sum(r * k * r_k, -1, keepdims=True) * v).reshape(B, S, RK_WIDTH)
    return (y + bonus) * g

def gla_mixer(q, k, v, gd, og, gB, gb, norm_g):
    B, S, _ = v.shape
    log_alpha = jax.nn.log_sigmoid(gd @ gB + gb) / GLA_TAU
    q = to_chunks(q.reshape(B, S, GLA_HEADS, GLA_DK) * (GLA_DK ** -0.5), GLA_CHUNK)
    k = to_chunks(k.reshape(B, S, GLA_HEADS, GLA_DK), GLA_CHUNK)
    v = to_chunks(v.reshape(B, S, GLA_HEADS, GLA_DV), GLA_CHUNK)
    la = to_chunks(log_alpha.reshape(B, S, GLA_HEADS, GLA_DK), GLA_CHUNK)
    bcum = jnp.cumsum(la, axis=3)
    q_dec = q * jnp.exp(bcum)
    k_inv = k * jnp.exp(-bcum)
    causal = jnp.tril(jnp.ones((GLA_CHUNK, GLA_CHUNK), bool))
    attn = jnp.where(causal, jnp.einsum('nbhid,nbhjd->nbhij', q_dec, k_inv), 0.0)
    o = jnp.einsum('nbhij,nbhje->nbhie', attn, v)
    b_last = bcum[..., -1, :]
    kv = jnp.einsum('nbhcd,nbhce->nbhde', k * jnp.exp(b_last[..., None, :] - bcum), v)

    def step(state, inp):
        dec, kv_c = inp
        return dec[..., None] * state + kv_c, state

    init = jnp.zeros((B, GLA_HEADS, GLA_DK, GLA_DV), jnp.float32)
    _, s_prev = lax.scan(step, init, (jnp.exp(b_last), kv))
    o = o + jnp.einsum('nbhcd,nbhde->nbhce', q_dec, s_prev)
    o = from_chunks(o)
    return head_norm(o, norm_g, None, GLA_NORM_EPS) * jax.nn.silu(og)

def even_mixer(x, w_in, w_out, rg_conv_w, rg_conv_b, rg_wa, rg_wx, rg_ba, rg_bx, rg_lambda,
               ml_conv_w, ml_conv_b, ml_i_bias, ml_f_bias, ml_norm_g):
    p = (x @ w_in).astype(jnp.float32)
    rg_x, rg_g, ml_qk, ml_v, ml_o, ml_if = split_cols(p, EVEN_SIZES)
    y_rg = rg_lru_mixer(rg_x, rg_g, rg_conv_w, rg_conv_b, rg_wa, rg_wx, rg_ba, rg_bx, rg_lambda)
    y_ml = mlstm_mixer(ml_qk, ml_v, ml_o, ml_if, ml_conv_w, ml_conv_b, ml_i_bias, ml_f_bias, ml_norm_g)
    return jnp.concatenate([y_rg, y_ml], axis=-1).astype(x.dtype) @ w_out

def odd_mixer(x, w_in, w_out, rk_mu, rk_w0, rk_wB, rk_a0, rk_aB, rk_gB, rk_k_k, rk_k_a, rk_r_k,
              rk_ln_g, rk_ln_b, gla_gB, gla_gb, gla_norm_g):
    p = (x @ w_in).astype(jnp.float32)
    p_rk, p_gla = p[..., :RK_IN], p[..., RK_IN:]
    y_rk = rwkv7_mixer(p_rk, rk_mu, rk_w0, rk_wB, rk_a0, rk_aB, rk_gB, rk_k_k, rk_k_a, rk_r_k, rk_ln_g, rk_ln_b)
    gq, gk, gv, ggd, gog = split_cols(p_gla, GLA_SIZES)
    y_gla = gla_mixer(gq, gk, gv, ggd, gog, gla_gB, gla_gb, gla_norm_g)
    return jnp.concatenate([y_rk, y_gla], axis=-1).astype(x.dtype) @ w_out

def first_inputs(seed: int = 0) -> dict:
    key = jax.random.key(seed)
    ks = iter(jax.random.split(key, 64))
    nrm = lambda shape, scale: scale * jax.random.normal(next(ks), shape, jnp.float32)
    unif = lambda shape, lo, hi: jax.random.uniform(next(ks), shape, jnp.float32, lo, hi)
    NE, NO = N_EVEN, N_ODD
    beta = DEEPNORM_BETA
    s_rg = unif((NE, RG_WIDTH), 0.9, 0.999) ** (1.0 / RG_C)
    return {
        "x": nrm((BATCH, SEQ, D_MODEL), 1.0),
        "ffn1_wi": nrm((DEPTH, D_MODEL, 2 * D_FF), D_MODEL ** -0.5),
        "ffn1_wo": nrm((DEPTH, D_FF, D_MODEL), beta * D_FF ** -0.5),
        "ffn2_wi": nrm((DEPTH, D_MODEL, 2 * D_FF), D_MODEL ** -0.5),
        "ffn2_wo": nrm((DEPTH, D_FF, D_MODEL), beta * D_FF ** -0.5),
        "ln_g": 1.0 + nrm((DEPTH, 3, D_MODEL), 0.02),
        "ln_b": nrm((DEPTH, 3, D_MODEL), 0.02),
        "ev_w_in": nrm((NE, D_MODEL, EVEN_IN), D_MODEL ** -0.5),
        "ev_w_out": nrm((NE, MIX_WIDTH, D_MODEL), beta * MIX_WIDTH ** -0.5),
        "rg_conv_w": nrm((NE, CONV_WIDTH, RG_WIDTH), CONV_WIDTH ** -0.5),
        "rg_conv_b": nrm((NE, RG_WIDTH), 0.02),
        "rg_wa": nrm((NE, RG_BLOCKS, RG_BLK, RG_BLK), RG_BLK ** -0.5),
        "rg_wx": nrm((NE, RG_BLOCKS, RG_BLK, RG_BLK), RG_BLK ** -0.5),
        "rg_ba": nrm((NE, RG_WIDTH), 0.02),
        "rg_bx": nrm((NE, RG_WIDTH), 0.02),
        "rg_lambda": jnp.log(s_rg) - jnp.log1p(-s_rg),
        "ml_conv_w": nrm((NE, CONV_WIDTH, 2 * HALF), CONV_WIDTH ** -0.5),
        "ml_conv_b": nrm((NE, 2 * HALF), 0.02),
        "ml_i_bias": nrm((NE, ML_HEADS), 0.1),
        "ml_f_bias": jnp.linspace(3.0, 6.0, ML_HEADS)[None, :] + nrm((NE, ML_HEADS), 0.1),
        "ml_norm_g": 1.0 + nrm((NE, HALF), 0.02),
        "od_w_in": nrm((NO, D_MODEL, ODD_IN), D_MODEL ** -0.5),
        "od_w_out": nrm((NO, MIX_WIDTH, D_MODEL), beta * MIX_WIDTH ** -0.5),
        "rk_mu": unif((NO, RK_IN), 0.0, 1.0),
        "rk_w0": jnp.linspace(-6.5, -1.5, RK_WIDTH)[None, :] + nrm((NO, RK_WIDTH), 0.1),
        "rk_wB": nrm((NO, RK_DECAY_LORA, RK_WIDTH), 0.1 * RK_DECAY_LORA ** -0.5),
        "rk_a0": nrm((NO, RK_WIDTH), 0.1),
        "rk_aB": nrm((NO, RK_A_LORA, RK_WIDTH), 0.1 * RK_A_LORA ** -0.5),
        "rk_gB": nrm((NO, RK_G_LORA, RK_WIDTH), RK_G_LORA ** -0.5),
        "rk_k_k": 0.85 + nrm((NO, RK_WIDTH), 0.02),
        "rk_k_a": 1.0 + nrm((NO, RK_WIDTH), 0.02),
        "rk_r_k": nrm((NO, RK_HEADS, RK_DH), 0.1),
        "rk_ln_g": 1.0 + nrm((NO, RK_WIDTH), 0.02),
        "rk_ln_b": nrm((NO, RK_WIDTH), 0.02),
        "gla_gB": nrm((NO, GLA_GATE_LORA, GLA_HEADS * GLA_DK), GLA_GATE_LORA ** -0.5),
        "gla_gb": nrm((NO, GLA_HEADS * GLA_DK), 0.1),
        "gla_norm_g": 1.0 + nrm((NO, HALF), 0.02),
    }

def first_block(x, ffn1_wi, ffn1_wo, ffn2_wi, ffn2_wo, ln_g, ln_b,
              ev_w_in, ev_w_out, rg_conv_w, rg_conv_b, rg_wa, rg_wx, rg_ba, rg_bx, rg_lambda,
              ml_conv_w, ml_conv_b, ml_i_bias, ml_f_bias, ml_norm_g,
              od_w_in, od_w_out, rk_mu, rk_w0, rk_wB, rk_a0, rk_aB, rk_gB, rk_k_k, rk_k_a, rk_r_k,
              rk_ln_g, rk_ln_b, gla_gB, gla_gb, gla_norm_g):
    alpha = DEEPNORM_ALPHA
    for l in range(DEPTH):
        x = layer_norm(alpha * x + 0.5 * swiglu_ffn(x, ffn1_wi[l], ffn1_wo[l]), ln_g[l, 0], ln_b[l, 0])
        if l % 2 == 0:
            e = l // 2
            mix = even_mixer(x, ev_w_in[e], ev_w_out[e], rg_conv_w[e], rg_conv_b[e], rg_wa[e], rg_wx[e],
                             rg_ba[e], rg_bx[e], rg_lambda[e], ml_conv_w[e], ml_conv_b[e],
                             ml_i_bias[e], ml_f_bias[e], ml_norm_g[e])
        else:
            o = l // 2
            mix = odd_mixer(x, od_w_in[o], od_w_out[o], rk_mu[o], rk_w0[o], rk_wB[o], rk_a0[o], rk_aB[o],
                            rk_gB[o], rk_k_k[o], rk_k_a[o], rk_r_k[o], rk_ln_g[o], rk_ln_b[o],
                            gla_gB[o], gla_gb[o], gla_norm_g[o])
        x = layer_norm(alpha * x + mix, ln_g[l, 1], ln_b[l, 1])
        x = layer_norm(alpha * x + 0.5 * swiglu_ffn(x, ffn2_wi[l], ffn2_wo[l]), ln_g[l, 2], ln_b[l, 2])
    return x


_first_inputs = first_inputs


def first_inputs(seed=0):
    import zlib

    import numpy as np

    out = dict(_first_inputs(seed))
    spreads = {}
    factors = {'rg_conv_b': 3.634,
     'rg_ba': 64.0,
     'rg_bx': 59.222,
     'ml_conv_b': 8.0,
     'ml_i_bias': 64.0,
     'ml_norm_g': 8.0,
     'rk_wB': 8.0,
     'rk_a0': 8.0,
     'rk_aB': 8.0,
     'rk_k_k': 28.871,
     'rk_k_a': 8.0,
     'rk_ln_g': 39.645,
     'rk_ln_b': 41.708,
     'gla_gB': 3.529,
     'gla_gb': 8.0,
     'gla_norm_g': 34.641}
    for name, (base, spread) in spreads.items():
        noise = np.random.default_rng([zlib.crc32(name.encode()), seed]).standard_normal(out[name].shape)
        drawn = base * np.exp(spread * noise) if base else spread * noise
        out[name] = __import__('jax').numpy.asarray(drawn.astype(out[name].dtype))
    for name, factor in factors.items():
        out[name] = (out[name] * factor).astype(out[name].dtype)
    return out


_narrow_inputs = first_inputs


def first_inputs(seed=0):
    out = dict(_narrow_inputs(seed))
    wider = {'rk_k_k': 3.41, 'rk_ln_g': 4.49, 'rk_ln_b': 4.43, 'gla_norm_g': 4.38}
    for name, times in wider.items():
        mean = out[name].mean()
        out[name] = (mean + times * (out[name] - mean)).astype(out[name].dtype)
    return out


GRID_W = 64
N_MEM = 256
HEAD_DIM = 64
NA_HEADS = 6
NA_KH = 8
NA_KW = 16
DIL_PAIRS = ((128, 1), (512, 4), (2048, 16))
DIL_HEADS_PER_GROUP = 2
DIL_HEADS = 6
MEM_HEADS = 4
D_A = 384
D_B = 384
D_B_OUT = 128
D_M = 256
N_BRANCH = 3
D_IN = 3 * D_A + 3 * D_B + D_M + N_BRANCH * D_MODEL
CONV_W = 3
Q_BLOCK = 128
RMS_EPS = 1e-6
NEG_INF = -1e30


def rms_norm(x, g):
    xf = x.astype(jnp.float32)
    y = xf * lax.rsqrt(jnp.mean(xf * xf, axis=-1, keepdims=True) + RMS_EPS)
    return (y * g.astype(jnp.float32)).astype(x.dtype)

def split_heads(t, n_heads):
    B, S, _ = t.shape
    return t.reshape(B, S, n_heads, HEAD_DIM).transpose(0, 2, 1, 3)

def alibi_slopes(n):
    return 2.0 ** (-8.0 * jnp.arange(1, n + 1, dtype=jnp.float32) / n)

def neighborhood_attention(q, k, v, rpb):
    B, H, S, d = q.shape
    rows = S // GRID_W
    kh = min(NA_KH, rows)
    kw = NA_KW
    scale = d ** -0.5
    qg = q.reshape(B, H, rows, GRID_W, d)
    kg = k.reshape(B, H, rows, GRID_W, d)
    vg = v.reshape(B, H, rows, GRID_W, d)
    cols = jnp.arange(GRID_W)
    col_start = jnp.clip(cols - kw // 2, 0, GRID_W - kw)
    col_idx = col_start[:, None] + jnp.arange(kw)[None, :]
    col_off = col_idx - cols[:, None] + (NA_KW - 1)
    rpb_c = rpb[:, :, col_off]

    def one_row(i):
        r0 = jnp.clip(i - kh // 2, 0, rows - kh)
        k_band = lax.dynamic_slice_in_dim(kg, r0, kh, axis=2)
        v_band = lax.dynamic_slice_in_dim(vg, r0, kh, axis=2)
        k_win = k_band[:, :, :, col_idx, :]
        v_win = v_band[:, :, :, col_idx, :]
        q_row = lax.dynamic_index_in_dim(qg, i, axis=2, keepdims=False)
        s = jnp.einsum('bhqd,bhrqcd->bhqrc', q_row, k_win).astype(jnp.float32) * scale
        row_off = r0 + jnp.arange(kh) - i + (NA_KH - 1)
        bias = jnp.take(rpb_c, row_off, axis=1).transpose(0, 2, 1, 3)
        s = s + bias.astype(jnp.float32)[None]
        p = jax.nn.softmax(s.reshape(B, H, GRID_W, kh * kw), axis=-1).reshape(B, H, GRID_W, kh, kw)
        return jnp.einsum('bhqrc,bhrqcd->bhqd', p.astype(v.dtype), v_win)

    out = lax.map(one_row, jnp.arange(rows))
    return out.transpose(1, 2, 0, 3, 4).reshape(B, H, S, d)

def dilated_attention(q, k, v):
    B, _, S, d = q.shape
    n_blk = S // Q_BLOCK
    scale = d ** -0.5
    slopes = alibi_slopes(DIL_HEADS)
    outs, lses = [], []
    for g, (window, dilation) in enumerate(DIL_PAIRS):
        hs = slice(g * DIL_HEADS_PER_GROUP, (g + 1) * DIL_HEADS_PER_GROUP)
        qg, kg, vg = q[:, hs], k[:, hs], v[:, hs]
        half = window // 2 // dilation
        offs = dilation * jnp.arange(-half, half + 1)
        alibi = -slopes[hs][:, None, None] * jnp.abs(offs).astype(jnp.float32)[None, None, :]
        qb = qg.reshape(B, DIL_HEADS_PER_GROUP, n_blk, Q_BLOCK, d)

        def one_block(bi):
            pos = bi * Q_BLOCK + jnp.arange(Q_BLOCK)
            idx = pos[:, None] + offs[None, :]
            valid = (idx >= 0) & (idx < S)
            idx_c = jnp.clip(idx, 0, S - 1)
            kk = jnp.take(kg, idx_c, axis=2)
            vv = jnp.take(vg, idx_c, axis=2)
            qq = lax.dynamic_index_in_dim(qb, bi, axis=2, keepdims=False)
            s = jnp.einsum('bhqd,bhqkd->bhqk', qq, kk).astype(jnp.float32) * scale + alibi[None]
            s = jnp.where(valid[None, None], s, NEG_INF)
            m = jnp.max(s, axis=-1, keepdims=True)
            p = jnp.exp(s - m)
            den = jnp.sum(p, axis=-1, keepdims=True)
            o = jnp.einsum('bhqk,bhqkd->bhqd', (p / den).astype(v.dtype), vv)
            lse = (m + jnp.log(den))[..., 0]
            return o, lse

        o, lse = lax.map(one_block, jnp.arange(n_blk))
        outs.append(o.transpose(1, 2, 0, 3, 4).reshape(B, DIL_HEADS_PER_GROUP, S, d))
        lses.append(lse.transpose(1, 2, 0, 3).reshape(B, DIL_HEADS_PER_GROUP, S))
    o_all = jnp.stack(outs, axis=0)
    alpha = jax.nn.softmax(jnp.stack(lses, axis=0), axis=0)
    out = jnp.einsum('gbhs,gbhsd->bshd', alpha.astype(o_all.dtype), o_all)
    return out.reshape(B, S, D_B_OUT)

def memory_attention(q, mem_n, w_kv):
    B, S, _ = q.shape
    kv = mem_n @ w_kv
    km, vm = jnp.split(kv, 2, axis=-1)
    qh = q.reshape(B, S, MEM_HEADS, HEAD_DIM)
    km = km.reshape(B, -1, MEM_HEADS, HEAD_DIM)
    vm = vm.reshape(B, -1, MEM_HEADS, HEAD_DIM)
    s = jnp.einsum('bshd,bmhd->bhsm', qh, km).astype(jnp.float32) * (HEAD_DIM ** -0.5)
    p = jax.nn.softmax(s, axis=-1)
    o = jnp.einsum('bhsm,bmhd->bshd', p.astype(vm.dtype), vm)
    return o.reshape(B, S, D_M)

def depthwise_conv_centred(u, w, b):
    S = u.shape[1]
    pad = CONV_W // 2
    up = jnp.pad(u, ((0, 0), (pad, pad), (0, 0)))
    y = b
    for j in range(CONV_W):
        y = y + up[:, j:j + S] * w[j]
    return y

def second_inputs(seed: int = 0) -> dict:
    key = jax.random.key(seed)
    ks = jax.random.split(key, 20)
    f32 = jnp.float32

    def nrm(k, shape, scale):
        return jax.random.normal(k, shape, f32) * scale

    def gain(k, shape):
        return 1.0 + 0.05 * jax.random.normal(k, shape, f32)

    return {
        'x': nrm(ks[0], (BATCH, SEQ, D_MODEL), 1.0),
        'mem': nrm(ks[1], (BATCH, N_MEM, D_MODEL), 1.0),
        'mem_norm_g': gain(ks[2], (D_MODEL,)),
        'g_pre_mix': gain(ks[3], (DEPTH, D_MODEL)),
        'w_in': nrm(ks[4], (DEPTH, D_MODEL, D_IN), D_MODEL ** -0.5),
        'rpb_na': nrm(ks[5], (DEPTH, NA_HEADS, 2 * NA_KH - 1, 2 * NA_KW - 1), 0.5),
        'w_mem_kv': nrm(ks[6], (DEPTH, D_MODEL, 2 * D_M), D_MODEL ** -0.5),
        'b_gate': nrm(ks[7], (DEPTH, N_BRANCH, D_MODEL), 0.1),
        'w_br_a': nrm(ks[8], (DEPTH, D_A, D_MODEL), D_A ** -0.5),
        'w_br_b': nrm(ks[9], (DEPTH, D_B_OUT, D_MODEL), D_B_OUT ** -0.5),
        'w_br_m': nrm(ks[10], (DEPTH, D_M, D_MODEL), D_M ** -0.5),
        'w_out': nrm(ks[11], (DEPTH, D_MODEL, D_MODEL), D_MODEL ** -0.5),
        'g_post_mix': gain(ks[12], (DEPTH, D_MODEL)),
        'g_pre_ffn': gain(ks[13], (DEPTH, D_MODEL)),
        'w_up': nrm(ks[14], (DEPTH, D_MODEL, 2 * D_FF), D_MODEL ** -0.5),
        'conv_w': nrm(ks[15], (DEPTH, CONV_W, 2 * D_FF), CONV_W ** -0.5),
        'conv_b': nrm(ks[16], (DEPTH, 2 * D_FF), 0.02),
        'w_down': nrm(ks[17], (DEPTH, D_FF, D_MODEL), D_FF ** -0.5),
        'g_post_ffn': gain(ks[18], (DEPTH, D_MODEL)),
    }

def second_block(x, mem, mem_norm_g, g_pre_mix, w_in, rpb_na, w_mem_kv, b_gate, w_br_a, w_br_b,
              w_br_m, w_out, g_post_mix, g_pre_ffn, w_up, conv_w, conv_b, w_down, g_post_ffn):
    B, S, D = x.shape
    splits = [D_A, 2 * D_A, 3 * D_A, 3 * D_A + D_B, 3 * D_A + 2 * D_B, 3 * D_A + 3 * D_B,
              3 * D_A + 3 * D_B + D_M]
    mem_n = rms_norm(mem, mem_norm_g)
    for l in range(DEPTH):
        h = rms_norm(x, g_pre_mix[l])
        proj = h @ w_in[l]
        q_a, k_a, v_a, q_b, k_b, v_b, q_m, gate_pre = jnp.split(proj, splits, axis=-1)
        o_a = neighborhood_attention(split_heads(q_a, NA_HEADS), split_heads(k_a, NA_HEADS),
                                     split_heads(v_a, NA_HEADS), rpb_na[l])
        o_a = o_a.transpose(0, 2, 1, 3).reshape(B, S, D_A)
        o_b = dilated_attention(split_heads(q_b, DIL_HEADS), split_heads(k_b, DIL_HEADS),
                                split_heads(v_b, DIL_HEADS))
        o_m = memory_attention(q_m, mem_n, w_mem_kv[l])
        gates = jax.nn.sigmoid(gate_pre.reshape(B, S, N_BRANCH, D) + b_gate[l])
        merged = (gates[:, :, 0] * (o_a @ w_br_a[l])
                  + gates[:, :, 1] * (o_b @ w_br_b[l])
                  + gates[:, :, 2] * (o_m @ w_br_m[l]))
        x = x + rms_norm(merged @ w_out[l], g_post_mix[l])
        h = rms_norm(x, g_pre_ffn[l])
        u = depthwise_conv_centred(h @ w_up[l], conv_w[l], conv_b[l])
        a, b = jnp.split(u, 2, axis=-1)
        f = jax.nn.gelu(a) * b
        x = x + rms_norm(f @ w_down[l], g_post_ffn[l])
    return x


def setup_inputs(seed=0):
    out = dict(first_inputs(seed))
    for name, value in second_inputs(seed + 1).items():
        if name != "x":
            out[name + "_2"] = value
    return out


def reference(
    x, ffn1_wi, ffn1_wo, ffn2_wi, ffn2_wo, ln_g, ln_b, ev_w_in, ev_w_out, rg_conv_w, rg_conv_b,
    rg_wa, rg_wx, rg_ba, rg_bx, rg_lambda, ml_conv_w, ml_conv_b, ml_i_bias, ml_f_bias,
    ml_norm_g, od_w_in, od_w_out, rk_mu, rk_w0, rk_wB, rk_a0, rk_aB, rk_gB, rk_k_k, rk_k_a,
    rk_r_k, rk_ln_g, rk_ln_b, gla_gB, gla_gb, gla_norm_g, mem_2, mem_norm_g_2, g_pre_mix_2,
    w_in_2, rpb_na_2, w_mem_kv_2, b_gate_2, w_br_a_2, w_br_b_2, w_br_m_2, w_out_2, g_post_mix_2,
    g_pre_ffn_2, w_up_2, conv_w_2, conv_b_2, w_down_2, g_post_ffn_2,
):
    x = first_block(
        x, ffn1_wi, ffn1_wo, ffn2_wi, ffn2_wo, ln_g, ln_b, ev_w_in, ev_w_out, rg_conv_w,
        rg_conv_b, rg_wa, rg_wx, rg_ba, rg_bx, rg_lambda, ml_conv_w, ml_conv_b, ml_i_bias,
        ml_f_bias, ml_norm_g, od_w_in, od_w_out, rk_mu, rk_w0, rk_wB, rk_a0, rk_aB, rk_gB,
        rk_k_k, rk_k_a, rk_r_k, rk_ln_g, rk_ln_b, gla_gB, gla_gb, gla_norm_g,
    )
    return second_block(
        x, mem_2, mem_norm_g_2, g_pre_mix_2, w_in_2, rpb_na_2, w_mem_kv_2, b_gate_2, w_br_a_2,
        w_br_b_2, w_br_m_2, w_out_2, g_post_mix_2, g_pre_ffn_2, w_up_2, conv_w_2, conv_b_2,
        w_down_2, g_post_ffn_2,
    )


_drawn_inputs = setup_inputs


def setup_inputs(seed=0):
    import zlib

    import numpy as np

    out = dict(_drawn_inputs(seed))
    spreads = {}
    factors = {'mem_norm_g_2': 2.716}
    for name, (base, spread) in spreads.items():
        noise = np.random.default_rng([zlib.crc32(name.encode()), seed]).standard_normal(out[name].shape)
        drawn = base * np.exp(spread * noise) if base else spread * noise
        out[name] = __import__('jax').numpy.asarray(drawn.astype(out[name].dtype))
    for name, factor in factors.items():
        out[name] = (out[name] * factor).astype(out[name].dtype)
    return out
```

```python
from contextlib import ExitStack

import numpy as np
import concourse.bass as bass
from concourse import mybir

F32 = mybir.dt.float32
F32R = mybir.dt.float32r
ALU = mybir.AluOpType
ACT = mybir.ActivationFunctionType
AX_X = mybir.AxisListType.X

P = 128
S = 512
D = 1024
KT = D // P
DEPTH = 2
DFF = 2816
FT = DFF // P
FH = FT // 2
CHUNK = 2 * KT * P
ALPHA = (2.0 * DEPTH) ** 0.25
LN_EPS = 1e-5
PRIME = 4



def stream_plan():
    plan = []
    for l in range(DEPTH):
        plan += [(f"ffn1_{l}", CHUNK)] * FT + [(f"ffn1_{l}", FH * P)] * (2 * KT)
        plan += [(f"mix_{l}", CHUNK)] * (13 + KT // 2)
        plan += [(f"ffn2_{l}", CHUNK)] * FT + [(f"ffn2_{l}", FH * P)] * (2 * KT)
    for l in range(DEPTH):
        plan += [(f"att_{l}", CHUNK)] * (10 + 2 + 12)
        plan += [(f"att_{l}", 2 * 6 * P)] * (KT // 2) + [(f"att_{l}", CHUNK)] * (KT // 2)
        plan += [(f"cffn_{l}", CHUNK)] * FT + [(f"cffn_{l}", FH * P)] * (2 * KT)
    return plan


class Signal:

    def __init__(self, sem, base=PRIME):
        self.sem, self.base = sem, base

    def at(self, n):
        return self.base + n

    def advance(self, n):
        self.base += n



def tiles_in(w):
    n = w.shape[1] // P
    return w.reshape(KT, P, n, P).transpose(2, 1, 0, 3)


def tiles_out(w):
    return w.reshape(2, FH, P, KT, P).transpose(3, 0, 2, 1, 4).reshape(2 * KT, P, FH * P)


def pad_cols(w, n):
    return np.pad(w, ((0, 0), (0, n - w.shape[1])))


def pairs(tiles):
    n = tiles.shape[0] // 2
    return tiles.reshape(n, 2, P, KT, P).transpose(0, 2, 1, 3, 4).reshape(n, P, CHUNK)


def gated(w):
    a, b = tiles_in(w[:, :DFF]), tiles_in(w[:, DFF:])
    return pairs(np.stack([a, b], 1).reshape(2 * FT, P, KT, P))


EVEN_TILES = 26
ODD_TILES = 26


def lay_out_weights(i):
    plan = stream_plan()
    out = np.zeros((len(plan), P, CHUNK), np.float32)
    at = 0

    def put(chunks):
        nonlocal at
        for c in chunks:
            out[at, :, : c.shape[-1]] = c
            at += 1

    for l in range(DEPTH):
        put(gated(i["ffn1_wi"][l]))
        put(tiles_out(i["ffn1_wo"][l]))
        if l % 2 == 0:
            w = i["ev_w_in"][l // 2]
            n = w.shape[1] - 8
            put(pairs(tiles_in(np.concatenate([w[:, :n], pad_cols(w[:, n:n + 4], P), pad_cols(w[:, n + 4:], P)], 1))))
            put(pairs(tiles_in(i["ev_w_out"][l // 2])))
        else:
            w = i["od_w_in"][l // 2]
            g = 1664 + 1024
            put(pairs(tiles_in(np.concatenate([w[:, :g], pad_cols(w[:, g:g + 16], P), w[:, g + 16:]], 1))))
            put(pairs(tiles_in(i["od_w_out"][l // 2])))
        put(gated(i["ffn2_wi"][l]))
        put(tiles_out(i["ffn2_wo"][l]))
    for l in range(DEPTH):
        w = i["w_in_2"][l]
        put(pairs(tiles_in(i["w_mem_kv_2"][l])))
        put(pairs(tiles_in(w[:, :2560])))
        g = tiles_in(w[:, 2560:]).reshape(3, KT, P, KT, P).transpose(1, 0, 2, 3, 4)
        put(pairs(g.reshape(3 * KT, P, KT, P)))
        br = np.concatenate([i["w_br_a_2"][l], i["w_br_b_2"][l], i["w_br_m_2"][l]], 0)
        br = br.reshape(6, P, KT // 2, 2, P).transpose(2, 1, 3, 0, 4).reshape(KT // 2, P, 12 * P)
        put(br)
        put(pairs(tiles_in(i["w_out_2"][l])))
        put(gated(i["w_up_2"][l]))
        put(tiles_out(i["w_down_2"][l]))
    assert at == len(plan)
    return out


def columns():
    return {
        "ln_g": 48, "ln_b": 48,
        "rg_conv_w": 16, "rg_conv_b": 4, "rg_ba": 4, "rg_bx": 4, "rg_lambda": 4,
        "ml_conv_w": 32, "ml_conv_b": 8, "ml_i_bias": 1, "ml_f_bias": 1, "ml_norm_g": 4,
        "rk_mu": 13, "rk_w0": 4, "rk_a0": 4, "rk_k_k": 4, "rk_k_a": 4, "rk_r_k": 4, "rk_ln_g": 4, "rk_ln_b": 4,
        "gla_gb": 2, "gla_norm_g": 4,
        "mem_norm_g_2": 8, "g_pre_mix_2": 16, "b_gate_2": 48, "g_post_mix_2": 16, "g_pre_ffn_2": 16,
        "conv_w_2": 6 * 44, "conv_b_2": 2 * 44, "g_post_ffn_2": 16,
        "eps_deepnorm": 1, "eps_rms": 1, "eps_ml": 1, "eps_rk": 1, "eps_gla": 1,
    }


def column_starts():
    at, out = 0, {}
    for name, n in columns().items():
        out[name] = at
        at += n
    return out, at


def lay_out_columns(i):
    start, n = column_starts()
    out = np.zeros((P, n), np.float32)
    shapes = {"eps_deepnorm": LN_EPS / ALPHA**2, "eps_rms": 1e-6, "eps_ml": 1e-6, "eps_rk": 64e-5, "eps_gla": 1e-5}
    for name, k in columns().items():
        at = start[name]
        if name in shapes:
            out[:, at] = shapes[name]
            continue
        v = np.asarray(i[name]).reshape(-1)
        if v.size < P:
            out[: v.size, at] = v
        else:
            out[:, at:at + k] = v.reshape(k, P).T
    return out


class Chain:

    def __init__(self, eng, sig):
        self.eng, self.sig, self.n = eng, sig, 0

    def add(self, ins):
        self.n += 1
        ins.then_inc(self.sig.sem, 1)
        return self.n

    def wait(self, n=None):
        self.eng.wait_ge(self.sig.sem, self.sig.at(self.n if n is None else n))



def constants():
    eye = np.eye(P, dtype=np.float32)
    half = np.kron(np.eye(2, dtype=np.float32), np.ones((64, 64), np.float32))
    return {
        "identity": eye,
        "mean_d": np.full((P, P), 1.0 / D, np.float32),
        "mean_p": np.full((P, P), 1.0 / P, np.float32),
        "ones": np.ones((P, P), np.float32),
        "half_ones": half,
        "half_mean": half / 64,
        **{f"pick{h}": np.repeat((np.arange(P) == h).astype(np.float32)[:, None], P, 1) for h in range(4)},
    }


def odd_masks():
    i = np.arange(P)
    s, u = i[:, None], i[None, :]
    reset = [np.repeat((np.arange(S) % c != 0)[None], P, 0) for c in (32, 64)]
    parts = reset + [(s // 32 == u // 32) & (s < u), (s // 32 == u // 32) & (s <= u), (s // 64 == u // 64) & (s <= u),
                     (s % 32) > np.arange(32)[None, :]]
    return np.concatenate(parts, 1).astype(np.float32)


def program(nc, t):
    plan = stream_plan()
    n_chunks = len(plan)
    col_at, n_cols = column_starts()
    ctx = ExitStack()
    with ctx:
        def sb(name, shape, dt=F32, scope=ctx):
            return scope.enter_context(nc.sbuf_tensor(name, shape, dt))

        signals = {}

        def signal(name):
            if name not in signals:
                signals[name] = Signal(ctx.enter_context(nc.semaphore(name)))
            return signals[name]

        raw = sb("raw", [P, 2, CHUNK])
        w_hi = sb("w_hi", [P, 2, CHUNK], F32R)
        w_lo = sb("w_lo", [P, 2, CHUNK], F32R)
        X = sb("X", [P, KT, S])
        x_hi = sb("x_hi", [P, KT, S], F32R)
        x_lo = sb("x_lo", [P, KT, S], F32R)
        cols = sb("cols", [P, n_cols])
        const_names = list(constants())
        consts = sb("consts", [P, 2, P])
        first_block = ExitStack()
        mixer_consts = sb("mixer_consts", [P, len(const_names) - 2, P], F32, first_block)
        bank = [ctx.enter_context(nc.psum_tensor(f"bank{b}", [P, S], F32)) for b in range(8)]
        const = {name: consts[:, n, :] if n < 2 else mixer_consts[:, n - 2, :] for n, name in enumerate(const_names)}

        def col(name, n=0):
            return cols[:, col_at[name] + n:col_at[name] + n + 1]

        raw_loaded = [ctx.enter_context(nc.semaphore(f"raw_loaded{s}")) for s in range(2)]
        loads_done = ctx.enter_context(nc.semaphore("loads_done"))
        stores_done = ctx.enter_context(nc.semaphore("stores_done"))
        primed = ctx.enter_context(nc.semaphore("primed"))
        loads = Signal(loads_done, 64)
        hi_ready, lo_ready, chunk_used = signal("hi_ready"), signal("lo_ready"), signal("chunk_used")
        psum_ready, psum_free = signal("psum_ready"), signal("psum_free")
        part_ready, part_free = signal("part_ready"), signal("part_free")
        zsum_ready, mean_ready, centred = signal("zsum_ready"), signal("mean_ready"), signal("centred")
        square_ready, square_used, scale_ready = signal("square_ready"), signal("square_used"), signal("scale_ready")
        scaled, x_ready, split_ready = signal("scaled"), signal("x_ready"), signal("split_ready")
        act_ready, product_ready, rounded = signal("act_ready"), signal("product_ready"), signal("rounded")
        rest_ready, z_ready = signal("rest_ready"), signal("z_ready")
        bank_free = [signal("bank_free0"), signal("bank_free1")]
        dve_chain, act_chain = signal("dve_chain"), signal("act_chain")
        gates_ready, decay_ready, inflow_ready, state_ready = (
            signal(n) for n in ("gates_ready", "decay_ready", "inflow_ready", "state_ready"))
        qk_ready, vt_ready, vt_psum, rows_ready, frame_ready, u_ready = (
            signal(n) for n in ("qk_ready", "vt_ready", "vt_psum", "rows_ready", "frame_ready", "u_ready"))
        score_ready, weight_arg, weight_ready, floor_ready, masked = (
            signal(n) for n in ("score_ready", "weight_arg", "weight_ready", "floor_ready", "masked"))
        attended, h_ready, y_ready, pair_ready = (signal(n) for n in ("attended", "h_ready", "y_ready", "pair_ready"))
        pool_zero = signal("pool_zero")
        conv_a, conv_b = signal("conv_a"), signal("conv_b")
        bias_loaded = [Signal(ctx.enter_context(nc.semaphore(f"bias_loaded{n}")), 0) for n in range(3)]
        stage_no = [0]

        def end_stage(**counts):
            for name, n in counts.items():
                signals[name].advance(n)
            stage_no[0] += 1


        def half(n0, i, u):
            return i + (n0 + u) // 2

        def fetch(sp, n0, i, u, size):
            c, s = i * 2 + (n0 + u), (n0 + u) % 2
            sp.wait_ge(lo_ready.sem, c + (PRIME - 1))
            sp.dma_start(raw[:, s, 0:size], t["weights"][c, :, 0:size]).then_inc(raw_loaded[s], 16)

        def split_hi(act, n0, i, u, size):
            c, s = i * 2 + (n0 + u), (n0 + u) % 2
            act.wait_ge(raw_loaded[s], (half(n0, i, u) + 1) * 16)
            act.wait_ge(chunk_used.sem, c + (PRIME - 1))
            act.activation(w_hi[:, s, 0:size], raw[:, s, 0:size], ACT.Copy).then_inc(hi_ready.sem, 1)

        def split_lo(dve, n0, i, u, size):
            c, s = i * 2 + (n0 + u), (n0 + u) % 2
            dve.wait_ge(hi_ready.sem, c + (PRIME + 1))
            dve.tensor_tensor(w_lo[:, s, 0:size], raw[:, s, 0:size], w_hi[:, s, 0:size].bitcast(F32),
                              ALU.subtract).then_inc(lo_ready.sem, 1)

        def for_chunks(eng, n, body, unroll=2, peel=2):
            turns = max(0, (n - peel) // unroll)
            if turns > 1:
                with eng.Fori(0, turns) as i:
                    for u in range(unroll):
                        body(i * (unroll // 2) + u // 2, u % 2)
            else:
                turns = 0
            for j in range(turns * unroll, n):
                body(j // 2, j % 2)

        def ahead(step, eng, n0, n, k):
            def body(i, u):
                if isinstance(i, int):
                    c = n0 + 2 * i + u + k
                    if c < n_chunks:
                        step(eng, c - c % 2, 0, c % 2, plan[c][1])
                else:
                    step(eng, n0 + k, i, u, plan[n0][1])
            return body

        def linear(pe, out, s, at, kts, hi, lo, first=True, last=True):
            for n, k in enumerate(kts):
                w = slice(at + n * P, at + n * P + P)
                pe.matmul(out, w_hi[:, s, w], hi(k), start=first and n == 0, stop=False)
                pe.matmul(out, w_hi[:, s, w], lo(k), start=False, stop=False)
                mm = pe.matmul(out, w_lo[:, s, w], hi(k), start=False, stop=last and n == len(kts) - 1)
            return mm

        def x_parts():
            return (lambda k: x_hi[:, k, :]), (lambda k: x_lo[:, k, :])


        with nc.Block() as block:
            @block.sync
            def _(sp):
                for sig in signals.values():
                    sp.sem_inc(sig.sem, PRIME)
                sp.sem_inc(primed, 1)
                sp.dma_start(X[:, :, :], t["x"]).then_inc(loads_done, 16)
                sp.dma_start(consts[:, :, :], t["consts"][:, 0:2, :]).then_inc(loads_done, 16)
                sp.dma_start(mixer_consts[:, :, :], t["consts"][:, 2:, :]).then_inc(loads_done, 16)
                sp.dma_start(cols[:, :], t["cols"]).then_inc(loads_done, 16)
                fetch(sp, 0, 0, 0, CHUNK)
                fetch(sp, 0, 0, 1, CHUNK)

            @block.scalar
            def _(act):
                act.wait_ge(primed, 1)
                act.wait_ge(loads_done, 64)
                split_hi(act, 0, 0, 0, CHUNK)
                for k in range(KT):
                    act.activation(x_hi[:, k, :], X[:, k, :], ACT.Copy).then_inc(x_ready.sem, 1)

            @block.vector
            def _(dve):
                dve.wait_ge(primed, 1)
                split_lo(dve, 0, 0, 0, CHUNK)
                for k in range(KT):
                    dve.wait_ge(x_ready.sem, x_ready.at(k + 1))
                    dve.tensor_tensor(x_lo[:, k, :], X[:, k, :], x_hi[:, k, :].bitcast(F32),
                                      ALU.subtract).then_inc(split_ready.sem, 1)
        end_stage(x_ready=KT, split_ready=KT)
        c_next = [0]


        def norm_tensor(pe, acc, sq):
            pe.wait_ge(zsum_ready.sem, zsum_ready.at(KT))
            pe.matmul(bank[6][:, :], const["mean_d"], acc[:, :], start=True, stop=True).then_inc(mean_ready.sem, 1)
            for k in range(KT):
                pe.wait_ge(square_ready.sem, square_ready.at(k + 1))
                pe.matmul(bank[7][:, :], const["mean_d"], sq[:, k % 2, :], start=k == 0,
                          stop=k == KT - 1).then_inc(square_used.sem, 1)

        def norm_vector(dve, rstd):
            dve.wait_ge(mean_ready.sem, mean_ready.at(1))
            for k in range(KT):
                dve.tensor_tensor(X[:, k, :], X[:, k, :], bank[6][:, :], ALU.subtract).then_inc(centred.sem, 1)
            dve.wait_ge(scale_ready.sem, scale_ready.at(2))
            for k in range(KT):
                dve.tensor_tensor(X[:, k, :], X[:, k, :], rstd[:, :], ALU.mult).then_inc(scaled.sem, 1)

        def norm_scalar(act, sq, rstd, l, which):
            for k in range(KT):
                act.wait_ge(centred.sem, centred.at(k + 1))
                act.wait_ge(square_used.sem, square_used.at(k - 1))
                act.activation(sq[:, k % 2, :], X[:, k, :], ACT.Square).then_inc(square_ready.sem, 1)
            act.wait_ge(square_used.sem, square_used.at(KT))
            act.activation(rstd[:, :], bank[7][:, :], ACT.Ln, bias=col("eps_deepnorm")).then_inc(scale_ready.sem, 1)
            act.wait_ge(scale_ready.sem, scale_ready.at(1))
            act.activation(rstd[:, :], rstd[:, :], ACT.Exp, scale=-0.5).then_inc(scale_ready.sem, 1)
            for k in range(KT):
                n = (l * 3 + which) * KT + k
                act.wait_ge(scaled.sem, scaled.at(k + 1))
                act.activation(X[:, k, :], X[:, k, :], ACT.Identity, bias=col("ln_b", n),
                               scale=col("ln_g", n)).then_inc(x_ready.sem, 1)
                act.wait_ge(x_ready.sem, x_ready.at(k + 1))
                act.activation(x_hi[:, k, :], X[:, k, :], ACT.Copy).then_inc(rounded.sem, 1)

        def norm_pool(pool, done):
            for k in range(KT):
                pool.wait_ge(rounded.sem, rounded.at(done + k + 1))
                pool.tensor_tensor(x_lo[:, k, :], X[:, k, :], x_hi[:, k, :].bitcast(F32),
                                   ALU.subtract).then_inc(split_ready.sem, 1)

        NORM = dict(zsum_ready=KT, mean_ready=1, centred=KT, square_ready=KT, square_used=KT, scale_ready=2,
                    scaled=KT, x_ready=KT, split_ready=KT)


        def residual_vector(dve, scale, banks, n, k):
            dve.wait_ge(psum_ready.sem, psum_ready.at(1) + n)
            dve.scalar_tensor_tensor(out=X[:, n, :], in0=bank[banks[k]][:, :], scalar=scale, in1=X[:, n, :],
                                     op0=ALU.mult, op1=ALU.add).then_inc(z_ready.sem, 1)

        def zsum_pool(pool, acc):
            for k in range(KT):
                pool.wait_ge(z_ready.sem, z_ready.at(max(k + 1, 2)))
                if k == 0:
                    continue
                pool.wait_ge(zsum_ready.sem, zsum_ready.at(k if k > 1 else 0))
                a = X[:, 0, :] if k == 1 else acc[:, :]
                pool.tensor_tensor(acc[:, :], a, X[:, k, :], ALU.add).then_inc(zsum_ready.sem, 2 if k == 1 else 1)


        def swiglu(l, which):
            n0 = c_next[0]
            n1 = n0 + FT
            c_next[0] = n1 + 2 * KT
            scope = ExitStack()
            with scope:
                nm = f"f{stage_no[0]}_"
                g_hi = sb(nm + "g_hi", [P, FT, S], F32R, scope)
                g_lo = sb(nm + "g_lo", [P, FT, S], F32R, scope)
                silu = sb(nm + "silu", [P, 2, S], F32, scope)
                prod = sb(nm + "prod", [P, 2, S], F32, scope)
                acc, rstd = prod[:, 0, :], prod[:, 1, :]
                sq = silu
                hi, lo = x_parts()
                with nc.Block() as block:
                    @block.sync
                    def _(sp):
                        for_chunks(sp, FT, ahead(fetch, sp, n0, FT, 2))
                        for_chunks(sp, 2 * KT, ahead(fetch, sp, n1, 2 * KT, 2))

                    @block.tensor
                    def _(pe):
                        def gate_up(i, u):
                            s, j = (n0 + u) % 2, i * 2 + u
                            pe.wait_ge(lo_ready.sem, j + (PRIME + n0 + 1))
                            pe.wait_ge(product_ready.sem, product_ready.at(-1) + j)
                            linear(pe, bank[2 * u][:, :], s, 0, range(KT), hi, lo)
                            linear(pe, bank[2 * u + 1][:, :], s, KT * P, range(KT), hi, lo)\
                                .then_inc(chunk_used.sem, 1)

                        for_chunks(pe, FT, gate_up)
                        pe.wait_ge(rest_ready.sem, rest_ready.at(FT))

                        def down(i, u):
                            s = (n1 + u) % 2
                            b = bank[4 + (i % 2 if isinstance(i, int) else parity[0])][:, :]
                            pe.wait_ge(lo_ready.sem, i * 2 + (PRIME + n1 + u + 1))
                            if u == 0:
                                pe.wait_ge(z_ready.sem, z_ready.at(-1) + i)
                            mm = linear(pe, b, s, 0, range(FH * u, FH * u + FH), lambda k: g_hi[:, k, :],
                                        lambda k: g_lo[:, k, :], first=u == 0, last=u == 1)
                            mm.then_inc(chunk_used.sem, 1)

                        parity = [0]
                        with pe.Fori(0, KT // 2) as i:
                            for v in range(2):
                                parity[0] = v
                                for u in range(2):
                                    down(i * 2 + v, u)
                        norm_tensor(pe, acc, sq)

                    @block.scalar
                    def _(act):
                        split = ahead(split_hi, act, n0, FT, 1)

                        def body(i, u):
                            split(i, u)
                            j = i * 2 + u
                            act.wait_ge(chunk_used.sem, j + (PRIME + n0 + 1))
                            act.wait_ge(product_ready.sem, product_ready.at(-1) + j)
                            act.activation(silu[:, u, :], bank[2 * u][:, :], ACT.Silu).then_inc(act_ready.sem, 1)
                            act.wait_ge(product_ready.sem, product_ready.at(1) + j)
                            act.activation(g_hi[:, j, :], prod[:, u, :], ACT.Copy).then_inc(rounded.sem, 1)

                        for_chunks(act, FT, body)
                        for_chunks(act, 2 * KT, ahead(split_hi, act, n1, 2 * KT, 1))
                        norm_scalar(act, sq, rstd, l, which)

                    def residual(dve, n, k):
                        dve.scalar_tensor_tensor(out=X[:, n, :], in0=bank[4 + k][:, :], scalar=0.5 / ALPHA,
                                                 in1=X[:, n, :], op0=ALU.mult, op1=ALU.add).then_inc(z_ready.sem, 1)

                    @block.vector
                    def _(dve):
                        split = ahead(split_lo, dve, n0, FT, 1)

                        def body(i, u):
                            split(i, u)
                            j = i * 2 + u
                            dve.wait_ge(act_ready.sem, act_ready.at(1) + j)
                            dve.wait_ge(rest_ready.sem, rest_ready.at(-1) + j)
                            dve.tensor_tensor(prod[:, u, :], silu[:, u, :], bank[2 * u + 1][:, :],
                                              ALU.mult).then_inc(product_ready.sem, 1)

                        for_chunks(dve, FT, body)
                        split2 = ahead(split_lo, dve, n1, 2 * KT, 1)

                        with dve.Fori(0, KT // 2 - 1) as i:
                            for v in range(2):
                                split2(i * 2 + v, 0)
                                split2(i * 2 + v, 1)
                                dve.wait_ge(chunk_used.sem, i * 4 + (PRIME + n1 + 2 * v + 2))
                                residual(dve, i * 2 + v, v)
                        for n in range(KT - 2, KT):
                            split2(n, 0)
                            split2(n, 1)
                            dve.wait_ge(chunk_used.sem, n * 2 + (PRIME + n1 + 2))
                            residual(dve, n, n % 2)
                        norm_vector(dve, rstd)

                    @block.gpsimd
                    def _(pool):
                        def body(i, u):
                            j = i * 2 + u
                            pool.wait_ge(rounded.sem, rounded.at(1) + j)
                            pool.tensor_tensor(g_lo[:, j, :], prod[:, u, :], g_hi[:, j, :].bitcast(F32),
                                               ALU.subtract).then_inc(rest_ready.sem, 1)

                        for_chunks(pool, FT, body)
                        zsum_pool(pool, acc)
                        norm_pool(pool, FT)
            end_stage(chunk_used=0, act_ready=FT, product_ready=FT, rounded=FT + KT, rest_ready=FT, z_ready=KT, **NORM)


        def mixer_out(l):
            n0 = c_next[0]
            n = KT // 2
            c_next[0] = n0 + n
            scope = ExitStack()
            with scope:
                nm = f"o{stage_no[0]}_"
                sq = sb(nm + "sq", [P, 2, S], F32, scope)
                acc = sb(nm + "acc", [P, S], F32, scope)
                rstd = sb(nm + "rstd", [P, S], F32, scope)
                hi, lo = x_parts()
                with nc.Block() as block:
                    @block.sync
                    def _(sp):
                        for_chunks(sp, n, ahead(fetch, sp, n0, n, 2), peel=n)

                    @block.tensor
                    def _(pe):
                        for j in range(n):
                            u = j % 2
                            s = (n0 + u) % 2
                            pe.wait_ge(lo_ready.sem, PRIME + n0 + j + 1)
                            pe.wait_ge(z_ready.sem, z_ready.at(2 * j - 2))
                            linear(pe, bank[2 * u][:, :], s, 0, range(KT), hi, lo).then_inc(psum_ready.sem, 1)
                            linear(pe, bank[2 * u + 1][:, :], s, KT * P, range(KT), hi, lo)\
                                .then_inc(chunk_used.sem, 1)
                        norm_tensor(pe, acc, sq)

                    @block.scalar
                    def _(act):
                        for_chunks(act, n, ahead(split_hi, act, n0, n, 1), peel=n)
                        norm_scalar(act, sq, rstd, l, 1)

                    @block.vector
                    def _(dve):
                        split = ahead(split_lo, dve, n0, n, 1)
                        for j in range(n):
                            split(j // 2, j % 2)
                            for v in range(2):
                                if v == 0:
                                    dve.wait_ge(psum_ready.sem, psum_ready.at(j + 1))
                                else:
                                    dve.wait_ge(chunk_used.sem, PRIME + n0 + j + 1)
                                k = 2 * j + v
                                dve.scalar_tensor_tensor(
                                    out=X[:, k, :], in0=bank[2 * (j % 2) + v][:, :], scalar=1.0 / ALPHA,
                                    in1=X[:, k, :], op0=ALU.mult, op1=ALU.add).then_inc(z_ready.sem, 1)
                        norm_vector(dve, rstd)

                    @block.gpsimd
                    def _(pool):
                        zsum_pool(pool, acc)
                        norm_pool(pool, 0)
            end_stage(psum_ready=n, z_ready=KT, rounded=KT, **NORM)


        def project(pe, n0, n, hi, lo):
            def body(i, u):
                s = (n0 + u) % 2
                pe.wait_ge(lo_ready.sem, i * 2 + (PRIME + n0 + u + 1))
                pe.wait_ge(bank_free[u].sem, bank_free[u].at(0) + i)
                linear(pe, bank[2 * u][:, :], s, 0, range(KT), hi, lo)
                linear(pe, bank[2 * u + 1][:, :], s, KT * P, range(KT), hi, lo).then_inc(chunk_used.sem, 1)
            for_chunks(pe, n, body)

        def causal_conv(dve, chain, out, src, name, tiles, t):
            w = [col(f"{name}_w", j * tiles + t) for j in range(4)]
            chain.add(dve.tensor_scalar(out, src, w[3], col(f"{name}_b", t), ALU.mult, ALU.add))
            for j in (2, 1, 0):
                d = 3 - j
                chain.wait()
                ins = dve.scalar_tensor_tensor(out=out[:, d:S], in0=src[:, 0:S - d], scalar=w[j], in1=out[:, d:S],
                                               op0=ALU.mult, op1=ALU.add)
                chain.add(ins)
            chain.wait()

        def even_mixer(l):
            n0 = c_next[0]
            n = EVEN_TILES // 2
            c_next[0] = n0 + n
            scope = ExitStack()
            with scope:
                U = sb("rg_u", [P, 4, S], F32, scope)
                RG = sb("rg_gelu", [P, 4, S], F32, scope)
                QK = sb("ml_qk", [P, 8, S], F32, scope)
                V = sb("ml_v", [P, 4, S], F32, scope)
                O = sb("ml_o", [P, 4, S], F32, scope)
                rows = sb("ml_rows", [4, 2, S], F32, scope)
                hi, lo = x_parts()

                with nc.Block() as block:
                    @block.sync
                    def _(sp):
                        for_chunks(sp, n, ahead(fetch, sp, n0, n, 2))

                    @block.tensor
                    def _(pe):
                        project(pe, n0, n, hi, lo)

                    @block.scalar
                    def _(act):
                        split = ahead(split_hi, act, n0, n, 1)
                        todo = {2: (RG, 0, ACT.Gelu_apprx_tanh), 3: (RG, 2, ACT.Gelu_apprx_tanh),
                                8: (V, 0, ACT.Copy), 9: (V, 2, ACT.Copy),
                                10: (O, 0, ACT.Sigmoid), 11: (O, 2, ACT.Sigmoid)}
                        for j in range(n):
                            split(j // 2, j % 2)
                            if j not in todo and j != n - 1:
                                continue
                            act.wait_ge(chunk_used.sem, PRIME + n0 + j + 1)
                            b = 2 * (j % 2)
                            if j < n - 1:
                                out, k, f = todo[j]
                                act.activation(out[:, k, :], bank[b][:, :], f)
                                act.activation(out[:, k + 1, :], bank[b + 1][:, :], f)\
                                    .then_inc(bank_free[j % 2].sem, 1)
                            else:
                                act.activation(rows[:, 0, :], bank[b][0:4, :], ACT.Identity,
                                               bias=col("ml_i_bias")[0:4])
                                act.activation(rows[:, 1, :], bank[b + 1][0:4, :], ACT.Identity,
                                               bias=col("ml_f_bias")[0:4]).then_inc(bank_free[j % 2].sem, 1)

                    @block.vector
                    def _(dve):
                        split = ahead(split_lo, dve, n0, n, 1)
                        chain = Chain(dve, dve_chain)
                        todo = {0: (U, 0, "rg_conv", 4), 1: (U, 2, "rg_conv", 4)}
                        todo |= {4 + j: (QK, 2 * j, "ml_conv", 8) for j in range(4)}
                        for j in range(n):
                            split(j // 2, j % 2)
                            if j in todo:
                                out, k, name, tiles = todo[j]
                                dve.wait_ge(chunk_used.sem, PRIME + n0 + j + 1)
                                for v in range(2):
                                    causal_conv(dve, chain, out[:, k + v, :], bank[2 * (j % 2) + v][:, :], name, tiles, k + v)
                                dve.sem_inc(bank_free[j % 2].sem, 1)
                end_stage(bank_free0=7, bank_free1=6, dve_chain=6 * 8)

                rg_lru(U, RG)
                mlstm(QK, V, O, rows)
            mixer_out(l)

        def rg_lru(U, RG):
            with ExitStack() as scope:
                R = sb("rg_r", [P, 4, S], F32, scope)
                I = sb("rg_i", [P, 4, S], F32, scope)
                TH = sb("rg_th", [P, 4, S], F32, scope)
                E = sb("rg_e", [P, 4, S], F32, scope)
                H = sb("rg_h", [P, 4, S], F32, scope)
                rate = sb("rg_rate", [P, 8], F32, scope)
                wab = sb("rg_w", [P, 8, P], F32, scope)
                with nc.Block() as block:
                    @block.sync
                    def _(sp):
                        sp.dma_start(wab[:, :, :], t["rg_w"]).then_inc(loads_done, 16)

                    @block.tensor
                    def _(pe):
                        pe.wait_ge(loads_done, loads.at(16))
                        for k in range(4):
                            pe.matmul(bank[k][:, :], wab[:, k, :], U[:, k, :], start=True, stop=True)\
                                .then_inc(psum_ready.sem, 1)
                            pe.matmul(bank[4 + k][:, :], wab[:, 4 + k, :], U[:, k, :], start=True, stop=True)\
                                .then_inc(psum_ready.sem, 1)

                    @block.scalar
                    def _(act):
                        lam = cols[:, col_at["rg_lambda"]:col_at["rg_lambda"] + 4]
                        ch = Chain(act, act_chain)
                        ch.add(act.activation(rate[:, 0:4], lam, ACT.Abs))
                        ch.wait()
                        ch.add(act.activation(rate[:, 0:4], rate[:, 0:4], ACT.Exp, scale=-1.0))
                        ch.wait()
                        act.activation(rate[:, 0:4], rate[:, 0:4], ACT.Ln, bias=1.0).then_inc(decay_ready.sem, 1)
                        for k in range(4):
                            act.wait_ge(psum_ready.sem, psum_ready.at(2 * k + 2))
                            act.activation(R[:, k, :], bank[k][:, :], ACT.Sigmoid, bias=col("rg_ba", k))
                            act.activation(I[:, k, :], bank[4 + k][:, :], ACT.Sigmoid, bias=col("rg_bx", k))\
                                .then_inc(gates_ready.sem, 1)
                        act.wait_ge(gates_ready.sem, gates_ready.at(4))
                        act.wait_ge(inflow_ready.sem, inflow_ready.at(1))
                        for k in range(4):
                            act.activation(TH[:, k, :], R[:, k, :], ACT.Tanh, scale=rate[:, k:k + 1])\
                                .then_inc(gates_ready.sem, 1)
                        for k in range(4):
                            act.activation(E[:, k, :], R[:, k, :], ACT.Exp, scale=rate[:, 4 + k:5 + k])\
                                .then_inc(gates_ready.sem, 1)
                        act.wait_ge(gates_ready.sem, gates_ready.at(12))
                        for k in range(4):
                            act.activation(R[:, k, :], TH[:, k, :], ACT.Sqrt).then_inc(gates_ready.sem, 1)
                        for k in range(4):
                            act.wait_ge(y_ready.sem, y_ready.at(k + 1))
                            act.activation(x_hi[:, k, :], H[:, k, :], ACT.Copy).then_inc(rounded.sem, 1)

                    @block.vector
                    def _(dve):
                        ch = Chain(dve, dve_chain)
                        lam = cols[:, col_at["rg_lambda"]:col_at["rg_lambda"] + 4]
                        ch.add(dve.tensor_scalar(rate[:, 4:8], lam, -1.0, 0.0, ALU.mult, ALU.max))
                        dve.wait_ge(decay_ready.sem, decay_ready.at(1))
                        ch.wait()
                        ch.add(dve.tensor_tensor(rate[:, 0:4], rate[:, 0:4], rate[:, 4:8], ALU.add))
                        ch.wait()
                        ch.add(dve.tensor_scalar(rate[:, 4:8], rate[:, 0:4], -8.0, None, ALU.mult))
                        ch.wait()
                        dve.tensor_scalar(rate[:, 0:4], rate[:, 0:4], 4.0, None, ALU.mult).then_inc(inflow_ready.sem, 1)
                        for k in range(4):
                            dve.wait_ge(gates_ready.sem, gates_ready.at(4 + 4 + k + 1))
                            ch.add(dve.tensor_scalar(E[:, k, :], E[:, k, :], 1.0, None, ALU.add))
                            ch.add(dve.tensor_tensor(I[:, k, :], I[:, k, :], U[:, k, :], ALU.mult))
                            ch.wait()
                            ch.add(dve.tensor_tensor(I[:, k, :], I[:, k, :], E[:, k, :], ALU.mult))
                            ch.add(dve.tensor_tensor(E[:, k, :], TH[:, k, :], E[:, k, :], ALU.mult))
                            dve.wait_ge(gates_ready.sem, gates_ready.at(12 + k + 1))
                            ch.wait()
                            ch.add(dve.tensor_scalar(E[:, k, :], E[:, k, :], -1.0, 1.0, ALU.mult, ALU.add))
                            ch.add(dve.tensor_tensor(I[:, k, :], I[:, k, :], R[:, k, :], ALU.mult))
                            ch.wait()
                            ch.add(dve.tensor_tensor_scan(H[:, k, :], E[:, k, :], I[:, k, :], 0.0, ALU.mult, ALU.add))
                            ch.wait()
                            dve.tensor_tensor(H[:, k, :], H[:, k, :], RG[:, k, :], ALU.mult).then_inc(y_ready.sem, 1)

                    @block.gpsimd
                    def _(pool):
                        for k in range(4):
                            pool.wait_ge(rounded.sem, rounded.at(k + 1))
                            pool.tensor_tensor(x_lo[:, k, :], H[:, k, :], x_hi[:, k, :].bitcast(F32), ALU.subtract)
                loads.advance(16)
                end_stage(psum_ready=8, act_chain=2, decay_ready=1, gates_ready=16, inflow_ready=1, y_ready=4,
                          rounded=4, dve_chain=3 + 4 * 7)

        def mlstm(QK, V, O, rows):
            H4, ST = 4, S // P
            scale = float(P) ** -0.5
            with ExitStack() as scope:
                VT = sb("ml_vt", [P, ST, S], F32, scope)
                fr = sb("ml_fr", [4, 6, S], F32, scope)
                ucol = sb("ml_ucol", [P, ST * 4], F32, scope)
                W = sb("ml_w", [P, ST, S], F32, scope)
                EM = sb("ml_em", [P, S], F32, scope)
                H = sb("ml_h", [P, 2, S], F32, scope)
                work = sb("ml_work", [P, 2, S], F32, scope)
                ident = const["identity"]

                def span(st):
                    return slice(st * P, S)

                with nc.Block() as block:
                    @block.tensor
                    def _(pe):
                        for st in range(ST):
                            for h in range(H4):
                                mm = pe.transpose(bank[st][:, h * P:(h + 1) * P], V[:, h, st * P:(st + 1) * P], ident)
                            mm.then_inc(vt_psum.sem, 1)
                        pe.wait_ge(u_ready.sem, u_ready.at(1))
                        for st in range(ST):
                            mm = pe.transpose(bank[4][:, st * 4:st * 4 + 4], fr[:, 2, st * P:(st + 1) * P], ident[0:4, 0:4])
                        mm.then_inc(vt_psum.sem, 1)
                        pe.wait_ge(frame_ready.sem, frame_ready.at(1))
                        pe.wait_ge(vt_ready.sem, vt_ready.at(ST + 1))
                        pe.wait_ge(qk_ready.sem, qk_ready.at(8))

                        def front(h):
                            pe.wait_ge(weight_arg.sem, weight_arg.at(ST * h))
                            pe.wait_ge(floor_ready.sem, floor_ready.at(h))
                            pe.matmul(bank[6][:, :], const[f"pick{h}"][0:4], fr[:, 3, :], start=True, stop=True)
                            pe.matmul(bank[7][:, :], const[f"pick{h}"][0:4], fr[:, 4, :], start=True, stop=True)\
                                .then_inc(psum_ready.sem, 1)
                            pe.wait_ge(weight_ready.sem, weight_ready.at(2 * ST * h))
                            for st in range(ST):
                                pe.matmul(bank[st][:, span(st)], QK[:, 4 + h, st * P:(st + 1) * P], QK[:, h, span(st)],
                                          start=True, stop=True).then_inc(score_ready.sem, 1)

                        front(0)
                        for h in range(H4):
                            pe.wait_ge(pair_ready.sem, pair_ready.at(h))
                            for st in range(ST):
                                pe.wait_ge(masked.sem, masked.at(ST * h + st + 1))
                                pe.matmul(bank[4][:, span(st)], VT[:, st, h * P:(h + 1) * P], W[:, st, span(st)],
                                          start=st == 0, stop=st == ST - 1)
                                mm = pe.matmul(bank[5][:, span(st)], const["ones"], W[:, st, span(st)],
                                               start=st == 0, stop=st == ST - 1)
                            mm.then_inc(attended.sem, 1)
                            if h + 1 < H4:
                                front(h + 1)
                            pe.wait_ge(h_ready.sem, h_ready.at(h + 1))
                            pe.matmul(bank[4][:, :], const["mean_p"], H[:, h % 2, :], start=True, stop=True)\
                                .then_inc(mean_ready.sem, 1)
                            pe.wait_ge(square_ready.sem, square_ready.at(h + 1))
                            pe.matmul(bank[5][:, :], const["mean_p"], work[:, 0, :], start=True, stop=True)\
                                .then_inc(square_used.sem, 1)

                    @block.scalar
                    def _(act):
                        ch = Chain(act, act_chain)
                        ch.add(act.activation(fr[:, 0, :], rows[:, 1, :], ACT.Abs))
                        ch.wait()
                        ch.add(act.activation(fr[:, 0, :], fr[:, 0, :], ACT.Exp, scale=-1.0))
                        ch.wait()
                        act.activation(fr[:, 0, :], fr[:, 0, :], ACT.Ln, bias=1.0).then_inc(rows_ready.sem, 1)
                        for k in range(8):
                            act.activation(QK[:, k, :], QK[:, k, :], ACT.Silu).then_inc(qk_ready.sem, 1)
                        for st in range(ST):
                            act.wait_ge(vt_psum.sem, vt_psum.at(st + 1))
                            act.activation(VT[:, st, :], bank[st][:, :], ACT.Copy).then_inc(vt_ready.sem, 1)
                        act.wait_ge(vt_psum.sem, vt_psum.at(ST + 1))
                        act.activation(ucol[:, :], bank[4][:, 0:4 * ST], ACT.Copy).then_inc(vt_ready.sem, 1)

                        def tail(h):
                            act.wait_ge(centred.sem, centred.at(h + 1))
                            act.activation(work[:, 0, :], H[:, h % 2, :], ACT.Square).then_inc(square_ready.sem, 1)
                            act.wait_ge(square_used.sem, square_used.at(h + 1))
                            act.activation(work[:, 1, :], bank[5][:, :], ACT.Ln, bias=col("eps_ml"))\
                                .then_inc(scale_ready.sem, 1)
                            act.wait_ge(scale_ready.sem, scale_ready.at(2 * h + 1))
                            act.activation(work[:, 1, :], work[:, 1, :], ACT.Exp, scale=-0.5)\
                                .then_inc(scale_ready.sem, 1)
                            act.wait_ge(y_ready.sem, y_ready.at(h + 1))
                            act.activation(x_hi[:, 4 + h, :], H[:, h % 2, :], ACT.Copy).then_inc(rounded.sem, 1)

                        for h in range(H4):
                            act.wait_ge(psum_ready.sem, psum_ready.at(h + 1))
                            act.wait_ge(h_ready.sem, h_ready.at(h))
                            act.activation(EM[:, :], bank[7][:, :], ACT.Exp, scale=-1.0).then_inc(floor_ready.sem, 1)
                            for st in range(ST):
                                act.wait_ge(weight_arg.sem, weight_arg.at(ST * h + st + 1))
                                act.activation(W[:, st, span(st)], W[:, st, span(st)], ACT.Exp, scale=-1.0)\
                                    .then_inc(weight_ready.sem, 1)
                            if h:
                                tail(h - 1)
                        tail(H4 - 1)

                    @block.vector
                    def _(dve):
                        ch = Chain(dve, dve_chain)
                        one = ch.add(dve.memset(fr[:, 5, :], 1.0))
                        dve.wait_ge(rows_ready.sem, rows_ready.at(1))
                        ch.add(dve.tensor_scalar(rows[:, 1, :], rows[:, 1, :], 0.0, None, ALU.min))
                        ch.wait()
                        ch.add(dve.tensor_tensor(fr[:, 0, :], rows[:, 1, :], fr[:, 0, :], ALU.subtract))
                        ch.wait()
                        ch.add(dve.tensor_tensor_scan(fr[:, 1, :], fr[:, 5, :], fr[:, 0, :], 0.0, ALU.mult, ALU.add))
                        ch.wait()
                        ch.add(dve.tensor_tensor(fr[:, 2, :], rows[:, 0, :], fr[:, 1, :], ALU.subtract))
                        ch.wait()
                        dve.sem_inc(u_ready.sem, 1)
                        ch.add(dve.tensor_tensor_scan(fr[:, 3, :], fr[:, 2, :], fr[:, 2, :], 0.0, ALU.max, ALU.max))
                        ch.wait()
                        dve.tensor_tensor(fr[:, 4, :], fr[:, 1, :], fr[:, 3, :], ALU.add).then_inc(frame_ready.sem, 1)
                        dve.wait_ge(vt_ready.sem, vt_ready.at(ST + 1))

                        def tail(h):
                            hb = H[:, h % 2, :]
                            dve.wait_ge(mean_ready.sem, mean_ready.at(h + 1))
                            dve.tensor_tensor(hb, hb, bank[4][:, :], ALU.subtract).then_inc(centred.sem, 1)
                            dve.wait_ge(scale_ready.sem, scale_ready.at(2 * h + 2))
                            ch.add(dve.scalar_tensor_tensor(out=hb, in0=hb, scalar=col("ml_norm_g", h), in1=work[:, 1, :],
                                                            op0=ALU.mult, op1=ALU.mult))
                            ch.wait()
                            dve.sem_inc(pair_ready.sem, 1)
                            dve.tensor_tensor(hb, hb, O[:, h, :], ALU.mult).then_inc(y_ready.sem, 1)

                        for h in range(H4):
                            dve.wait_ge(psum_ready.sem, psum_ready.at(h + 1))
                            dve.wait_ge(attended.sem, attended.at(h))
                            for st in range(ST):
                                dve.tensor_scalar(W[:, st, span(st)], bank[6][:, span(st)],
                                                  ucol[:, st * 4 + h:st * 4 + h + 1], 0.0, ALU.subtract, ALU.max)\
                                    .then_inc(weight_arg.sem, 1)
                            if h:
                                tail(h - 1)
                            for st in range(ST):
                                dve.wait_ge(score_ready.sem, score_ready.at(ST * h + st + 1))
                                dve.wait_ge(weight_ready.sem, weight_ready.at(2 * ST * h + ST))
                                dve.scalar_tensor_tensor(out=W[:, st, span(st)], in0=bank[st][:, span(st)], scalar=scale,
                                                         in1=W[:, st, span(st)], op0=ALU.mult, op1=ALU.mult)\
                                    .then_inc(weight_ready.sem, 1)
                            dve.wait_ge(attended.sem, attended.at(h + 1))
                            hb = H[:, h % 2, :]
                            dve.wait_ge(floor_ready.sem, floor_ready.at(h + 1))
                            dve.wait_ge(rest_ready.sem, rest_ready.at(h - 1))
                            ch.add(dve.tensor_tensor(hb, bank[5][:, :], EM[:, :], ALU.max))
                            ch.wait()
                            ch.add(dve.scalar_tensor_tensor(out=hb, in0=bank[5][:, :], scalar=-1.0, in1=hb,
                                                            op0=ALU.mult, op1=ALU.max))
                            ch.wait()
                            ch.add(dve.reciprocal(hb, hb))
                            ch.wait()
                            dve.tensor_tensor(hb, bank[4][:, :], hb, ALU.mult).then_inc(h_ready.sem, 1)
                        tail(H4 - 1)

                    @block.gpsimd
                    def _(pool):
                        def split_y(h):
                            pool.wait_ge(rounded.sem, rounded.at(h + 1))
                            pool.tensor_tensor(x_lo[:, 4 + h, :], H[:, h % 2, :], x_hi[:, 4 + h, :].bitcast(F32),
                                               ALU.subtract).then_inc(rest_ready.sem, 1)

                        for h in range(H4):
                            for st in range(ST):
                                pool.wait_ge(weight_ready.sem, weight_ready.at(2 * ST * h + ST + st + 1))
                                d = W[:, st, st * P:(st + 1) * P]
                                pool.affine_select(out=d, in_=d, pattern=[[1, P]], compare_op=ALU.is_ge, fill=0.0,
                                                   base=0, channel_multiplier=-1).then_inc(masked.sem, 1)
                            if h:
                                split_y(h - 1)
                        split_y(H4 - 1)
                end_stage(vt_psum=ST + 1, vt_ready=ST + 1, u_ready=1, frame_ready=1, rows_ready=1, qk_ready=8,
                          psum_ready=H4, score_ready=ST * H4, weight_arg=ST * H4, weight_ready=2 * ST * H4,
                          floor_ready=H4, masked=ST * H4, attended=H4, h_ready=H4, mean_ready=H4, centred=H4,
                          square_ready=H4, square_used=H4, scale_ready=2 * H4, y_ready=H4, pair_ready=H4, rounded=H4,
                          rest_ready=H4, act_chain=2, dve_chain=6 + 4 * H4)


        def odd_mixer(l):
            n0 = c_next[0]
            n = ODD_TILES // 2
            c_next[0] = n0 + n
            scope = ExitStack()
            with scope:
                RK = sb("rk_p", [P, 13, S], F32, scope)
                one_less = sb("rk_one_less", [P, 17], F32, scope)
                inner = ExitStack()
                with inner:
                    GQ = sb("gla_q", [P, 2, S], F32, inner)
                    GK = sb("gla_k", [P, 2, S], F32, inner)
                    GV = sb("gla_v", [P, 4, S], F32, inner)
                    GD = sb("gla_gd", [16, S], F32, inner)
                    GO = sb("gla_og", [P, 4, S], F32, inner)
                    hi, lo = x_parts()
                    dest = [(RK, k) for k in range(13)] + [(GQ, 0), (GQ, 1), (GK, 0), (GK, 1)]
                    dest += [(GV, k) for k in range(4)] + [(GD, None)] + [(GO, k) for k in range(4)]

                    with nc.Block() as block:
                        @block.sync
                        def _(sp):
                            for_chunks(sp, n, ahead(fetch, sp, n0, n, 2))

                        @block.tensor
                        def _(pe):
                            project(pe, n0, n, hi, lo)

                        @block.scalar
                        def _(act):
                            split = ahead(split_hi, act, n0, n, 1)
                            for j in range(n):
                                split(j // 2, j % 2)
                                if j < 6:
                                    continue
                                act.wait_ge(chunk_used.sem, PRIME + n0 + j + 1)
                                for v in range(2):
                                    out, k = dest[2 * j + v]
                                    b = bank[2 * (j % 2) + v]
                                    if out is RK:
                                        act.wait_ge(product_ready.sem, product_ready.at(1))
                                        continue
                                    if out is GD:
                                        ins = act.activation(GD[:, :], b[0:16, :], ACT.Copy)
                                    else:
                                        ins = act.activation(out[:, k, :], b[:, :], ACT.Silu if out is GO else ACT.Copy)
                                ins.then_inc(bank_free[j % 2].sem, 1)

                        @block.vector
                        def _(dve):
                            ch = Chain(dve, dve_chain)
                            split = ahead(split_lo, dve, n0, n, 1)
                            mu = cols[:, col_at["rk_mu"]:col_at["rk_mu"] + 13]
                            ka = cols[:, col_at["rk_k_a"]:col_at["rk_k_a"] + 4]
                            ch.add(dve.tensor_scalar(one_less[:, 0:13], mu, -1.0, 1.0, ALU.mult, ALU.add))
                            ch.add(dve.tensor_scalar(one_less[:, 13:17], ka, -1.0, 1.0, ALU.mult, ALU.add))
                            ch.wait()
                            for j in range(n):
                                split(j // 2, j % 2)
                                if j > 6:
                                    continue
                                dve.wait_ge(chunk_used.sem, PRIME + n0 + j + 1)
                                for v in range(2 if j < 6 else 1):
                                    k, b = 2 * j + v, bank[2 * (j % 2) + v]
                                    ch.add(dve.tensor_scalar(RK[:, k, :], b[:, :], one_less[:, k:k + 1], None, ALU.mult))
                                    ch.wait()
                                    ins = dve.scalar_tensor_tensor(
                                        out=RK[:, k, 1:S], in0=b[:, 0:S - 1], scalar=col("rk_mu", k), in1=RK[:, k, 1:S],
                                        op0=ALU.mult, op1=ALU.add)
                                    ch.add(ins)
                                ch.wait()
                                dve.sem_inc((bank_free[j % 2] if j < 6 else product_ready).sem, 1)
                    end_stage(bank_free0=7, bank_free1=6, product_ready=1, dve_chain=2 + 2 * 13)
                    gla(GQ, GK, GV, GD, GO)
                rwkv(RK, one_less)
            mixer_out(l)

        def gla(GQ, GK, GV, GD, GO):
            C, NB, H4 = 64, S // P, 4
            NC = S // C
            tau = 1.0 / 16.0
            with ExitStack() as scope:
                Z = sb("gla_z", [P, 2, S], F32, scope)
                CUM = sb("gla_cum", [P, 2, S], F32, scope)
                E1 = sb("gla_e1", [P, 2, S], F32, scope)
                E2 = sb("gla_e2", [P, 2, S], F32, scope)
                K2 = sb("gla_k2", [P, 2, S], F32, scope)
                VT = sb("gla_vt", [P, NB, S], F32, scope)
                K2T = sb("gla_k2t", [P, 2, S], F32, scope)
                ST = sb("gla_state", [P, NC + 1, 2 * P], F32, scope)
                dec = sb("gla_dec", [P, 2, NC], F32, scope)
                gB = sb("gla_gB", [16, 2 * P], F32, scope)
                reset = sb("gla_reset", [P, S], F32, scope)
                mask = sb("gla_mask", [P, P], F32, scope)
                AT = GV
                H, work = Z, E1
                ident = const["identity"]

                def chunks(ap):
                    return ap.rearrange("p k (c s) -> p k c s", s=C)

                with nc.Block() as block:
                    @block.sync
                    def _(sp):
                        sp.dma_start(gB[:, :], t["gla_gB"]).then_inc(loads_done, 16)
                        sp.dma_start(reset[:, :], t["masks"][:, S:2 * S]).then_inc(loads_done, 16)
                        sp.dma_start(mask[:, :], t["masks"][:, 2 * S + 2 * P:2 * S + 3 * P]).then_inc(loads_done, 16)

                    @block.tensor
                    def _(pe):
                        pe.wait_ge(loads_done, loads.at(48))
                        for k in range(2):
                            mm = pe.matmul(bank[k][:, :], gB[:, k * P:(k + 1) * P], GD[:, :], start=True, stop=True)
                        mm.then_inc(psum_ready.sem, 1)
                        for b in range(NB):
                            for h in range(H4):
                                mm = pe.transpose(bank[2 + b][:, h * P:(h + 1) * P], GV[:, h, b * P:(b + 1) * P], ident)
                            mm.then_inc(vt_psum.sem, 1)
                        pe.wait_ge(decay_ready.sem, decay_ready.at(3))
                        for b in range(NB):
                            for k in range(2):
                                at = 256 * (b % 2) + P * k
                                mm = pe.transpose(bank[b // 2][:, at:at + P], K2[:, k, b * P:(b + 1) * P], ident)
                            if b % 2:
                                mm.then_inc(vt_psum.sem, 1)
                        for b in range(NB):
                            pe.wait_ge(vt_ready.sem, vt_ready.at(NB))
                            for h in range(H4):
                                f, k, tok = slice(64 * (h % 2), 64 * (h % 2) + 64), h // 2, slice(b * P, (b + 1) * P)
                                at = 256 * (b % 2) + P * k
                                mm = pe.matmul(bank[2 + b // 2 * 2 + h % 2][:, at:at + P], GK[f, k, tok], GQ[f, k, tok],
                                               start=True, stop=True)
                            mm.then_inc(score_ready.sem, 1)
                        for b in range(NB):
                            pe.wait_ge(vt_ready.sem, vt_ready.at(NB + 2))
                            for c in range(2):
                                tok = slice(C * c, C * c + C)
                                for h in range(H4):
                                    f, k = slice(64 * (h % 2), 64 * (h % 2) + 64), h // 2
                                    at = 256 * (b % 2) + P * k + 64 * (h % 2)
                                    to = 256 * (b % 2) + P * k
                                    mm = pe.matmul(bank[(6, 0)[b // 2] + c][f, to:to + P], K2T[tok, b // 2, at:at + 64],
                                                   VT[tok, b, h * P:(h + 1) * P], start=True, stop=True)
                            mm.then_inc(qk_ready.sem, 1)
                        pe.wait_ge(masked.sem, masked.at(NB))
                        pe.wait_ge(state_ready.sem, state_ready.at(2 * NC))
                        for h in range(H4):
                            f, k = slice(64 * (h % 2), 64 * (h % 2) + 64), h // 2
                            o = bank[2 + h % 2]
                            pe.wait_ge(h_ready.sem, h_ready.at(h - 1))
                            for b in range(NB):
                                pe.matmul(o[:, b * P:(b + 1) * P], VT[:, b, h * P:(h + 1) * P],
                                          AT[:, b, h * P:(h + 1) * P], start=True, stop=False, skip_group_check=True)
                                for c in (2 * b, 2 * b + 1):
                                    mm = pe.matmul(o[:, c * C:(c + 1) * C], ST[f, c, k * P:(k + 1) * P],
                                                   GQ[f, k, c * C:(c + 1) * C], start=False, stop=c % 2 == 1,
                                                   skip_group_check=True)
                            mm.then_inc(attended.sem, 1)
                            pe.wait_ge(h_ready.sem, h_ready.at(h + 1))
                            pe.matmul(bank[4][:, :], const["mean_p"], H[:, h % 2, :], start=True, stop=True)\
                                .then_inc(mean_ready.sem, 1)
                            pe.wait_ge(square_ready.sem, square_ready.at(h + 1))
                            pe.matmul(bank[5][:, :], const["mean_p"], work[:, 0, :], start=True, stop=True)\
                                .then_inc(square_used.sem, 1)

                    @block.scalar
                    def _(act):
                        ch = Chain(act, act_chain)
                        act.wait_ge(psum_ready.sem, psum_ready.at(1))
                        for k in range(2):
                            ch.add(act.activation(Z[:, k, :], bank[k][:, :], ACT.Identity, bias=col("gla_gb", k)))
                        ch.wait()
                        ch.add(act.activation(E1[:, :, :], Z[:, :, :], ACT.Abs))
                        ch.wait()
                        ch.add(act.activation(E1[:, :, :], E1[:, :, :], ACT.Exp, scale=-1.0))
                        ch.wait()
                        act.activation(E1[:, :, :], E1[:, :, :], ACT.Ln, bias=1.0).then_inc(gates_ready.sem, 1)
                        for b in range(NB):
                            act.wait_ge(vt_psum.sem, vt_psum.at(b + 1))
                            act.activation(VT[:, b, :], bank[2 + b][:, :], ACT.Copy).then_inc(vt_ready.sem, 1)
                        act.wait_ge(frame_ready.sem, frame_ready.at(1))
                        act.activation(E1[:, :, :], CUM[:, :, :], ACT.Exp, scale=tau).then_inc(gates_ready.sem, 1)
                        act.activation(E2[:, :, :], CUM[:, :, :], ACT.Exp, scale=-tau).then_inc(gates_ready.sem, 1)
                        act.activation(dec[:, :, :], CUM[:, :, C - 1::C], ACT.Exp, scale=tau)
                        act.wait_ge(frame_ready.sem, frame_ready.at(2))
                        act.activation(K2[:, :, :], Z[:, :, :], ACT.Exp, scale=tau).then_inc(gates_ready.sem, 1)
                        for n in range(2):
                            act.wait_ge(vt_psum.sem, vt_psum.at(NB + n + 1))
                            act.activation(K2T[:, n, :], bank[n][:, :], ACT.Copy).then_inc(vt_ready.sem, 1)
                        for h in range(H4):
                            hb = H[:, h % 2, :]
                            act.wait_ge(attended.sem, attended.at(h + 1))
                            act.wait_ge(rest_ready.sem, rest_ready.at(h - 1))
                            act.activation(hb, bank[2 + h % 2][:, :], ACT.Copy).then_inc(h_ready.sem, 1)
                            act.wait_ge(centred.sem, centred.at(h + 1))
                            act.activation(work[:, 0, :], hb, ACT.Square).then_inc(square_ready.sem, 1)
                            act.wait_ge(square_used.sem, square_used.at(h + 1))
                            act.activation(work[:, 1, :], bank[5][:, :], ACT.Ln, bias=col("eps_gla"))\
                                .then_inc(scale_ready.sem, 1)
                            act.wait_ge(scale_ready.sem, scale_ready.at(2 * h + 1))
                            act.activation(work[:, 1, :], work[:, 1, :], ACT.Exp, scale=-0.5).then_inc(scale_ready.sem, 1)
                            act.wait_ge(y_ready.sem, y_ready.at(h + 1))
                            act.activation(x_hi[:, 4 + h, :], hb, ACT.Copy).then_inc(rounded.sem, 1)

                    @block.vector
                    def _(dve):
                        ch = Chain(dve, dve_chain)
                        dve.wait_ge(loads_done, loads.at(48))
                        dve.wait_ge(gates_ready.sem, gates_ready.at(1))
                        ch.add(dve.scalar_tensor_tensor(out=Z[:, :, :], in0=Z[:, :, :], scalar=0.0, in1=E1[:, :, :],
                                                        op0=ALU.min, op1=ALU.subtract))
                        ch.wait()
                        for k in range(2):
                            ch.add(dve.tensor_tensor_scan(CUM[:, k, :], reset[:, :], Z[:, k, :], 0.0, ALU.mult, ALU.add))
                        ch.wait()
                        dve.sem_inc(frame_ready.sem, 1)
                        for k in range(2):
                            cum = CUM[:, k, :].rearrange("p (c s) -> p c s", s=C)
                            ins = dve.tensor_tensor(Z[:, k, :].rearrange("p (c s) -> p c s", s=C),
                                                    cum[:, :, C - 1:C].broadcast_to([P, NC, C]), cum, ALU.subtract)
                        ins.then_inc(frame_ready.sem, 1)
                        dve.wait_ge(gates_ready.sem, gates_ready.at(3))
                        dve.scalar_tensor_tensor(out=GQ[:, :, :], in0=GQ[:, :, :], scalar=0.125, in1=E1[:, :, :],
                                                 op0=ALU.mult, op1=ALU.mult).then_inc(decay_ready.sem, 1)
                        dve.wait_ge(gates_ready.sem, gates_ready.at(4))
                        dve.tensor_tensor(K2[:, :, :], K2[:, :, :], GK[:, :, :], ALU.mult).then_inc(decay_ready.sem, 1)
                        dve.wait_ge(decay_ready.sem, decay_ready.at(2))
                        dve.tensor_tensor(GK[:, :, :], E2[:, :, :], GK[:, :, :], ALU.mult).then_inc(decay_ready.sem, 1)
                        dve.wait_ge(vt_psum.sem, vt_psum.at(NB))
                        ch.add(dve.memset(AT[:, :, :], 0.0))
                        ch.add(dve.memset(ST[:, 0, :], 0.0))
                        ch.wait()
                        m = mask[:, :].bitcast(mybir.dt.uint32).unsqueeze(1).broadcast_to([P, 2, P])
                        for b in range(NB):
                            dve.wait_ge(score_ready.sem, score_ready.at(b // 2 * 2 + 2))
                            for r in range(2):
                                src = bank[2 + b // 2 * 2 + r][:, 256 * (b % 2):256 * (b % 2) + 256]
                                ins = dve.copy_predicated(AT[:, b, :].rearrange("p (k r s) -> p k r s", k=2, r=2)[:, :, r, :],
                                                          m, src.rearrange("p (k s) -> p k s", k=2))
                            ins.then_inc(masked.sem, 1)
                        for c in range(NC):
                            b = c // 2
                            dve.wait_ge(qk_ready.sem, qk_ready.at(b // 2 * 2 + 2))
                            if c:
                                dve.wait_ge(state_ready.sem, state_ready.at(2 * c))
                            for k in range(2):
                                at = 256 * (b % 2) + P * k
                                dve.scalar_tensor_tensor(
                                    out=ST[:, c + 1, k * P:(k + 1) * P], in0=ST[:, c, k * P:(k + 1) * P],
                                    scalar=dec[:, k, c:c + 1], in1=bank[(6, 0)[b // 2] + c % 2][:, at:at + P],
                                    op0=ALU.mult, op1=ALU.add).then_inc(state_ready.sem, 1)
                        for h in range(H4):
                            hb = H[:, h % 2, :]
                            dve.wait_ge(mean_ready.sem, mean_ready.at(h + 1))
                            dve.tensor_tensor(hb, hb, bank[4][:, :], ALU.subtract).then_inc(centred.sem, 1)
                            dve.wait_ge(scale_ready.sem, scale_ready.at(2 * h + 2))
                            ch.add(dve.scalar_tensor_tensor(out=hb, in0=hb, scalar=col("gla_norm_g", h), in1=work[:, 1, :],
                                                            op0=ALU.mult, op1=ALU.mult))
                            ch.wait()
                            dve.tensor_tensor(hb, hb, GO[:, h, :], ALU.mult).then_inc(y_ready.sem, 1)

                    @block.gpsimd
                    def _(pool):
                        for h in range(H4):
                            pool.wait_ge(rounded.sem, rounded.at(h + 1))
                            pool.tensor_tensor(x_lo[:, 4 + h, :], H[:, h % 2, :], x_hi[:, 4 + h, :].bitcast(F32),
                                               ALU.subtract).then_inc(rest_ready.sem, 1)
                loads.advance(48)
                end_stage(psum_ready=1, vt_psum=NB + 2, decay_ready=3, vt_ready=NB + 2, score_ready=NB, qk_ready=NB,
                          masked=NB, state_ready=2 * NC, h_ready=H4, attended=H4, mean_ready=H4, square_ready=H4,
                          square_used=H4, act_chain=4, gates_ready=4, frame_ready=2, centred=H4, scale_ready=2 * H4,
                          y_ready=H4, rounded=H4, rest_ready=H4, dve_chain=5 + H4)

        def rwkv(RK, one_less):
            C, NB, H8 = 32, S // P, 8
            NC = S // C
            kappa = float(np.exp(-0.5))
            ident = const["identity"]

            with ExitStack() as scope:
                KD = sb("rk_kd", [P, 4, S], F32, scope)
                BI = sb("rk_bi", [P, 4, S], F32, scope)
                BV = sb("rk_bv", [P, 4, S], F32, scope)
                TT = sb("rk_tt", [P, C, 32], F32, scope)
                last = sb("rk_last", [P, 4, NC], F32, scope)
                masks = sb("rk_masks", [P, 2 * P + C], F32, scope)
                strict, incl, low = masks[:, 0:P], masks[:, P:2 * P], masks[:, 2 * P:2 * P + C]
                rwkv_features(RK, one_less, KD, BI, BV, last, masks, kappa)
                rwkv_solve(KD, BI, TT, low)
                rwkv_chunks(RK, KD, BI, TT, last, strict, incl)
                rwkv_output(RK, KD, BV)

        def rwkv_features(RK, one_less, KD, BI, BV, last, masks, kappa):
            C = 32
            with ExitStack() as scope:
                LW, A, CUM, CE, CI, CP, SQ, RN = (sb("rk_" + n, [P, S], F32, scope) for n in
                                                  ("lw", "a", "cum", "ce", "ci", "cp", "sq", "rn"))
                lora = sb("rk_lora", [P, S], F32, scope)
                reset = sb("rk_reset", [P, S], F32, scope)
                with nc.Block() as block:
                    @block.sync
                    def _(sp):
                        sp.dma_start(lora[:, :], t["rk_lora"]).then_inc(loads_done, 16)
                        sp.dma_start(reset[:, :], t["masks"][:, 0:S]).then_inc(loads_done, 16)
                        sp.dma_start(masks[:, 0:2 * P], t["masks"][:, 2 * S:2 * S + 2 * P]).then_inc(loads_done, 16)
                        sp.dma_start(masks[:, 2 * P:], t["masks"][:, 2 * S + 3 * P:]).then_inc(loads_done, 16)

                    @block.tensor
                    def _(pe):
                        pe.wait_ge(loads_done, loads.at(64))
                        pe.wait_ge(rows_ready.sem, rows_ready.at(1))
                        for k in range(4):
                            w = slice(k * P, (k + 1) * P)
                            pe.wait_ge(gates_ready.sem, gates_ready.at(k))
                            pe.matmul(bank[0][:, :], lora[0:32, w], RK[0:32, 12, :], start=True, stop=True)
                            pe.matmul(bank[1][:, :], lora[32:64, w], RK[32:64, 12, :], start=True, stop=True)\
                                .then_inc(psum_ready.sem, 1)
                            pe.wait_ge(square_ready.sem, square_ready.at(k + 1))
                            pe.matmul(bank[2][:, :], const["half_ones"], SQ[:, :], start=True, stop=True)\
                                .then_inc(square_used.sem, 1)
                            pe.wait_ge(product_ready.sem, product_ready.at(k + 1))
                            pe.matmul(bank[3][:, :], const["half_ones"], SQ[:, :], start=True, stop=True)\
                                .then_inc(attended.sem, 1)

                    @block.scalar
                    def _(act):
                        act.activation(RK[0:32, 12, :], RK[0:32, 12, :], ACT.Tanh)
                        act.activation(RK[64:P, 12, :], RK[64:P, 12, :], ACT.Sigmoid).then_inc(rows_ready.sem, 1)
                        for k in range(4):
                            act.wait_ge(psum_ready.sem, psum_ready.at(k + 1))
                            act.wait_ge(h_ready.sem, h_ready.at(k))
                            act.activation(LW[:, :], bank[0][:, :], ACT.Sigmoid, bias=col("rk_w0", k))
                            act.activation(A[:, :], bank[1][:, :], ACT.Sigmoid, bias=col("rk_a0", k))\
                                .then_inc(gates_ready.sem, 1)
                            act.wait_ge(attended.sem, attended.at(k))
                            act.activation(SQ[:, :], RK[:, 4 + k, :], ACT.Square, scale=col("rk_k_k", k))\
                                .then_inc(square_ready.sem, 1)
                            act.wait_ge(square_used.sem, square_used.at(k + 1))
                            act.activation(RN[:, :], bank[2][:, :], ACT.Sqrt).then_inc(scale_ready.sem, 1)
                            act.wait_ge(frame_ready.sem, frame_ready.at(k + 1))
                            act.activation(CE[:, :], CUM[:, :], ACT.Exp, scale=-kappa)
                            act.activation(CI[:, :], CUM[:, :], ACT.Exp, scale=kappa)
                            act.activation(CP[:, :], CP[:, :], ACT.Exp, scale=-kappa)
                            act.activation(last[:, k, :], CUM[:, C - 1::C], ACT.Exp, scale=-kappa)\
                                .then_inc(decay_ready.sem, 1)

                    @block.vector
                    def _(dve):
                        ch = Chain(dve, dve_chain)
                        dve.wait_ge(loads_done, loads.at(64))
                        for k in range(4):
                            r, key, v = RK[:, k, :], RK[:, 4 + k, :], RK[:, 8 + k, :]
                            dve.wait_ge(gates_ready.sem, gates_ready.at(k + 1))
                            ch.add(dve.tensor_tensor_scan(CUM[:, :], reset[:, :], LW[:, :], 0.0, ALU.mult, ALU.add))
                            ch.wait()
                            dve.tensor_tensor(CP[:, :], CUM[:, :], LW[:, :], ALU.subtract).then_inc(frame_ready.sem, 1)
                            dve.wait_ge(scale_ready.sem, scale_ready.at(k + 1))
                            ch.add(dve.tensor_scalar(RN[:, :], RN[:, :], 1e-12, None, ALU.max))
                            ch.wait()
                            ch.add(dve.reciprocal(RN[:, :], RN[:, :]))
                            ch.wait()
                            ch.add(dve.scalar_tensor_tensor(out=KD[:, k, :], in0=key, scalar=col("rk_k_k", k), in1=RN[:, :],
                                                            op0=ALU.mult, op1=ALU.mult))
                            ch.wait()
                            ch.add(dve.tensor_tensor(BI[:, k, :], KD[:, k, :], A[:, :], ALU.mult))
                            ch.wait()
                            ch.add(dve.tensor_scalar(A[:, :], A[:, :], col("rk_k_a", k), one_less[:, 13 + k:14 + k],
                                                     ALU.mult, ALU.add))
                            ch.wait()
                            ch.add(dve.tensor_tensor(key, key, A[:, :], ALU.mult))
                            ch.wait()
                            dve.scalar_tensor_tensor(out=SQ[:, :], in0=r, scalar=col("rk_r_k", k), in1=key,
                                                     op0=ALU.mult, op1=ALU.mult).then_inc(product_ready.sem, 1)
                            dve.wait_ge(product_ready.sem, product_ready.at(k + 1))
                            dve.wait_ge(decay_ready.sem, decay_ready.at(k + 1))
                            dve.tensor_tensor(r, r, CE[:, :], ALU.mult)
                            dve.tensor_tensor(key, key, CI[:, :], ALU.mult)
                            dve.tensor_tensor(BI[:, k, :], BI[:, k, :], CI[:, :], ALU.mult)
                            dve.tensor_tensor(KD[:, k, :], KD[:, k, :], CP[:, :], ALU.mult)
                            dve.wait_ge(attended.sem, attended.at(k + 1))
                            dve.tensor_tensor(BV[:, k, :], bank[3][:, :], v, ALU.mult).then_inc(h_ready.sem, 1)
                loads.advance(64)
                end_stage(rows_ready=1, gates_ready=4, psum_ready=4, square_ready=4, square_used=4, product_ready=4,
                          attended=4, h_ready=4, scale_ready=4, frame_ready=4, decay_ready=4, dve_chain=4 * 7)

        def rwkv_solve(KD, BI, TT, low):
            C, NB, H8 = 32, S // P, 8
            with ExitStack() as scope:
                LT = sb("rk_l", [P, 32, C], F32, scope)
                LS = sb("rk_ls", [P, C, C], F32, scope)
                T = sb("rk_t", [P, C, C], F32, scope)
                prod = sb("rk_prod", [P, C * C], F32, scope)
                with nc.Block() as block:
                    @block.tensor
                    def _(pe):
                        for g in range(2 * NB):
                            b, tok = g // 2, slice(g // 2 * P, g // 2 * P + P)
                            pe.wait_ge(masked.sem, masked.at(g - 3))
                            for n in range(4):
                                f, k = slice(64 * (g % 2), 64 * (g % 2) + 64), n
                                mm = pe.matmul(bank[g % 4][:, n * P:(n + 1) * P], KD[f, k, tok], BI[f, k, tok],
                                               start=True, stop=True)
                            mm.then_inc(score_ready.sem, 1)

                    @block.vector
                    def _(dve):
                        ch = Chain(dve, dve_chain)
                        for g in range(2 * NB):
                            dve.wait_ge(score_ready.sem, score_ready.at(g + 1))
                            for c in range(4):
                                p = slice(C * c, C * c + C)
                                src = bank[g % 4][p, :].rearrange("p (h s) -> p h s", h=4)[:, :, C * c:C * c + C]
                                ins = dve.tensor_tensor(LT[p, 4 * g:4 * g + 4, :], src,
                                                        low[p, :].unsqueeze(1).broadcast_to([C, 4, C]), ALU.mult)
                            ins.then_inc(masked.sem, 1)
                        ch.add(dve.memset(T[:, :, :], 0.0))
                        ch.wait()
                        ch.add(dve.memset(T[:, :, :].rearrange("p s t -> p (s t)")[:, 0::C + 1], 1.0))
                        dve.wait_ge(masked.sem, masked.at(2 * NB))
                        ch.add(dve.transpose(LS[:, :, :], LT[:, :, :].rearrange("p h s -> p s h")))
                        ch.wait()
                        for i in range(1, C):
                            pr = prod[:, 0:i * i].rearrange("p (j s) -> p j s", s=i)
                            row = LS[:, 0:i, i:i + 1].rearrange("p s o -> p o s").broadcast_to([P, i, i])
                            ch.add(dve.tensor_tensor(pr, T[:, 0:i, 0:i], row, ALU.mult))
                            ch.wait()
                            ch.add(dve.tensor_reduce(T[:, 0:i, i:i + 1], pr, AX_X, ALU.add, negate=True))
                            ch.wait()
                        dve.transpose(TT[:, :, :], T[:, :, :].rearrange("p s t -> p t s"))
                end_stage(masked=2 * NB, score_ready=2 * NB, dve_chain=3 + 2 * (C - 1))

        def rwkv_chunks(RK, KD, BI, TT, last, strict, incl):
            C, NB, H8 = 32, S // P, 8
            ident = const["identity"]
            with ExitStack() as scope:
                M = sb("rk_m", [P, H8, P], F32, scope)
                A1 = sb("rk_a1", [P, H8, P], F32, scope)
                A2 = sb("rk_a2", [P, H8, P], F32, scope)
                BD = sb("rk_bd", [P, H8, P], F32, scope)
                KDT, VT, BT, KT2 = (sb("rk_" + n, [P, S], F32, scope) for n in ("kdt", "vt", "bt", "kt"))
                B2, K2 = (sb("rk_" + n, [P, 4, P], F32, scope) for n in ("b2", "k2"))
                U, U1, SA = (sb("rk_" + n, [P, S], F32, scope) for n in ("u", "u1", "sa"))
                W1 = sb("rk_w1", [P, 4, P], F32, scope)
                ST = sb("rk_state", [P, 5, 4 * 64], F32, scope)
                DS = sb("rk_ds", [P, 4 * 64], F32, scope)

                def heads(h):
                    return slice(64 * (h // 4), 64 * (h // 4) + 64), h % 4

                def cells(h):
                    at = P * (h % 4) + 64 * (h // 4)
                    return slice(at, at + 64)

                with nc.Block() as block:
                    @block.tensor
                    def _(pe):
                        for b in range(NB):
                            tok = slice(b * P, (b + 1) * P)
                            pe.wait_ge(y_ready.sem, y_ready.at(b))
                            pe.wait_ge(state_ready.sem, state_ready.at(4 * b + 1))
                            for x, (lhs, lk, rhs, rk) in enumerate(((RK, 4, KD, 0), (BI, 0, RK, 0), (RK, 4, RK, 0))):
                                for h in range(H8):
                                    f, k = heads(h)
                                    mm = pe.matmul(bank[2 * x + h // 4][:, (h % 4) * P:(h % 4) * P + P],
                                                   lhs[f, lk + k, tok], rhs[f, rk + k, tok], start=True, stop=True)
                                mm.then_inc(score_ready.sem, 1)
                            for x, (src, off) in enumerate(((KD, 0), (RK, 8))):
                                for k in range(4):
                                    mm = pe.transpose(bank[6 + x][:, k * P:(k + 1) * P], src[:, off + k, tok], ident)
                                mm.then_inc(vt_psum.sem, 1)
                            pe.wait_ge(decay_ready.sem, decay_ready.at(2 * (b + 1)))
                            for x, src in enumerate((B2, K2)):
                                pe.wait_ge(vt_ready.sem, vt_ready.at(4 * b + 1 + x))
                                for k in range(4):
                                    mm = pe.transpose(bank[6 + x][:, k * P:(k + 1) * P], src[:, k, :], ident)
                                mm.then_inc(vt_psum.sem, 1)
                            pe.wait_ge(masked.sem, masked.at(3 * b + 1))
                            for h in range(H8):
                                mm = pe.matmul(bank[0][:, cells(h)], M[:, h, :], VT[:, cells(h)], start=True, stop=True)
                            mm.then_inc(attended.sem, 1)
                            pe.wait_ge(frame_ready.sem, frame_ready.at(b + 1))
                            for h in range(H8):
                                f, k = heads(h)
                                mm = pe.matmul(bank[1][f, k * P:(k + 1) * P], KDT[:, cells(h)], BD[:, h, :],
                                               start=True, stop=True)
                            mm.then_inc(attended.sem, 1)
                            pe.wait_ge(masked.sem, masked.at(3 * b + 2))
                            pe.wait_ge(u_ready.sem, u_ready.at(3 * b + 1))
                            for h in range(H8):
                                mm = pe.matmul(bank[2][:, cells(h)], BD[:, h, :], U[:, cells(h)], start=True, stop=True)
                            mm.then_inc(attended.sem, 1)
                            pe.wait_ge(u_ready.sem, u_ready.at(3 * b + 3))
                            pe.wait_ge(masked.sem, masked.at(3 * b + 3))
                            pe.wait_ge(vt_ready.sem, vt_ready.at(4 * b + 4))
                            for c in range(4):
                                g = 4 * b + c
                                p = slice(C * c, C * c + C)
                                pe.wait_ge(state_ready.sem, state_ready.at(g + 1))
                                for h in range(H8):
                                    f, k = heads(h)
                                    mm = pe.matmul(bank[3 - 3 * (h // 4)][p, k * 64:k * 64 + 64], W1[f, k, p],
                                                   ST[f, g % 5, k * 64:k * 64 + 64], start=True, stop=True)
                                mm.then_inc(qk_ready.sem, 1)
                                pe.wait_ge(h_ready.sem, h_ready.at(g + 1))
                                for h in range(H8):
                                    f, k = heads(h)
                                    o = bank[4][f, k * 64:k * 64 + 64]
                                    pe.matmul(o, KT2[p, cells(h)], VT[p, cells(h)], start=True, stop=False)
                                    mm = pe.matmul(o, BT[p, cells(h)], SA[p, cells(h)], start=False, stop=True)
                                mm.then_inc(psum_ready.sem, 1)
                            for h in range(H8):
                                f, k = heads(h)
                                o = bank[5]
                                pe.matmul(o[f, k * P:(k + 1) * P], VT[:, cells(h)], A2[:, h, :], start=True, stop=False,
                                          skip_group_check=True)
                                pe.matmul(o[f, k * P:(k + 1) * P], SA[:, cells(h)], A1[:, h, :], start=False, stop=False,
                                          skip_group_check=True)
                                for c in range(4):
                                    at = b * P + C * c
                                    mm = pe.matmul(o[f, k * P + C * c:k * P + C * c + C],
                                                   ST[f, (4 * b + c) % 5, k * 64:k * 64 + 64], RK[f, k, at:at + C],
                                                   start=False, stop=c == 3, skip_group_check=True)
                            mm.then_inc(pair_ready.sem, 1)

                    @block.scalar
                    def _(act):
                        for b in range(NB):
                            for x, (out, bk) in enumerate(((KDT, 6), (VT, 7), (BT, 6), (KT2, 7))):
                                act.wait_ge(vt_psum.sem, vt_psum.at(4 * b + x + 1))
                                act.activation(out[:, :], bank[bk][:, :], ACT.Copy).then_inc(vt_ready.sem, 1)
                            for x, (out, bk) in enumerate(((U[:, :], 0), (W1[:, :, :], 1), (U1[:, :], 2))):
                                act.wait_ge(attended.sem, attended.at(3 * b + x + 1))
                                src = bank[bk][:, :]
                                if bk == 1:
                                    src = src.rearrange("p (k t) -> p k t", k=4)
                                act.activation(out, src, ACT.Copy).then_inc(u_ready.sem, 1)
                            act.wait_ge(pair_ready.sem, pair_ready.at(b + 1))
                            act.activation(KD[:, :, b * P:(b + 1) * P], bank[5][:, :].rearrange("p (k t) -> p k t", k=4),
                                           ACT.Copy).then_inc(y_ready.sem, 1)

                    @block.gpsimd
                    def _(pool):
                        pool.memset(BD[:, :, :], 0.0).then_inc(pool_zero.sem, 1)
                        for b in range(NB):
                            tok = slice(b * P, (b + 1) * P)
                            if b:
                                pool.wait_ge(vt_psum.sem, vt_psum.at(4 * b))
                            for out, src, off in ((B2, BI, 0), (K2, RK, 4)):
                                for k in range(4):
                                    o = out[:, k, :].rearrange("p (c s) -> p c s", s=C)
                                    i = src[:, off + k, tok].rearrange("p (c s) -> p c s", s=C)
                                    e = last[:, k, 4 * b:4 * b + 4].unsqueeze(2).broadcast_to([P, 4, C])
                                    ins = pool.tensor_tensor(o, i, e, ALU.mult)
                                ins.then_inc(decay_ready.sem, 1)
                            for c in range(4):
                                g = 4 * b + c
                                pool.wait_ge(state_ready.sem, state_ready.at(g + 1))
                                e = last[:, :, g:g + 1].broadcast_to([P, 4, 64])
                                pool.tensor_tensor(DS[:, :].rearrange("p (k i) -> p k i", k=4),
                                                   ST[:, g % 5, :].rearrange("p (k i) -> p k i", k=4), e, ALU.mult)\
                                    .then_inc(rest_ready.sem, 1)

                    @block.vector
                    def _(dve):
                        dve.memset(ST[:, 0, :], 0.0).then_inc(state_ready.sem, 1)
                        dve.wait_ge(pool_zero.sem, pool_zero.at(1))
                        for b in range(NB):
                            for c in range(4):
                                p = slice(C * c, C * c + C)
                                ins = dve.tensor_copy(BD[p, :, p],
                                                      TT[p, :, 8 * b:8 * b + 8].rearrange("p t h -> p h t"))
                            ins.then_inc(frame_ready.sem, 1)
                            for x, (out, m) in enumerate(((M, strict), (A1, incl), (A2, incl))):
                                dve.wait_ge(score_ready.sem, score_ready.at(3 * b + x + 1))
                                for v in range(2):
                                    ins = dve.tensor_tensor(out[:, 4 * v:4 * v + 4, :],
                                                            bank[2 * x + v][:, :].rearrange("p (h t) -> p h t", h=4),
                                                            m.unsqueeze(1).broadcast_to([P, 4, P]), ALU.mult)
                                ins.then_inc(masked.sem, 1)
                            dve.wait_ge(u_ready.sem, u_ready.at(3 * b + 3))
                            for c in range(4):
                                g = 4 * b + c
                                p = slice(C * c, C * c + C)
                                dve.wait_ge(qk_ready.sem, qk_ready.at(g + 1))
                                for r in range(2):
                                    out, u1 = (a[p, :].rearrange("p (k r i) -> p k r i", k=4, r=2)[:, :, r, :] for a in (SA, U1))
                                    ins = dve.scalar_tensor_tensor(
                                        out=out, in0=bank[3 - 3 * r][p, 0:256].rearrange("p (k i) -> p k i", k=4),
                                        scalar=-1.0, in1=u1, op0=ALU.mult, op1=ALU.subtract)
                                ins.then_inc(h_ready.sem, 1)
                                dve.wait_ge(psum_ready.sem, psum_ready.at(g + 1))
                                dve.wait_ge(rest_ready.sem, rest_ready.at(g + 1))
                                dve.tensor_tensor(ST[:, (g + 1) % 5, :], bank[4][:, 0:256], DS[:, :], ALU.add)\
                                    .then_inc(state_ready.sem, 1)
                            dve.wait_ge(pair_ready.sem, pair_ready.at(b + 1))
                end_stage(y_ready=NB, score_ready=3 * NB, vt_psum=4 * NB, decay_ready=2 * NB, vt_ready=4 * NB,
                          masked=3 * NB, attended=3 * NB, frame_ready=NB, u_ready=3 * NB, state_ready=4 * NB + 1,
                          qk_ready=4 * NB, h_ready=4 * NB, psum_ready=4 * NB, pair_ready=NB, pool_zero=1,
                          rest_ready=4 * NB)

        def rwkv_output(RK, Y, BV):
            with ExitStack() as scope:
                lora = sb("rk_lora2", [P, S], F32, scope)
                sq = sb("rk_sq2", [P, S], F32, scope)
                rs = sb("rk_rs", [P, S], F32, scope)
                with nc.Block() as block:
                    @block.sync
                    def _(sp):
                        sp.dma_start(lora[:, :], t["rk_lora"]).then_inc(loads_done, 16)

                    @block.tensor
                    def _(pe):
                        pe.wait_ge(loads_done, loads.at(16))
                        for k in range(4):
                            pe.matmul(bank[k][:, :], lora[64:P, k * P:(k + 1) * P], RK[64:P, 12, :], start=True, stop=True)
                            pe.matmul(bank[4 + k % 2][:, :], const["half_mean"], Y[:, k, :], start=True, stop=True)\
                                .then_inc(mean_ready.sem, 1)
                            pe.wait_ge(square_ready.sem, square_ready.at(k + 1))
                            pe.matmul(bank[6 + k % 2][:, :], const["half_mean"], sq[:, :], start=True, stop=True)\
                                .then_inc(square_used.sem, 1)

                    @block.scalar
                    def _(act):
                        for k in range(4):
                            act.wait_ge(centred.sem, centred.at(k + 1))
                            act.activation(sq[:, :], Y[:, k, :], ACT.Square).then_inc(square_ready.sem, 1)
                            act.wait_ge(square_used.sem, square_used.at(k + 1))
                            act.wait_ge(y_ready.sem, y_ready.at(k))
                            act.activation(rs[:, :], bank[6 + k % 2][:, :], ACT.Ln, bias=col("eps_rk"))\
                                .then_inc(scale_ready.sem, 1)
                            act.wait_ge(scale_ready.sem, scale_ready.at(2 * k + 1))
                            act.activation(rs[:, :], rs[:, :], ACT.Exp, scale=-0.5).then_inc(scale_ready.sem, 1)
                            act.wait_ge(y_ready.sem, y_ready.at(k + 1))
                            act.activation(x_hi[:, k, :], Y[:, k, :], ACT.Copy).then_inc(rounded.sem, 1)

                    @block.vector
                    def _(dve):
                        ch = Chain(dve, dve_chain)
                        for k in range(4):
                            y = Y[:, k, :]
                            dve.wait_ge(mean_ready.sem, mean_ready.at(k + 1))
                            dve.tensor_tensor(y, y, bank[4 + k % 2][:, :], ALU.subtract).then_inc(centred.sem, 1)
                            dve.wait_ge(scale_ready.sem, scale_ready.at(2 * k + 2))
                            ch.add(dve.scalar_tensor_tensor(out=y, in0=y, scalar=col("rk_ln_g", k), in1=rs[:, :],
                                                            op0=ALU.mult, op1=ALU.mult))
                            ch.wait()
                            ch.add(dve.scalar_tensor_tensor(out=y, in0=y, scalar=col("rk_ln_b", k), in1=BV[:, k, :],
                                                            op0=ALU.add, op1=ALU.add))
                            ch.wait()
                            dve.tensor_tensor(y, y, bank[k][:, :], ALU.mult).then_inc(y_ready.sem, 1)

                    @block.gpsimd
                    def _(pool):
                        for k in range(4):
                            pool.wait_ge(rounded.sem, rounded.at(k + 1))
                            pool.tensor_tensor(x_lo[:, k, :], Y[:, k, :], x_hi[:, k, :].bitcast(F32), ALU.subtract)
                loads.advance(16)
                end_stage(mean_ready=4, square_ready=4, square_used=4, centred=4, scale_ready=8, y_ready=4, rounded=4,
                          dve_chain=8)


        def mean_square_tensor(pe, sq, width=S):
            for k in range(KT):
                pe.wait_ge(square_ready.sem, square_ready.at(k + 1))
                pe.matmul(bank[7][:, 0:width], const["mean_d"], sq[:, k % 2, 0:width], start=k == 0,
                          stop=k == KT - 1).then_inc(square_used.sem, 1)

        def squares_scalar(act, src, sq, k, width=S):
            act.wait_ge(square_used.sem, square_used.at(k - 1))
            act.activation(sq[:, k % 2, 0:width], src, ACT.Square).then_inc(square_ready.sem, 1)

        def scale_scalar(act, rs, width=S):
            act.wait_ge(square_used.sem, square_used.at(KT))
            act.activation(rs, bank[7][:, 0:width], ACT.Ln, bias=col("eps_rms")).then_inc(scale_ready.sem, 1)
            act.wait_ge(scale_ready.sem, scale_ready.at(1))
            act.activation(rs, rs, ACT.Exp, scale=-0.5).then_inc(scale_ready.sem, 1)

        RMS = dict(square_ready=KT, square_used=KT, scale_ready=2)

        def rms_split(src, gain, l, out_hi, out_lo, width=S, load=None):
            with ExitStack() as scope:
                nm = f"r{stage_no[0]}_"
                sq = sb(nm + "sq", [P, 2, width], F32, scope)
                rs = sb(nm + "rs", [P, width], F32, scope)
                h = sb(nm + "h", [P, 2, width], F32, scope)
                with nc.Block() as block:
                    if load is not None:
                        @block.sync
                        def _(sp):
                            sp.dma_start(src[:, :, :], load).then_inc(loads_done, 16)

                    @block.tensor
                    def _(pe):
                        mean_square_tensor(pe, sq, width)

                    @block.scalar
                    def _(act):
                        if load is not None:
                            act.wait_ge(loads_done, loads.at(16))
                        for k in range(KT):
                            squares_scalar(act, src[:, k, :], sq, k, width)
                        scale_scalar(act, rs[:, :], width)
                        for k in range(KT):
                            act.wait_ge(scaled.sem, scaled.at(k + 1))
                            act.activation(out_hi[:, k, :], h[:, k % 2, :], ACT.Copy).then_inc(rounded.sem, 1)

                    @block.vector
                    def _(dve):
                        if load is not None:
                            dve.wait_ge(loads_done, loads.at(16))
                        dve.wait_ge(scale_ready.sem, scale_ready.at(2))
                        for k in range(KT):
                            dve.wait_ge(split_ready.sem, split_ready.at(k - 1))
                            dve.scalar_tensor_tensor(out=h[:, k % 2, :], in0=src[:, k, :], scalar=col(gain, l * KT + k),
                                                     in1=rs[:, :], op0=ALU.mult, op1=ALU.mult).then_inc(scaled.sem, 1)

                    @block.gpsimd
                    def _(pool):
                        for k in range(KT):
                            pool.wait_ge(rounded.sem, rounded.at(k + 1))
                            pool.tensor_tensor(out_lo[:, k, :], h[:, k % 2, :], out_hi[:, k, :].bitcast(F32),
                                               ALU.subtract).then_inc(split_ready.sem, 1)
            if load is not None:
                loads.advance(16)
            end_stage(scaled=KT, rounded=KT, split_ready=KT, **RMS)

        def post_norm_vector(dve, y, rs, tmp, gain, l):
            ch = Chain(dve, dve_chain)
            dve.wait_ge(scale_ready.sem, scale_ready.at(2))
            done = [0, 0]
            for k in range(KT):
                if done[k % 2]:
                    ch.wait(done[k % 2])
                ch.add(dve.scalar_tensor_tensor(out=tmp[:, k % 2, :], in0=y(k), scalar=col(gain, l * KT + k), in1=rs,
                                                op0=ALU.mult, op1=ALU.mult))
                ch.wait()
                done[k % 2] = ch.add(dve.tensor_tensor(X[:, k, :], X[:, k, :], tmp[:, k % 2, :], ALU.add))


        def attention(l):
            n0 = c_next[0]
            NQ, NKV, NG, NBR = 10, 2, 12, KT // 2
            c_next[0] = n0 + NQ + NKV + NG + NBR + KT // 2
            outer = ExitStack()
            with outer:
                o_hi = sb(f"o{l}_hi", [P, 6, S], F32R, outer)
                o_lo = sb(f"o{l}_lo", [P, 6, S], F32R, outer)
                inner = ExitStack()
                with inner:
                    KM = sb(f"a{l}_km", [P, 2, 256], F32, inner)
                    VM = sb(f"a{l}_vm", [P, 2, 256], F32, inner)
                    memory_kv(l, n0, KM, VM)
                    rms_split(X, "g_pre_mix_2", l, x_hi, x_lo)
                    Q = sb(f"a{l}_qkv", [P, 20, S], F32, inner)
                    project_qkv(l, n0 + NKV, NQ, Q)
                    attend(l, Q, KM, VM, o_hi, o_lo)
                gated_merge(l, n0 + NQ + NKV, NG, NBR, o_hi, o_lo)

        def project_qkv(l, n0, n, Q):
            hi, lo = x_parts()
            with nc.Block() as block:
                @block.sync
                def _(sp):
                    for_chunks(sp, n, ahead(fetch, sp, n0, n, 2))

                @block.tensor
                def _(pe):
                    project(pe, n0, n, hi, lo)

                @block.scalar
                def _(act):
                    split = ahead(split_hi, act, n0, n, 1)

                    def body(i, u):
                        split(i, u)
                        act.wait_ge(chunk_used.sem, i * 2 + (PRIME + n0 + u + 1))
                        act.activation(Q[:, i * 4 + 2 * u, :], bank[2 * u][:, :], ACT.Copy)
                        act.activation(Q[:, i * 4 + (2 * u + 1), :], bank[2 * u + 1][:, :], ACT.Copy)\
                            .then_inc(bank_free[u].sem, 1)

                    for_chunks(act, n, body)

                @block.vector
                def _(dve):
                    for_chunks(dve, n, ahead(split_lo, dve, n0, n, 1))
            end_stage(bank_free0=(n + 1) // 2, bank_free1=n // 2)

        def memory_kv(l, n0, KM, VM):
            M = 256
            with ExitStack() as scope:
                mem = sb(f"m{l}_mem", [P, KT, M], F32, scope)
                v = sb(f"m{l}_v", [P, 2, M], F32, scope)
                rms_split(mem, "mem_norm_g_2", 0, x_hi[:, :, 0:M], x_lo[:, :, 0:M], M, t["mem"])
                with nc.Block() as block:
                    @block.sync
                    def _(sp):
                        for_chunks(sp, 2, ahead(fetch, sp, n0, 2, 2))

                    @block.tensor
                    def _(pe):
                        for j in range(2):
                            s = (n0 + j) % 2
                            pe.wait_ge(lo_ready.sem, PRIME + n0 + j + 1)
                            for k in range(2):
                                mm = linear(pe, bank[2 * j + k][:, 0:M], s, k * KT * P, range(KT),
                                            lambda i: x_hi[:, i, 0:M], lambda i: x_lo[:, i, 0:M])
                            mm.then_inc(chunk_used.sem, 1)
                        pe.wait_ge(vt_ready.sem, vt_ready.at(1))
                        for m in range(2):
                            for k in range(2):
                                mm = pe.transpose(bank[4][:, m * M + k * P:m * M + (k + 1) * P],
                                                  v[:, k, m * P:(m + 1) * P], const["identity"])
                        mm.then_inc(vt_psum.sem, 1)

                    @block.scalar
                    def _(act):
                        split = ahead(split_hi, act, n0, 2, 1)
                        for j in range(2):
                            split(0, j)
                            act.wait_ge(chunk_used.sem, PRIME + n0 + j + 1)
                            for k in range(2):
                                ins = act.activation((KM, v)[j][:, k, :], bank[2 * j + k][:, 0:M], ACT.Copy)
                        ins.then_inc(vt_ready.sem, 1)
                        act.wait_ge(vt_psum.sem, vt_psum.at(1))
                        act.activation(VM[:, :, :], bank[4][:, :].rearrange("p (m f) -> p m f", m=2), ACT.Copy)

                    @block.vector
                    def _(dve):
                        for_chunks(dve, 2, ahead(split_lo, dve, n0, 2, 1))
                end_stage(vt_ready=1, vt_psum=1)

        def attend(l, Q, KM, VM, o_hi, o_lo):
            scale = 64.0 ** -0.5
            QA, KA, VA_, QB, KB, VB_, QM = 0, 3, 6, 9, 12, 15, 18
            ident = const["identity"]
            RING = 3
            OT = lambda k: Q[:, (6, 7, 8, 15, 16, 17)[k], :]
            items = [("a", h, qt) for h in range(6) for qt in range(4)] + [("m", h, b) for h in range(4) for b in range(2)]
            NI = len(items)
            with ExitStack() as scope:
                VA = sb(f"t{l}_va", [P, 4, 384], F32, scope)
                VB = sb(f"t{l}_vb", [P, 3, 4, P], F32, scope)
                SC = sb(f"t{l}_sc", [P, 6, S], F32, scope)
                PT = sb(f"t{l}_pt", [P, 2, S], F32, scope)
                bias = sb(f"t{l}_bias", [P, RING, S], F32, scope)
                alibi = sb(f"t{l}_alibi", [P, 4, P], F32, scope)
                small = sb(f"t{l}_small", [P, 64], F32, scope)

                def rows(h):
                    return slice(64 * (h % 2), 64 * (h % 2) + 64)

                with nc.Block() as block:
                    @block.sync
                    def _(sp):
                        for x, (kind, h, qt) in enumerate(items[:24]):
                            if x >= RING:
                                sp.wait_ge(score_ready.sem, score_ready.at(x - RING + 1))
                            for i2 in range(2):
                                i = 2 * qt + i2
                                sp.dma_start(bias[64 * i2:64 * i2 + 64, x % RING, :],
                                             t["rpb"][l, h, :, (7 - i) * 64:(15 - i) * 64])\
                                    .then_inc(bias_loaded[x % RING].sem, 16)

                    @block.tensor
                    def _(pe):
                        for n in range(6):
                            for j in range(4):
                                if n < 3:
                                    src = Q[:, VA_ + n, j * P:(j + 1) * P]
                                elif n == 3:
                                    src = Q[:, VB_, j * P:(j + 1) * P]
                                else:
                                    src = Q[:, VB_ + n - 3, j::4]
                                mm = pe.transpose(bank[n][:, j * P:(j + 1) * P], src, ident)
                            mm.then_inc(vt_psum.sem, 1)

                        def scores(x):
                            kind, h, n = items[x]
                            b, f = bank[x % 2], rows(h)
                            pe.wait_ge(vt_ready.sem, vt_ready.at(6))
                            pe.wait_ge(score_ready.sem, score_ready.at(x - 1))
                            if kind == "a":
                                mm = pe.matmul(b[:, :], Q[f, QA + h // 2, n * P:(n + 1) * P], Q[f, KA + h // 2, :],
                                               start=True, stop=True)
                            else:
                                for v in range(2):
                                    q = (2 * n + v) * P
                                    mm = pe.matmul(b[:, 256 * v:256 * v + 256], Q[f, QM + h // 2, q:q + P],
                                                   KM[f, h // 2, :], start=True, stop=True)
                            mm.then_inc(psum_ready.sem, 1)

                        def turn(x):
                            pe.wait_ge(scaled.sem, scaled.at(x + 1))
                            pe.wait_ge(u_ready.sem, u_ready.at(x - 1))
                            for j in range(4):
                                mm = pe.transpose(bank[2 + x % 2][:, j * P:(j + 1) * P], SC[:, x % RING, j * P:(j + 1) * P], ident)
                            mm.then_inc(masked.sem, 1)

                        def values(x):
                            kind, h, n = items[x]
                            f = rows(h)
                            pe.wait_ge(u_ready.sem, u_ready.at(x + 1))
                            k = h // 2 if kind == "a" else 3 + h // 2
                            pe.wait_ge(y_ready.sem, y_ready.at(k - 1))
                            o = bank[4 + k % 2]
                            if kind == "a":
                                for j in range(4):
                                    mm = pe.matmul(o[f, n * P:(n + 1) * P], VA[:, j, h * 64:h * 64 + 64],
                                                   PT[:, x % 2, j * P:(j + 1) * P], start=j == 0, stop=j == 3)
                            else:
                                for v in range(2):
                                    q = (2 * n + v) * P
                                    for j in range(2):
                                        mm = pe.matmul(o[f, q:q + P], VM[:, j, h * 64:h * 64 + 64],
                                                       PT[:, x % 2, (2 * v + j) * P:(2 * v + j + 1) * P],
                                                       start=j == 0, stop=j == 1)
                            mm.then_inc(attended.sem, 1)

                        for x in range(NI + 2):
                            if x < NI:
                                scores(x)
                            if 0 <= x - 1 < NI:
                                turn(x - 1)
                            if x >= 2:
                                values(x - 2)

                    @block.scalar
                    def _(act):
                        for n in range(6):
                            act.wait_ge(vt_psum.sem, vt_psum.at(n + 1))
                            src = bank[n][:, :].rearrange("p (j f) -> p j f", j=4)
                            act.activation(VA[:, :, n * P:(n + 1) * P] if n < 3 else VB[:, n - 3, :, :], src, ACT.Copy)\
                                .then_inc(vt_ready.sem, 1)

                        def exps(x):
                            G = 1 if items[x][0] == "a" else 2
                            w = S // G
                            act.wait_ge(frame_ready.sem, frame_ready.at(x + 1))
                            for g in range(G):
                                at = 16 * (x % RING) + g
                                ins = act.activation(SC[:, x % RING, g * w:(g + 1) * w], SC[:, x % RING, g * w:(g + 1) * w],
                                                     ACT.Exp, bias=small[:, at:at + 1], accum_out=small[:, at + 2:at + 3])
                            ins.then_inc(weight_ready.sem, 1)

                        def copy(x):
                            act.wait_ge(masked.sem, masked.at(x + 1))
                            act.wait_ge(attended.sem, attended.at(x - 1))
                            act.activation(PT[:, x % 2, :], bank[2 + x % 2][:, :], ACT.Copy).then_inc(u_ready.sem, 1)

                        def tile_out(n):
                            k = n if n < 3 else n + 1
                            act.wait_ge(attended.sem, attended.at((8, 16, 24, 28, 32)[n]))
                            act.activation(OT(k), bank[4 + n % 2][:, :], ACT.Copy).then_inc(y_ready.sem, 1)
                            act.wait_ge(y_ready.sem, y_ready.at(n + 1))
                            act.activation(o_hi[:, k, :], OT(k), ACT.Copy).then_inc(rounded.sem, 1)

                        done = {8: 0, 16: 1, 24: 2, 28: 3, 32: 4}
                        for x in range(NI + 1):
                            if x < NI:
                                exps(x)
                            if x >= 1:
                                copy(x - 1)
                            if x - 2 in done:
                                tile_out(done[x - 2])
                        tile_out(4)

                    @block.vector
                    def _(dve):
                        ch = Chain(dve, dve_chain)

                        def top(x):
                            G = 1 if items[x][0] == "a" else 2
                            sc = SC[:, x % RING, :]
                            dve.wait_ge(psum_ready.sem, psum_ready.at(x + 1))
                            dve.wait_ge(masked.sem, masked.at(x - RING + 1))
                            if x < 24:
                                bs = bias_loaded[x % RING]
                                dve.wait_ge(bs.sem, bs.at(32 * (x // RING + 1)))
                                ins = dve.scalar_tensor_tensor(out=sc, in0=bank[x % 2][:, :], scalar=scale,
                                                               in1=bias[:, x % RING, :], op0=ALU.mult, op1=ALU.add)
                            else:
                                ins = dve.tensor_scalar(sc, bank[x % 2][:, :], scale, None, ALU.mult)
                            ins.then_inc(score_ready.sem, 1)
                            dve.wait_ge(score_ready.sem, score_ready.at(x + 1))
                            at = 16 * (x % RING)
                            dve.tensor_reduce(small[:, at:at + G], sc.rearrange("p (g s) -> p g s", g=G), AX_X, ALU.max,
                                              negate=True).then_inc(frame_ready.sem, 1)

                        def norm(x):
                            G = 1 if items[x][0] == "a" else 2
                            w, at = S // G, 16 * (x % RING)
                            dve.wait_ge(weight_ready.sem, weight_ready.at(x + 1))
                            ch.add(dve.reciprocal(small[:, at + 4:at + 4 + G], small[:, at + 2:at + 2 + G]))
                            ch.wait()
                            for g in range(G):
                                sc = SC[:, x % RING, g * w:(g + 1) * w]
                                ins = dve.tensor_scalar(sc, sc, small[:, at + 4 + g:at + 5 + g], None, ALU.mult)
                            ins.then_inc(scaled.sem, 1)

                        for x in range(NI + 1):
                            if x < NI:
                                top(x)
                            if x:
                                norm(x - 1)

                    @block.gpsimd
                    def _(pool):
                        for n in range(5):
                            k = n if n < 3 else n + 1
                            pool.wait_ge(rounded.sem, rounded.at(n + 1))
                            pool.tensor_tensor(o_lo[:, k, :], OT(k), o_hi[:, k, :].bitcast(F32), ALU.subtract)
                for bs in bias_loaded:
                    bs.advance(32 * 24 // RING)
                end_stage(vt_psum=6, vt_ready=6, score_ready=NI, psum_ready=NI, scaled=NI, u_ready=NI, masked=NI,
                          attended=NI, frame_ready=NI, weight_ready=NI, y_ready=5, rounded=5, dve_chain=NI)

                with nc.Block() as block:
                    @block.sync
                    def _(sp):
                        sp.dma_start(alibi[:, :, :], t["alibi"]).then_inc(loads_done, 16)
                        for x in range(8):
                            if x >= RING:
                                sp.wait_ge(score_ready.sem, score_ready.at(x - RING + 1 + 2 * (x - RING > 3)))
                            sp.dma_start(bias[:, x % RING, :], t["near"][x]).then_inc(bias_loaded[x % RING].sem, 16)

                    @block.tensor
                    def _(pe):
                        def scores(hh, y):
                            x = 6 * hh + y
                            f = rows(hh)
                            b = bank[x % 2]
                            pe.wait_ge(score_ready.sem, score_ready.at(x - 1))
                            if y < 4:
                                mm = pe.matmul(b[:, :], Q[f, QB, y::4], Q[f, KB, :], start=True, stop=True)
                            else:
                                g = y - 3
                                for r in range(4):
                                    mm = pe.matmul(b[:, r * P:(r + 1) * P], Q[f, QB + g, r::4], Q[f, KB + g, r::4],
                                                   start=True, stop=True)
                            mm.then_inc(psum_ready.sem, 1)

                        def turn(hh, y):
                            x = 6 * hh + y
                            pe.wait_ge(scaled.sem, scaled.at(x + 1))
                            pe.wait_ge(u_ready.sem, u_ready.at(x - 1))
                            for j in range(4):
                                mm = pe.transpose(bank[2 + x % 2][:, j * P:(j + 1) * P], SC[:, y, j * P:(j + 1) * P], ident)
                            mm.then_inc(masked.sem, 1)

                        def values(hh, y):
                            x = 6 * hh + y
                            f = rows(hh)
                            pe.wait_ge(u_ready.sem, u_ready.at(x + 1))
                            o = bank[4]
                            for j in range(4):
                                r, g = (y, 0) if y < 4 else (j, y - 3)
                                mm = pe.matmul(o[f, r * P:(r + 1) * P], VB[:, g, j, 64 * hh:64 * hh + 64],
                                               PT[:, x % 2, j * P:(j + 1) * P], start=y == 0 and j == 0,
                                               stop=y == 5 and j == 3, skip_group_check=True)
                            mm.then_inc(attended.sem, 1)

                        for hh in range(2):
                            for y in range(6):
                                scores(hh, y)
                            for y in range(7):
                                if y < 6:
                                    turn(hh, y)
                                if y:
                                    values(hh, y - 1)

                    @block.scalar
                    def _(act):
                        for hh in range(2):
                            for y in range(6):
                                x = 6 * hh + y
                                act.wait_ge(frame_ready.sem, frame_ready.at(x + 1))
                                for r in range(1 if y < 4 else 4):
                                    at = y if y < 4 else 4 * (y - 3) + r
                                    sc = SC[:, y, :] if y < 4 else SC[:, y, r * P:(r + 1) * P]
                                    ins = act.activation(sc, sc, ACT.Exp, bias=small[:, at:at + 1],
                                                         accum_out=small[:, 12 + at:13 + at])
                            ins.then_inc(weight_ready.sem, 1)
                            act.wait_ge(weight_arg.sem, weight_arg.at(hh + 1))
                            act.activation(small[:, 24:36], small[:, 24:36], ACT.Exp).then_inc(decay_ready.sem, 1)
                            for y in range(6):
                                x = 6 * hh + y
                                act.wait_ge(masked.sem, masked.at(x + 1))
                                act.wait_ge(attended.sem, attended.at(x - 1))
                                act.activation(PT[:, x % 2, :], bank[2 + x % 2][:, :], ACT.Copy).then_inc(u_ready.sem, 1)
                        act.wait_ge(attended.sem, attended.at(12))
                        act.activation(OT(3).rearrange("p (n r) -> p r n", r=4),
                                       bank[4][:, :].rearrange("p (r n) -> p r n", r=4), ACT.Copy).then_inc(y_ready.sem, 1)
                        act.wait_ge(y_ready.sem, y_ready.at(1))
                        act.activation(o_hi[:, 3, :], OT(3), ACT.Copy).then_inc(rounded.sem, 1)

                    @block.vector
                    def _(dve):
                        ch = Chain(dve, dve_chain)
                        dve.wait_ge(loads_done, loads.at(16))
                        for hh in range(2):
                            for y in range(6):
                                x = 6 * hh + y
                                sc = SC[:, y, :]
                                dve.wait_ge(psum_ready.sem, psum_ready.at(x + 1))
                                if hh:
                                    dve.wait_ge(masked.sem, masked.at(y + 1))
                                if y < 4:
                                    n = 4 * hh + y
                                    bs = bias_loaded[n % RING]
                                    dve.wait_ge(bs.sem, bs.at(16 * (n // RING + 1)))
                                    dve.scalar_tensor_tensor(out=sc, in0=bank[x % 2][:, :], scalar=scale,
                                                             in1=bias[:, n % RING, :], op0=ALU.mult, op1=ALU.add)\
                                        .then_inc(score_ready.sem, 1)
                                    out = small[:, y:y + 1]
                                else:
                                    a = alibi[:, 2 * (y - 4) + hh, :].unsqueeze(1).broadcast_to([P, 4, P])
                                    dve.scalar_tensor_tensor(out=sc.rearrange("p (r s) -> p r s", r=4),
                                                             in0=bank[x % 2][:, :].rearrange("p (r s) -> p r s", r=4),
                                                             scalar=scale, in1=a, op0=ALU.mult, op1=ALU.add)\
                                        .then_inc(score_ready.sem, 1)
                                    out = small[:, 4 * (y - 3):4 * (y - 3) + 4]
                                dve.wait_ge(score_ready.sem, score_ready.at(x + 1))
                                src = sc if y < 4 else sc.rearrange("p (r s) -> p r s", r=4)
                                dve.tensor_reduce(out, src, AX_X, ALU.max, negate=True).then_inc(frame_ready.sem, 1)
                            neg, arg, den = small[:, 0:12], small[:, 24:36], small[:, 12:24]
                            low, z = small[:, 36:40], small[:, 40:44]
                            by = lambda ap: ap.rearrange("p (g r) -> p g r", g=3)
                            dve.wait_ge(frame_ready.sem, frame_ready.at(6 * hh + 6))
                            ch.add(dve.tensor_tensor(low, neg[:, 0:4], neg[:, 4:8], ALU.min))
                            ch.wait()
                            ch.add(dve.tensor_tensor(low, low, neg[:, 8:12], ALU.min))
                            ch.wait()
                            dve.tensor_tensor(by(arg), low.unsqueeze(1).broadcast_to([P, 3, 4]), by(neg),
                                              ALU.subtract).then_inc(weight_arg.sem, 1)
                            dve.wait_ge(decay_ready.sem, decay_ready.at(hh + 1))
                            dve.wait_ge(weight_ready.sem, weight_ready.at(hh + 1))
                            ch.add(dve.tensor_tensor(den, den, arg, ALU.mult))
                            ch.wait()
                            ch.add(dve.tensor_reduce(z, den.rearrange("p (g r) -> p r g", g=3), AX_X, ALU.add))
                            ch.wait()
                            ch.add(dve.reciprocal(z, z))
                            ch.wait()
                            ch.add(dve.tensor_tensor(by(arg), by(arg), z.unsqueeze(1).broadcast_to([P, 3, 4]), ALU.mult))
                            ch.wait()
                            for y in range(6):
                                sc = SC[:, y, :]
                                if y < 4:
                                    ins = dve.tensor_scalar(sc, sc, arg[:, y:y + 1], None, ALU.mult)
                                else:
                                    w = arg[:, 4 * (y - 3):4 * (y - 3) + 4].unsqueeze(2).broadcast_to([P, 4, P])
                                    v = sc.rearrange("p (r s) -> p r s", r=4)
                                    ins = dve.tensor_tensor(v, v, w, ALU.mult)
                                ins.then_inc(scaled.sem, 1)

                    @block.gpsimd
                    def _(pool):
                        pool.wait_ge(rounded.sem, rounded.at(1))
                        pool.tensor_tensor(o_lo[:, 3, :], OT(3), o_hi[:, 3, :].bitcast(F32), ALU.subtract)
                loads.advance(16)
                for n in range(8):
                    bias_loaded[n % RING].advance(16)
                end_stage(score_ready=12, psum_ready=12, scaled=12, u_ready=12, masked=12, attended=12, frame_ready=12,
                          weight_ready=2, weight_arg=2, decay_ready=2, y_ready=1, rounded=1, dve_chain=12)

        def gated_merge(l, n0, NG, NBR, o_hi, o_lo):
            n1, n2 = n0 + NG, n0 + NG + NBR
            NO = KT // 2
            with ExitStack() as scope:
                G = sb(f"g{l}_gates", [P, 3 * KT, S], F32, scope)
                mg = sb(f"g{l}_merged", [P, 2, S], F32, scope)
                part = sb(f"g{l}_part", [P, 2, S], F32, scope)
                hi, lo = x_parts()
                with nc.Block() as block:
                    @block.sync
                    def _(sp):
                        for_chunks(sp, NG, ahead(fetch, sp, n0, NG, 2))
                        for_chunks(sp, NBR, ahead(fetch, sp, n1, NBR, 2), peel=NBR)

                    @block.tensor
                    def _(pe):
                        project(pe, n0, NG, hi, lo)
                        for j in range(NBR):
                            s = (n1 + j) % 2
                            pe.wait_ge(lo_ready.sem, PRIME + n1 + j + 1)
                            if j == 0:
                                pe.wait_ge(bank_free[0].sem, bank_free[0].at(NG // 2))
                                pe.wait_ge(bank_free[1].sem, bank_free[1].at(NG // 2))
                            for v in range(2):
                                n = 2 * j + v
                                pe.wait_ge(z_ready.sem, z_ready.at(n - 1))
                                for x, ks in enumerate((range(0, 3), range(3, 4), range(4, 6))):
                                    mm = linear(pe, bank[4 * v + x][:, :], s, (6 * v + ks[0]) * P, ks,
                                                lambda k: o_hi[:, k, :], lambda k: o_lo[:, k, :])
                                mm.then_inc((psum_ready if v == 0 else chunk_used).sem, 1)

                    @block.scalar
                    def _(act):
                        split = ahead(split_hi, act, n0, NG, 1)
                        for j in range(NG):
                            split(j // 2, j % 2)
                            act.wait_ge(chunk_used.sem, PRIME + n0 + j + 1)
                            for v in range(2):
                                k = 2 * j + v
                                ins = act.activation(G[:, k, :], bank[2 * (j % 2) + v][:, :], ACT.Sigmoid,
                                                     bias=col("b_gate_2", (l * 3 + k % 3) * KT + k // 3))
                            ins.then_inc(bank_free[j % 2].sem, 1)
                        split = ahead(split_hi, act, n1, NBR, 1)
                        for j in range(NBR):
                            split(j // 2, j % 2)
                            for v in range(2):
                                n = 2 * j + v
                                act.wait_ge(z_ready.sem, z_ready.at(n + 1))
                                act.activation(x_hi[:, n, :], mg[:, v, :], ACT.Copy).then_inc(rounded.sem, 1)

                    @block.vector
                    def _(dve):
                        ch = Chain(dve, dve_chain)
                        for_chunks(dve, NG, ahead(split_lo, dve, n0, NG, 1))
                        split = ahead(split_lo, dve, n1, NBR, 1)
                        dve.wait_ge(bank_free[0].sem, bank_free[0].at(NG // 2))
                        dve.wait_ge(bank_free[1].sem, bank_free[1].at(NG // 2))
                        for j in range(NBR):
                            split(j // 2, j % 2)
                            for v in range(2):
                                n = 2 * j + v
                                if v == 0:
                                    dve.wait_ge(psum_ready.sem, psum_ready.at(j + 1))
                                else:
                                    dve.wait_ge(chunk_used.sem, PRIME + n1 + j + 1)
                                dve.wait_ge(split_ready.sem, split_ready.at(n - 1))
                                m, q = mg[:, v, :], part[:, v, :]
                                ch.add(dve.tensor_tensor(m, bank[4 * v][:, :], G[:, 3 * n, :], ALU.mult))
                                ch.add(dve.tensor_tensor(q, bank[4 * v + 1][:, :], G[:, 3 * n + 1, :], ALU.mult))
                                ch.wait()
                                ch.add(dve.tensor_tensor(m, m, q, ALU.add))
                                ch.wait()
                                ch.add(dve.tensor_tensor(q, bank[4 * v + 2][:, :], G[:, 3 * n + 2, :], ALU.mult))
                                ch.wait()
                                dve.tensor_tensor(m, m, q, ALU.add).then_inc(z_ready.sem, 1)

                    @block.gpsimd
                    def _(pool):
                        for n in range(KT):
                            pool.wait_ge(rounded.sem, rounded.at(n + 1))
                            pool.tensor_tensor(x_lo[:, n, :], mg[:, n % 2, :], x_hi[:, n, :].bitcast(F32),
                                               ALU.subtract).then_inc(split_ready.sem, 1)
                end_stage(bank_free0=NG // 2, bank_free1=NG // 2, psum_ready=NBR, z_ready=KT, rounded=KT, split_ready=KT,
                          dve_chain=4 * KT)
            with ExitStack() as scope:
                Y = sb(f"g{l}_y", [P, KT, S], F32, scope)
                sq = sb(f"g{l}_sq", [P, 2, S], F32, scope)
                rs = sb(f"g{l}_rs", [P, S], F32, scope)
                hi, lo = x_parts()
                with nc.Block() as block:
                    @block.sync
                    def _(sp):
                        for_chunks(sp, NO, ahead(fetch, sp, n2, NO, 2), peel=NO)

                    @block.tensor
                    def _(pe):
                        project(pe, n2, NO, hi, lo)
                        mean_square_tensor(pe, sq)

                    @block.scalar
                    def _(act):
                        split = ahead(split_hi, act, n2, NO, 1)
                        for j in range(NO):
                            split(j // 2, j % 2)
                            act.wait_ge(chunk_used.sem, PRIME + n2 + j + 1)
                            for v in range(2):
                                ins = act.activation(Y[:, 2 * j + v, :], bank[2 * (j % 2) + v][:, :], ACT.Copy)
                            ins.then_inc(bank_free[j % 2].sem, 1)
                        act.wait_ge(bank_free[0].sem, bank_free[0].at(NO // 2))
                        act.wait_ge(bank_free[1].sem, bank_free[1].at(NO // 2))
                        for k in range(KT):
                            squares_scalar(act, Y[:, k, :], sq, k)
                        scale_scalar(act, rs[:, :])

                    @block.vector
                    def _(dve):
                        for_chunks(dve, NO, ahead(split_lo, dve, n2, NO, 1), peel=NO)
                        post_norm_vector(dve, lambda k: Y[:, k, :], rs[:, :], sq, "g_post_mix_2", l)
                end_stage(bank_free0=NO // 2, bank_free1=NO // 2, dve_chain=2 * KT, **RMS)


        def conv_ffn(l):
            rms_split(X, "g_pre_ffn_2", l, x_hi, x_lo)
            n0 = c_next[0]
            n1 = n0 + FT
            c_next[0] = n1 + 2 * KT
            with ExitStack() as scope:
                g_hi = sb(f"c{l}_g_hi", [P, FT, S], F32R, scope)
                g_lo = sb(f"c{l}_g_lo", [P, FT, S], F32R, scope)
                W8 = sb(f"c{l}_work", [P, KT, S], F32, scope)
                ca, cb, prod = (W8[:, 2 * n:2 * n + 2, :] for n in range(3))
                Y, sq, rs = W8[:, 0:4, :], W8[:, 4:6, :], W8[:, 6, :]
                hi, lo = x_parts()

                def ccol(name, n):
                    at = col_at[name] + n
                    return cols[:, bass.ds(at, 1)]

                with nc.Block() as block:
                    @block.sync
                    def _(sp):
                        for_chunks(sp, FT, ahead(fetch, sp, n0, FT, 2))
                        for_chunks(sp, 2 * KT, ahead(fetch, sp, n1, 2 * KT, 2))

                    def tail_square(pe, k):
                        pe.wait_ge(square_ready.sem, square_ready.at(k + 1))
                        pe.matmul(bank[7][:, :], const["mean_d"], sq[:, k % 2, :], start=k == 0,
                                  stop=k == KT - 1).then_inc(square_used.sem, 1)

                    @block.tensor
                    def _(pe):
                        def up(i, u):
                            s, j = (n0 + u) % 2, i * 2 + u
                            pe.wait_ge(lo_ready.sem, j + (PRIME + n0 + 1))
                            pe.wait_ge(frame_ready.sem, frame_ready.at(-1) + j)
                            linear(pe, bank[2 * u][:, :], s, 0, range(KT), hi, lo)
                            linear(pe, bank[2 * u + 1][:, :], s, KT * P, range(KT), hi, lo)\
                                .then_inc(chunk_used.sem, 1)

                        for_chunks(pe, FT, up)
                        pe.wait_ge(rest_ready.sem, rest_ready.at(FT))
                        for n in range(KT):
                            for u in range(2):
                                c = n1 + 2 * n + u
                                pe.wait_ge(lo_ready.sem, PRIME + c + 1)
                                if n >= 6 and u == 0:
                                    pe.wait_ge(z_ready.sem, z_ready.at(n - 5))
                                mm = linear(pe, bank[n if n < 4 else 4 + n % 2][:, :], c % 2, 0, range(FH * u, FH * u + FH),
                                            lambda k: g_hi[:, k, :], lambda k: g_lo[:, k, :], first=u == 0, last=u == 1)
                                mm.then_inc(chunk_used.sem, 1)
                            if n:
                                tail_square(pe, n - 1)
                        tail_square(pe, KT - 1)

                    @block.scalar
                    def _(act):
                        split = ahead(split_hi, act, n0, FT, 1)

                        def body(i, u):
                            split(i, u)
                            j = i * 2 + u
                            act.wait_ge(frame_ready.sem, frame_ready.at(1) + j)
                            act.activation(ca[:, u, :], ca[:, u, :], ACT.Gelu_apprx_tanh).then_inc(act_ready.sem, 1)
                            act.wait_ge(product_ready.sem, product_ready.at(1) + j)
                            act.activation(g_hi[:, j, :], prod[:, u, :], ACT.Copy).then_inc(rounded.sem, 1)

                        for_chunks(act, FT, body)
                        for n in range(KT):
                            for u in range(2):
                                ahead(split_hi, act, n1, 2 * KT, 1)(n, u)
                            act.wait_ge(chunk_used.sem, PRIME + n1 + 2 * n + 2)
                            b = bank[n if n < 4 else 4 + n % 2]
                            if n >= 4:
                                act.activation(Y[:, n - 4, :], b[:, :], ACT.Copy).then_inc(z_ready.sem, 1)
                                act.wait_ge(z_ready.sem, z_ready.at(n - 3))
                                squares_scalar(act, Y[:, n - 4, :], sq, n)
                            else:
                                squares_scalar(act, b[:, :], sq, n)
                        scale_scalar(act, rs)

                    @block.vector
                    def _(dve):
                        ch = Chain(dve, dve_chain)
                        split = ahead(split_lo, dve, n0, FT, 1)

                        def body(i, u):
                            split(i, u)
                            j = i * 2 + u
                            dve.wait_ge(chunk_used.sem, j + (PRIME + n0 + 1))
                            dve.wait_ge(product_ready.sem, product_ready.at(-1) + j)
                            for out, b, off, signal_ in ((ca, 2 * u, 0, conv_a), (cb, 2 * u + 1, FT, conv_b)):
                                o, p = out[:, u, :], bank[b]
                                w = [ccol("conv_w_2", (l * 3 + tap) * 2 * FT + off + j) for tap in range(3)]
                                dve.tensor_scalar(o, p[:, :], w[1], ccol("conv_b_2", l * 2 * FT + off + j),
                                                  ALU.mult, ALU.add).then_inc(signal_.sem, 1)
                            for out, b, off, signal_ in ((ca, 2 * u, 0, conv_a), (cb, 2 * u + 1, FT, conv_b)):
                                o, p = out[:, u, :], bank[b]
                                w = ccol("conv_w_2", (l * 3) * 2 * FT + off + j)
                                dve.wait_ge(signal_.sem, signal_.at(1) + j * 2)
                                dve.scalar_tensor_tensor(out=o[:, 1:S], in0=p[:, 0:S - 1], scalar=w, in1=o[:, 1:S],
                                                         op0=ALU.mult, op1=ALU.add).then_inc(signal_.sem, 1)
                            for out, b, off, signal_ in ((ca, 2 * u, 0, conv_a), (cb, 2 * u + 1, FT, conv_b)):
                                o, p = out[:, u, :], bank[b]
                                w = ccol("conv_w_2", (l * 3 + 2) * 2 * FT + off + j)
                                dve.wait_ge(signal_.sem, signal_.at(2) + j * 2)
                                ins = dve.scalar_tensor_tensor(out=o[:, 0:S - 1], in0=p[:, 1:S], scalar=w,
                                                               in1=o[:, 0:S - 1], op0=ALU.mult, op1=ALU.add)
                            ins.then_inc(frame_ready.sem, 1)
                            dve.wait_ge(act_ready.sem, act_ready.at(1) + j)
                            dve.wait_ge(rest_ready.sem, rest_ready.at(-1) + j)
                            dve.tensor_tensor(prod[:, u, :], ca[:, u, :], cb[:, u, :], ALU.mult)\
                                .then_inc(product_ready.sem, 1)

                        for_chunks(dve, FT, body)
                        for_chunks(dve, 2 * KT, ahead(split_lo, dve, n1, 2 * KT, 1))
                        post_norm_vector(dve, lambda k: bank[k][:, :] if k < 4 else Y[:, k - 4, :], rs, sq, "g_post_ffn_2", l)

                    @block.gpsimd
                    def _(pool):
                        def body(i, u):
                            j = i * 2 + u
                            pool.wait_ge(rounded.sem, rounded.at(1) + j)
                            pool.tensor_tensor(g_lo[:, j, :], prod[:, u, :], g_hi[:, j, :].bitcast(F32),
                                               ALU.subtract).then_inc(rest_ready.sem, 1)

                        for_chunks(pool, FT, body)
            end_stage(frame_ready=FT, act_ready=FT, product_ready=FT, rounded=FT, rest_ready=FT, z_ready=4,
                      conv_a=2 * FT, conv_b=2 * FT, dve_chain=2 * KT, **RMS)


        stages = []
        for l in range(DEPTH):
            stages.append(lambda l=l: swiglu(l, 0))
            stages.append(lambda l=l: even_mixer(l) if l % 2 == 0 else odd_mixer(l))
            stages.append(lambda l=l: swiglu(l, 2))
        for l in range(DEPTH):
            stages.append(lambda l=l: attention(l))
            stages.append(lambda l=l: conv_ffn(l))
        for n, st in enumerate(stages):
            if n == 3 * DEPTH:
                first_block.close()
            st()

        with nc.Block() as block:
            @block.sync
            def _(sp):
                sp.dma_start(t["out"], X[:, :, :]).then_inc(stores_done, 16)
                sp.wait_ge(stores_done, 16)


def block_diagonal(w):
    out = np.zeros((P, 4, P), np.float32)
    for b in range(8):
        at = 64 * (b % 2)
        out[at:at + 64, b // 2, at:at + 64] = w[b]
    return out


MASKED = -1e30


def lay_out_rpb(rpb):
    c, k = np.arange(64)[:, None], np.arange(64)[None, :]
    start = np.clip(c - 8, 0, 48)
    seen = (k >= start) & (k < start + 16)
    out = rpb[:, :, :, np.where(seen, k - c + 15, 0)]
    out = np.where(seen, out, np.float32(MASKED)).astype(rpb.dtype)
    return np.ascontiguousarray(out.transpose(0, 1, 3, 2, 4)).reshape(DEPTH, 6, 64, 15 * 64)


def slopes():
    return (2.0 ** (-8.0 * np.arange(1, 7, dtype=np.float32) / 6)).astype(np.float32)


def near_bias():
    q = 4 * np.arange(P)[None, :, None] + np.arange(4)[:, None, None]
    far = np.abs(np.arange(S)[None, None, :] - q)
    return np.concatenate([np.where(far <= 64, -s * far, MASKED) for s in slopes()[:2]], 0).astype(np.float32)


def dilated_bias():
    n = np.abs(np.arange(P)[:, None] - np.arange(P)[None, :])
    s = slopes()
    parts = [np.where(n <= 64, -s[2 + h] * 4 * n, MASKED) for h in range(2)]
    parts += [np.where(n % 4 == 0, -s[4 + h] * 4 * n, MASKED) for h in range(2)]
    return np.ascontiguousarray(np.stack(parts, 1).astype(np.float32))


def lay_out(i):
    return {"weights": lay_out_weights(i), "cols": lay_out_columns(i),
            "consts": np.ascontiguousarray(np.stack(list(constants().values()), 1)),
            "x": np.ascontiguousarray(np.asarray(i["x"])[0].T.reshape(KT, P, S).transpose(1, 0, 2)),
            "rg_w": np.concatenate([block_diagonal(i["rg_wa"][0]), block_diagonal(i["rg_wx"][0])], 1),
            "masks": odd_masks(), "gla_gB": i["gla_gB"][0],
            "mem": np.ascontiguousarray(np.asarray(i["mem_2"])[0].T.reshape(KT, P, 256).transpose(1, 0, 2)),
            "rpb": lay_out_rpb(np.asarray(i["rpb_na_2"])), "near": near_bias(), "alibi": dilated_bias(),
            "rk_lora": np.concatenate([i["rk_wB"][0], i["rk_aB"][0], i["rk_gB"][0]], 0)}


def kernel(**inputs):
    from concourse import bacc
    from concourse.bass_utils import run_bass_kernel_spmd

    arrays = lay_out({name: np.asarray(a) for name, a in inputs.items()})
    nc = bacc.Bacc("TRN2", target_bir_lowering=False, num_devices=1)
    t = {}
    for name, a in arrays.items():
        t[name] = nc.dram_tensor(f"in_{name}", a.shape, mybir.dt.from_np(a.dtype), kind="ExternalInput").ap()
    t["out"] = nc.dram_tensor("out_x", (P, KT, S), F32, kind="ExternalOutput").ap()
    program(nc, t)
    got = run_bass_kernel_spmd(nc, [{f"in_{name}": a for name, a in arrays.items()}], core_ids=[0])
    x = np.asarray(got.results[0]["out_x"])
    return np.ascontiguousarray(x.transpose(1, 0, 2).reshape(D, S).T[None])
```

```python
from contextlib import ExitStack

import numpy as np
import concourse.bass as bass
from concourse import mybir

F32 = mybir.dt.float32
F32R = mybir.dt.float32r
ALU = mybir.AluOpType
ACT = mybir.ActivationFunctionType
AX_X = mybir.AxisListType.X

P = 128
S = 512
D = 1024
KT = D // P
DEPTH = 2
DFF = 2816
FT = DFF // P
FH = FT // 2
CHUNK = 2 * KT * P
LOG_EXP = "natural_log_exp_and_others"
ALPHA = (2.0 * DEPTH) ** 0.25
LN_EPS = 1e-5
PRIME = 4



def stream_plan():
    plan = []
    for l in range(DEPTH):
        plan += [(f"ffn1_{l}", CHUNK)] * FT + [(f"ffn1_{l}", FH * P)] * (2 * KT)
        plan += [(f"mix_{l}", CHUNK)] * (13 + KT // 2)
        plan += [(f"ffn2_{l}", CHUNK)] * FT + [(f"ffn2_{l}", FH * P)] * (2 * KT)
    for l in range(DEPTH):
        plan += [(f"att_{l}", CHUNK)] * (10 + 2)
        plan += ([(f"att_{l}", CHUNK)] * 3 + [(f"att_{l}", 2 * 6 * P)]) * (KT // 2) + [(f"att_{l}", CHUNK)] * (KT // 2)
        plan += [(f"cffn_{l}", CHUNK)] * FT + [(f"cffn_{l}", FH * P)] * (2 * KT)
    return plan


class Signal:

    def __init__(self, sem, base=PRIME):
        self.sem, self.base = sem, base

    def at(self, n):
        return self.base + n

    def advance(self, n):
        self.base += n



def tiles_in(w):
    n = w.shape[1] // P
    return w.reshape(KT, P, n, P).transpose(2, 1, 0, 3)


def tiles_out(w):
    return w.reshape(2, FH, P, KT, P).transpose(3, 0, 2, 1, 4).reshape(2 * KT, P, FH * P)


def pad_cols(w, n):
    return np.pad(w, ((0, 0), (0, n - w.shape[1])))


def pairs(tiles):
    n = tiles.shape[0] // 2
    return tiles.reshape(n, 2, P, KT, P).transpose(0, 2, 1, 3, 4).reshape(n, P, CHUNK)


def gated(w):
    a, b = tiles_in(w[:, :DFF]), tiles_in(w[:, DFF:])
    return pairs(np.stack([a, b], 1).reshape(2 * FT, P, KT, P))


EVEN_TILES = 26
ODD_TILES = 26


def lay_out_weights(i):
    plan = stream_plan()
    out = np.zeros((len(plan), P, CHUNK), np.float32)
    at = 0

    def put(chunks):
        nonlocal at
        for c in chunks:
            out[at, :, : c.shape[-1]] = c
            at += 1

    for l in range(DEPTH):
        put(gated(i["ffn1_wi"][l]))
        put(tiles_out(i["ffn1_wo"][l]))
        if l % 2 == 0:
            w = i["ev_w_in"][l // 2]
            n = w.shape[1] - 8
            tiles = tiles_in(np.concatenate([w[:, :n], pad_cols(w[:, n:n + 4], P), pad_cols(w[:, n + 4:], P)], 1))
            put(pairs(np.concatenate([tiles[0:4], tiles[24:26], tiles[4:8], tiles[16:20], tiles[8:16], tiles[20:24]], 0)))
            put(pairs(tiles_in(i["ev_w_out"][l // 2])))
        else:
            w = i["od_w_in"][l // 2]
            g = 1664 + 1024
            tiles = tiles_in(np.concatenate([w[:, :g], pad_cols(w[:, g:g + 16], P), w[:, g + 16:]], 1))
            put(pairs(np.concatenate([tiles[13:], tiles[12:13], tiles[:12]], 0)))
            put(pairs(tiles_in(i["od_w_out"][l // 2])))
        put(gated(i["ffn2_wi"][l]))
        put(tiles_out(i["ffn2_wo"][l]))
    for l in range(DEPTH):
        w = i["w_in_2"][l]
        qkv = tiles_in(w[:, :2560])
        put(pairs(qkv[[0, 1, 2, 3, 4, 5, 9, 10, 11, 12, 13, 14, 18, 19, 6, 7, 8, 15, 16, 17]]))
        put(pairs(tiles_in(i["w_mem_kv_2"][l])))
        g = tiles_in(w[:, 2560:]).reshape(3, KT, P, KT, P).transpose(1, 0, 2, 3, 4)
        g = pairs(g.reshape(3 * KT, P, KT, P))
        br = np.concatenate([i["w_br_a_2"][l], i["w_br_b_2"][l], i["w_br_m_2"][l]], 0)
        br = br.reshape(6, P, KT // 2, 2, P).transpose(2, 1, 3, 0, 4).reshape(KT // 2, P, 12 * P)
        for j in range(KT // 2):
            put(g[3 * j:3 * j + 3])
            put(br[j:j + 1])
        put(pairs(tiles_in(i["w_out_2"][l])))
        put(gated(i["w_up_2"][l]))
        put(tiles_out(i["w_down_2"][l]))
    assert at == len(plan)
    return out


def columns():
    return {
        "ln_g": 48, "ln_b": 48,
        "rg_conv_w": 16, "rg_conv_b": 4, "rg_ba": 4, "rg_bx": 4, "rg_lambda": 4,
        "ml_conv_w": 32, "ml_conv_b": 8, "ml_i_bias": 1, "ml_f_bias": 1, "ml_norm_g": 4,
        "rk_mu": 13, "rk_w0": 4, "rk_a0": 4, "rk_k_k": 4, "rk_k_a": 4, "rk_r_k": 4, "rk_ln_g": 4, "rk_ln_b": 4,
        "gla_gb": 2, "gla_norm_g": 4,
        "mem_norm_g_2": 8, "g_pre_mix_2": 16, "b_gate_2": 48, "g_post_mix_2": 16, "g_pre_ffn_2": 16,
        "conv_w_2": 6 * 44, "conv_b_2": 2 * 44, "g_post_ffn_2": 16,
        "eps_deepnorm": 1, "eps_rms": 1, "eps_ml": 1, "eps_rk": 1, "eps_gla": 1,
    }


def column_starts():
    at, out = 0, {}
    for name, n in columns().items():
        out[name] = at
        at += n
    return out, at


def lay_out_columns(i):
    start, n = column_starts()
    out = np.zeros((P, n), np.float32)
    shapes = {"eps_deepnorm": LN_EPS / ALPHA**2, "eps_rms": 1e-6, "eps_ml": 1e-6, "eps_rk": 64e-5, "eps_gla": 1e-5}
    for name, k in columns().items():
        at = start[name]
        if name in shapes:
            out[:, at] = shapes[name]
            continue
        v = np.asarray(i[name]).reshape(-1)
        if v.size < P:
            out[: v.size, at] = v
        else:
            out[:, at:at + k] = v.reshape(k, P).T
    return out


class Chain:

    def __init__(self, eng, sig):
        self.eng, self.sig, self.n = eng, sig, 0

    def add(self, ins):
        self.n += 1
        ins.then_inc(self.sig.sem, 1)
        return self.n

    def wait(self, n=None):
        self.eng.wait_ge(self.sig.sem, self.sig.at(self.n if n is None else n))



def constants():
    eye = np.eye(P, dtype=np.float32)
    half = np.kron(np.eye(2, dtype=np.float32), np.ones((64, 64), np.float32))
    return {
        "identity": eye,
        "mean_d": np.full((P, P), 1.0 / D, np.float32),
        "mean_p": np.full((P, P), 1.0 / P, np.float32),
        "centre_p": eye - np.float32(1.0 / P),
        "ones": np.ones((P, P), np.float32),
        "half_ones": half,
        "half_mean": half / 64,
        **{f"pick{h}": np.repeat((np.arange(P) == h).astype(np.float32)[:, None], P, 1) for h in range(4)},
    }


def odd_masks():
    i = np.arange(P)
    s, u = i[:, None], i[None, :]
    reset = [np.repeat((np.arange(S) % c != 0)[None], P, 0) for c in (32, 64)]
    parts = reset + [(s // 32 == u // 32) & (s < u), (s // 32 == u // 32) & (s <= u), (s // 64 == u // 64) & (s <= u),
                     (s % 32) > np.arange(32)[None, :]]
    return np.concatenate(parts, 1).astype(np.float32)


def program(nc, t):
    plan = stream_plan()
    n_chunks = len(plan)
    col_at, n_cols = column_starts()
    ctx = ExitStack()
    with ctx:
        def sb(name, shape, dt=F32, scope=ctx):
            return scope.enter_context(nc.sbuf_tensor(name, shape, dt))

        signals = {}

        def signal(name):
            if name not in signals:
                signals[name] = Signal(ctx.enter_context(nc.semaphore(name)))
            return signals[name]

        raw = sb("raw", [P, 2, CHUNK])
        w_hi = sb("w_hi", [P, 2, CHUNK], F32R)
        w_lo = sb("w_lo", [P, 2, CHUNK], F32R)
        X = sb("X", [P, KT, S])
        x_hi = sb("x_hi", [P, KT, S], F32R)
        x_lo = sb("x_lo", [P, KT, S], F32R)
        cols = sb("cols", [P, n_cols])
        stats = sb("stats", [P, 2, S])
        const_names = list(constants())
        consts = sb("consts", [P, 2, P])
        first_block = ExitStack()
        mixer_consts = sb("mixer_consts", [P, len(const_names) - 2, P], F32, first_block)
        bank = [ctx.enter_context(nc.psum_tensor(f"bank{b}", [P, S], F32)) for b in range(8)]
        const = {name: consts[:, n, :] if n < 2 else mixer_consts[:, n - 2, :] for n, name in enumerate(const_names)}

        def col(name, n=0):
            return cols[:, col_at[name] + n:col_at[name] + n + 1]

        raw_loaded = [ctx.enter_context(nc.semaphore(f"raw_loaded{s}")) for s in range(2)]
        loads_done = ctx.enter_context(nc.semaphore("loads_done"))
        stores_done = ctx.enter_context(nc.semaphore("stores_done"))
        primed = ctx.enter_context(nc.semaphore("primed"))
        x_loaded = [ctx.enter_context(nc.semaphore(f"x_loaded{k}")) for k in range(KT)]
        loads = Signal(loads_done, 48)
        hi_ready, lo_ready, chunk_used = signal("hi_ready"), signal("lo_ready"), signal("chunk_used")
        psum_ready = signal("psum_ready")
        part_ready, part_free = signal("part_ready"), signal("part_free")
        zsum_ready, mean_ready, centred = signal("zsum_ready"), signal("mean_ready"), signal("centred")
        lead_scaled, lead_shifted, var_ready = signal("lead_scaled"), signal("lead_shifted"), signal("var_ready")
        square_ready, square_used, scale_ready = signal("square_ready"), signal("square_used"), signal("scale_ready")
        scaled, x_ready, split_ready = signal("scaled"), signal("x_ready"), signal("split_ready")
        act_ready, product_ready, rounded = signal("act_ready"), signal("product_ready"), signal("rounded")
        rest_ready, z_ready = signal("rest_ready"), signal("z_ready")
        bank_free = [signal("bank_free0"), signal("bank_free1")]
        dve_chain, act_chain = signal("dve_chain"), signal("act_chain")
        gates_ready, decay_ready, inflow_ready, state_ready = (
            signal(n) for n in ("gates_ready", "decay_ready", "inflow_ready", "state_ready"))
        qk_ready, vt_ready, vt_psum, rows_ready, frame_ready, u_ready = (
            signal(n) for n in ("qk_ready", "vt_ready", "vt_psum", "rows_ready", "frame_ready", "u_ready"))
        score_ready, weight_arg, weight_ready, floor_ready, masked = (
            signal(n) for n in ("score_ready", "weight_arg", "weight_ready", "floor_ready", "masked"))
        attended, h_ready, y_ready, pair_ready = (signal(n) for n in ("attended", "h_ready", "y_ready", "pair_ready"))
        pool_zero, r_scaled = signal("pool_zero"), signal("r_scaled")
        conv_a, conv_b = signal("conv_a"), signal("conv_b")
        bias_loaded = [Signal(ctx.enter_context(nc.semaphore(f"bias_loaded{n}")), 0) for n in range(3)]
        stage_no = [0]

        def end_stage(**counts):
            for name, n in counts.items():
                signals[name].advance(n)
            stage_no[0] += 1


        def half(n0, i, u):
            return i + (n0 + u) // 2

        def fetch(sp, n0, i, u, size):
            c, s = i * 2 + (n0 + u), (n0 + u) % 2
            sp.wait_ge(lo_ready.sem, c + (PRIME - 1))
            sp.dma_start(raw[:, s, 0:size], t["weights"][c, :, 0:size]).then_inc(raw_loaded[s], 16)

        def split_hi(act, n0, i, u, size):
            c, s = i * 2 + (n0 + u), (n0 + u) % 2
            act.wait_ge(raw_loaded[s], (half(n0, i, u) + 1) * 16)
            act.wait_ge(chunk_used.sem, c + (PRIME - 1))
            act.activation(w_hi[:, s, 0:size], raw[:, s, 0:size], ACT.Copy).then_inc(hi_ready.sem, 1)

        def split_lo(dve, n0, i, u, size):
            c, s = i * 2 + (n0 + u), (n0 + u) % 2
            dve.wait_ge(hi_ready.sem, c + (PRIME + 1))
            dve.tensor_tensor(w_lo[:, s, 0:size], raw[:, s, 0:size], w_hi[:, s, 0:size].bitcast(F32),
                              ALU.subtract).then_inc(lo_ready.sem, 1)

        def for_chunks(eng, n, body, unroll=2, peel=2):
            turns = max(0, (n - peel) // unroll)
            if turns > 1:
                with eng.Fori(0, turns) as i:
                    for u in range(unroll):
                        body(i * (unroll // 2) + u // 2, u % 2)
            else:
                turns = 0
            for j in range(turns * unroll, n):
                body(j // 2, j % 2)

        def ahead(step, eng, n0, n, k):
            def body(i, u):
                if isinstance(i, int):
                    c = n0 + 2 * i + u + k
                    if c < n_chunks:
                        step(eng, c - c % 2, 0, c % 2, plan[c][1])
                else:
                    step(eng, n0 + k, i, u, plan[n0][1])
            return body

        def linear(pe, out, s, at, kts, hi, lo, first=True, last=True):
            for n, k in enumerate(kts):
                w = slice(at + n * P, at + n * P + P)
                pe.matmul(out, w_hi[:, s, w], hi(k), start=first and n == 0, stop=False)
                pe.matmul(out, w_hi[:, s, w], lo(k), start=False, stop=False)
                mm = pe.matmul(out, w_lo[:, s, w], hi(k), start=False, stop=last and n == len(kts) - 1)
            return mm

        def warm(pe, b, n):
            for _ in range(n):
                pe.matmul(bank[b][:, :], const["identity"], X[:, 0, :], start=True, stop=True)

        def x_parts():
            return (lambda k: x_hi[:, k, :]), (lambda k: x_lo[:, k, :])


        with nc.Block() as block:
            @block.sync
            def _(sp):
                for sig in signals.values():
                    sp.sem_inc(sig.sem, PRIME)
                sp.sem_inc(primed, 1)
                fetch(sp, 0, 0, 0, CHUNK)
                for k in range(KT):
                    sp.dma_start(X[:, k, :], t["x"][:, k, :]).then_inc(x_loaded[k], 16)
                fetch(sp, 0, 0, 1, CHUNK)
                sp.dma_start(consts[:, :, :], t["consts"][:, 0:2, :]).then_inc(loads_done, 16)
                sp.dma_start(mixer_consts[:, :, :], t["consts"][:, 2:, :]).then_inc(loads_done, 16)
                sp.dma_start(cols[:, :], t["cols"]).then_inc(loads_done, 16)

            @block.scalar
            def _(act):
                act.wait_ge(primed, 1)
                split_hi(act, 0, 0, 0, CHUNK)

            @block.vector
            def _(dve):
                dve.wait_ge(primed, 1)
                split_lo(dve, 0, 0, 0, CHUNK)
        c_next = [0]


        norm = [None]

        def lead_vector(dve):
            if norm[0] is None:
                return
            for n in range(KT + 1):
                if n < KT:
                    dve.tensor_tensor(X[:, n, :], X[:, n, :], stats[:, 0, :], ALU.mult).then_inc(lead_scaled.sem, 1)
                if n:
                    dve.wait_ge(lead_scaled.sem, lead_scaled.at(n))
                    dve.tensor_tensor(X[:, n - 1, :], X[:, n - 1, :], stats[:, 1, :], ALU.subtract).then_inc(lead_shifted.sem, 1)

        def lead_gain(act, k):
            n = (norm[0][0] * 3 + norm[0][1]) * KT + k
            act.wait_ge(lead_shifted.sem, lead_shifted.at(k + 1))
            act.activation(X[:, k, :], X[:, k, :], ACT.Identity, bias=col("ln_b", n), scale=col("ln_g", n))\
                .then_inc(x_ready.sem, 1)
            act.wait_ge(x_ready.sem, x_ready.at(k + 1))

        def lead_scalar(act):
            for k in range(KT):
                if norm[0] is None:
                    act.wait_ge(x_loaded[k], 16)
                else:
                    lead_gain(act, k)
                act.activation(x_hi[:, k, :], X[:, k, :], ACT.Copy).then_inc(rounded.sem, 1)

        def lead_pool(pool):
            for k in range(KT):
                pool.wait_ge(rounded.sem, rounded.at(k + 1))
                pool.tensor_tensor(x_lo[:, k, :], X[:, k, :], x_hi[:, k, :].bitcast(F32),
                                   ALU.subtract).then_inc(split_ready.sem, 1)

        def lead_tensor(pe, n0):
            pe.wait_ge(lo_ready.sem, PRIME + n0 + 1)
            for k in range(KT):
                pe.wait_ge(split_ready.sem, split_ready.at(k + 1))
                for v in range(2):
                    mm = linear(pe, bank[v][:, :], n0 % 2, (v * KT + k) * P, [k], lambda i: x_hi[:, i, :],
                                lambda i: x_lo[:, i, :], first=k == 0, last=k == KT - 1)
            mm.then_inc(chunk_used.sem, 1)

        def lead_counts():
            n = 0 if norm[0] is None else KT
            return dict(lead_scaled=n, lead_shifted=n, x_ready=n, rounded=KT, split_ready=KT)


        SHIFT = 4
        BEFORE = 6

        def shift_tensor(pe, acc):
            if norm[0] is None:
                pe.wait_ge(loads_done, 48)
            pe.wait_ge(zsum_ready.sem, zsum_ready.at(SHIFT - 1))
            pe.matmul(bank[6][:, :], const["mean_d"], acc, start=True, stop=True).then_inc(mean_ready.sem, 1)

        def tail_tensor(pe, acc, accq, sq, vb):
            pe.wait_ge(part_ready.sem, part_ready.at(KT - 2))
            pe.matmul(bank[7][:, :], const["mean_d"], acc, start=True, stop=False)
            pe.wait_ge(square_used.sem, square_used.at(KT - 2))
            pe.matmul(bank[vb][:, :], const["mean_d"], accq, start=True, stop=False)
            pe.wait_ge(centred.sem, centred.at(KT))
            pe.matmul(bank[7][:, :], const["mean_d"], X[:, KT - 1, :], start=False, stop=True)
            pe.wait_ge(square_ready.sem, square_ready.at(KT))
            pe.matmul(bank[vb][:, :], const["mean_d"], sq[:, (KT - 1) % 2, :], start=False, stop=True)\
                .then_inc(mean_ready.sem, 1)

        def centre_vector(dve, n, scale, b):
            dve.scalar_tensor_tensor(out=X[:, n, :], in0=b[:, :], scalar=scale, in1=X[:, n, :],
                                     op0=ALU.mult, op1=ALU.add).then_inc(z_ready.sem, 1)
            if n < BEFORE - 1:
                return
            if n == BEFORE - 1:
                dve.wait_ge(mean_ready.sem, mean_ready.at(1))
            for k in range(BEFORE) if n == BEFORE - 1 else [n]:
                dve.wait_ge(z_ready.sem, z_ready.at(k + 1))
                dve.scalar_tensor_tensor(out=X[:, k, :], in0=bank[6][:, :], scalar=-float(KT / SHIFT), in1=X[:, k, :],
                                         op0=ALU.mult, op1=ALU.add).then_inc(centred.sem, 1)

        def tail_vector(dve, vb):
            dve.wait_ge(var_ready.sem, var_ready.at(1))
            dve.tensor_tensor(stats[:, 0, :], bank[vb][:, :], stats[:, 1, :], ALU.subtract).then_inc(var_ready.sem, 1)
            dve.wait_ge(scale_ready.sem, scale_ready.at(2))
            dve.tensor_tensor(stats[:, 1, :], bank[7][:, :], stats[:, 0, :], ALU.mult)

        def square_scalar(act, k, accq, sq):
            act.wait_ge(centred.sem, centred.at(k + 1))
            if k > 2:
                act.wait_ge(square_used.sem, square_used.at(k - 2))
            act.activation(sq[:, k % 2, :] if k else accq, X[:, k, :], ACT.Square).then_inc(square_ready.sem, 1)

        def tail_scalar(act):
            act.preload_act_table_set(LOG_EXP)
            act.wait_ge(mean_ready.sem, mean_ready.at(2))
            act.activation(stats[:, 1, :], bank[7][:, :], ACT.Square).then_inc(var_ready.sem, 1)
            act.wait_ge(var_ready.sem, var_ready.at(2))
            rstd = stats[:, 0, :]
            act.activation(rstd, rstd, ACT.Ln, bias=col("eps_deepnorm")).then_inc(scale_ready.sem, 1)
            act.wait_ge(scale_ready.sem, scale_ready.at(1))
            act.activation(rstd, rstd, ACT.Exp, scale=-0.5).then_inc(scale_ready.sem, 1)

        def sums_pool(pool, acc, accq, sq):
            for k in range(1, SHIFT):
                pool.wait_ge(z_ready.sem, z_ready.at(k + 1))
                pool.wait_ge(zsum_ready.sem, zsum_ready.at(k - 1))
                pool.tensor_tensor(acc, acc if k > 1 else X[:, 0, :], X[:, k, :], ALU.add).then_inc(zsum_ready.sem, 1)
            for k in range(1, KT - 1):
                pool.wait_ge(centred.sem, centred.at(k + 1))
                pool.wait_ge(part_ready.sem, part_ready.at(k - 1))
                pool.tensor_tensor(acc, acc if k > 1 else X[:, 0, :], X[:, k, :], ALU.add).then_inc(part_ready.sem, 1)
                pool.wait_ge(square_ready.sem, square_ready.at(k + 1))
                pool.wait_ge(square_used.sem, square_used.at(k - 1))
                pool.tensor_tensor(accq, accq, sq[:, k % 2, :], ALU.add).then_inc(square_used.sem, 1)

        NORM = dict(zsum_ready=SHIFT - 1, mean_ready=2, centred=KT, square_ready=KT, square_used=KT - 2, part_ready=KT - 2,
                    var_ready=2, scale_ready=2, z_ready=KT)


        def swiglu(l, which):
            n0 = c_next[0]
            n1 = n0 + FT
            c_next[0] = n1 + 2 * KT
            scope = ExitStack()
            with scope:
                nm = f"f{stage_no[0]}_"
                g_hi = sb(nm + "g_hi", [P, FT, S], F32R, scope)
                g_lo = sb(nm + "g_lo", [P, FT, S], F32R, scope)
                silu = sb(nm + "silu", [P, 2, S], F32, scope)
                prod = sb(nm + "prod", [P, 2, S], F32, scope)
                acc, accq, sq, VB = prod[:, 0, :], prod[:, 1, :], silu, 3
                hi, lo = x_parts()
                with nc.Block() as block:
                    @block.sync
                    def _(sp):
                        for_chunks(sp, FT, ahead(fetch, sp, n0, FT, 2))
                        for_chunks(sp, 2 * KT, ahead(fetch, sp, n1, 2 * KT, 2))

                    @block.tensor
                    def _(pe):
                        def gate_up(i, u):
                            s, j = (n0 + u) % 2, i * 2 + u
                            pe.wait_ge(lo_ready.sem, j + (PRIME + n0 + 1))
                            pe.wait_ge(product_ready.sem, product_ready.at(-1) + j)
                            linear(pe, bank[2 * u][:, :], s, 0, range(KT), hi, lo)
                            linear(pe, bank[2 * u + 1][:, :], s, KT * P, range(KT), hi, lo)\
                                .then_inc(chunk_used.sem, 1)

                        def g_tile(g, first):
                            def tile(k):
                                if first and k in (FH - 1, FT - 2, FT - 1):
                                    pe.wait_ge(rest_ready.sem, rest_ready.at(k + 1))
                                return g[:, k, :]
                            return tile

                        def down(i, v, first=False):
                            for u in range(2):
                                s = (n1 + u) % 2
                                pe.wait_ge(lo_ready.sem, i * 4 + (PRIME + n1 + 2 * v + u + 1))
                                if u == 0:
                                    pe.wait_ge(z_ready.sem, z_ready.at(-1 + v) + i * 2)
                                linear(pe, bank[4 + v][:, :], s, 0, range(FH * u, FH * u + FH), g_tile(g_hi, first),
                                       g_tile(g_lo, first), first=u == 0, last=u == 1).then_inc(chunk_used.sem, 1)

                        lead_tensor(pe, n0)
                        gate_up(0, 1)
                        with pe.Fori(1, FT // 2) as i:
                            for u in range(2):
                                gate_up(i, u)
                        down(0, 0, first=True)
                        down(0, 1)
                        with pe.Fori(1, BEFORE // 2) as i:
                            for v in range(2):
                                down(i, v)
                        shift_tensor(pe, acc)
                        for v in range(2):
                            down(BEFORE // 2, v)
                        tail_tensor(pe, acc, accq, sq, VB)

                    @block.scalar
                    def _(act):
                        split = ahead(split_hi, act, n0, FT, 1)

                        def rest(i, u):
                            j = i * 2 + u
                            act.wait_ge(chunk_used.sem, j + (PRIME + n0 + 1))
                            act.wait_ge(product_ready.sem, product_ready.at(-1) + j)
                            act.activation(silu[:, u, :], bank[2 * u][:, :], ACT.Silu).then_inc(act_ready.sem, 1)
                            act.wait_ge(product_ready.sem, product_ready.at(1) + j)
                            act.activation(g_hi[:, j, :], prod[:, u, :], ACT.Copy).then_inc(rounded.sem, 1)

                        def body(i, u):
                            split(i, u)
                            rest(i, u)

                        if norm[0] is None:
                            lead_scalar(act)
                            split(0, 0)
                        else:
                            split(0, 0)
                            lead_scalar(act)
                        rest(0, 0)
                        body(0, 1)
                        with act.Fori(1, FT // 2 - 1) as i:
                            for u in range(2):
                                body(i, u)
                        for u in range(2):
                            body(FT // 2 - 1, u)
                        split2 = ahead(split_hi, act, n1, 2 * KT, 1)
                        for_chunks(act, 2 * BEFORE, split2, peel=0)
                        for j in range(2 * BEFORE, 2 * KT):
                            split2(j // 2, j % 2)
                            if j == 2 * BEFORE:
                                for k in range(BEFORE):
                                    square_scalar(act, k, accq, sq)
                        for k in range(BEFORE, KT):
                            square_scalar(act, k, accq, sq)
                        tail_scalar(act)

                    @block.vector
                    def _(dve):
                        split = ahead(split_lo, dve, n0, FT, 1)

                        def rest(i, u):
                            j = i * 2 + u
                            dve.wait_ge(act_ready.sem, act_ready.at(1) + j)
                            dve.wait_ge(rest_ready.sem, rest_ready.at(-1) + j)
                            dve.tensor_tensor(prod[:, u, :], silu[:, u, :], bank[2 * u + 1][:, :],
                                              ALU.mult).then_inc(product_ready.sem, 1)

                        def body(i, u):
                            split(i, u)
                            rest(i, u)

                        lead_vector(dve)
                        body(0, 0)
                        body(0, 1)
                        with dve.Fori(1, FT // 2 - 1) as i:
                            for u in range(2):
                                body(i, u)
                        for u in range(2):
                            body(FT // 2 - 1, u)
                        split2 = ahead(split_lo, dve, n1, 2 * KT, 1)
                        for n in range(KT):
                            split2(n, 0)
                            split2(n, 1)
                            dve.wait_ge(chunk_used.sem, PRIME + n1 + 2 * n + 2)
                            centre_vector(dve, n, 0.5 / ALPHA, bank[4 + n % 2])
                        tail_vector(dve, VB)

                    @block.gpsimd
                    def _(pool):
                        def body(i, u):
                            j = i * 2 + u
                            pool.wait_ge(rounded.sem, rounded.at(KT + 1) + j)
                            pool.tensor_tensor(g_lo[:, j, :], prod[:, u, :], g_hi[:, j, :].bitcast(F32),
                                               ALU.subtract).then_inc(rest_ready.sem, 1)

                        lead_pool(pool)
                        for_chunks(pool, FT, body)
                        sums_pool(pool, acc, accq, sq)
            counts = lead_counts()
            counts["rounded"] += FT
            end_stage(act_ready=FT, product_ready=FT, rest_ready=FT, **counts, **NORM)
            norm[0] = (l, which)


        def mixer_out(l):
            n0 = c_next[0]
            n = KT // 2
            c_next[0] = n0 + n
            scope = ExitStack()
            with scope:
                nm = f"o{stage_no[0]}_"
                sq = sb(nm + "sq", [P, 2, S], F32, scope)
                sums = sb(nm + "sums", [P, 2, S], F32, scope)
                acc, accq, VB = sums[:, 0, :], sums[:, 1, :], 5
                hi, lo = x_parts()
                with nc.Block() as block:
                    @block.sync
                    def _(sp):
                        for_chunks(sp, n, ahead(fetch, sp, n0, n, 2), peel=n)

                    @block.tensor
                    def _(pe):
                        for j in range(n):
                            u = j % 2
                            s = (n0 + u) % 2
                            pe.wait_ge(lo_ready.sem, PRIME + n0 + j + 1)
                            pe.wait_ge(z_ready.sem, z_ready.at(2 * j - 2))
                            linear(pe, bank[2 * u][:, :], s, 0, range(KT), hi, lo).then_inc(psum_ready.sem, 1)
                            linear(pe, bank[2 * u + 1][:, :], s, KT * P, range(KT), hi, lo)\
                                .then_inc(chunk_used.sem, 1)
                            if 2 * j + 2 == BEFORE:
                                shift_tensor(pe, acc)
                        tail_tensor(pe, acc, accq, sq, VB)

                    @block.scalar
                    def _(act):
                        for_chunks(act, n, ahead(split_hi, act, n0, n, 1), peel=n)
                        for k in range(KT):
                            square_scalar(act, k, accq, sq)
                        tail_scalar(act)

                    @block.vector
                    def _(dve):
                        split = ahead(split_lo, dve, n0, n, 1)
                        for j in range(n):
                            split(j // 2, j % 2)
                            for v in range(2):
                                if v == 0:
                                    dve.wait_ge(psum_ready.sem, psum_ready.at(j + 1))
                                else:
                                    dve.wait_ge(chunk_used.sem, PRIME + n0 + j + 1)
                                centre_vector(dve, 2 * j + v, 1.0 / ALPHA, bank[2 * (j % 2) + v])
                        tail_vector(dve, VB)

                    @block.gpsimd
                    def _(pool):
                        sums_pool(pool, acc, accq, sq)
            end_stage(psum_ready=n, **NORM)
            norm[0] = (l, 1)


        def even_mixer(l):
            n0 = c_next[0]
            c_next[0] = n0 + EVEN_TILES // 2
            with ExitStack() as scope:
                arena = sb("even_arena", [P, 93 * 256], F32, scope)
                rate = sb("rg_rate", [P, 8], F32, scope)
                ucol = sb("ml_ucol", [P, S // P * 4], F32, scope)

                def at(kb, *shape, rows=P):
                    n = int(np.prod(shape))
                    ap = arena[0:rows, kb * 256:kb * 256 + n]
                    return ap.rearrange("p (a b) -> p a b", b=shape[-1])

                U = at(0, 4, S)
                QK = at(16, 8, S)
                O = at(40, 4, S)
                VT = at(48, S // P, S)
                fr = at(76, 6, S, rows=4)
                even_project(n0, at, U, QK, O, VT, fr, rate, ucol)
                mlstm(at, U, QK, O, VT, fr, ucol)
            mixer_out(l)

        def even_project(n0, at, U, QK, O, VT, fr, rate, ucol):
            n, NS = EVEN_TILES // 2, S // P
            RG = at(8, 4, S)
            V = at(32, 4, S)
            E, TH, R, I = (at(40 + 8 * m, 4, S) for m in range(4))
            rows = at(72, 2, S, rows=4)
            wab = at(88, 8, P)
            ident = const["identity"]
            hi, lo = x_parts()
            GATES, RGG, VV, QKK, OO = 2, 3, 5, 7, 11

            with nc.Block() as block:
                @block.sync
                def _(sp):
                    sp.dma_start(wab[:, :, :], t["rg_w"]).then_inc(loads_done, 16)
                    for_chunks(sp, n, ahead(fetch, sp, n0, n, 2))

                @block.tensor
                def _(pe):
                    def chunk(i, u):
                        s = (n0 + u) % 2
                        pe.wait_ge(lo_ready.sem, i * 2 + (PRIME + n0 + u + 1))
                        pe.wait_ge(bank_free[u].sem, bank_free[u].at(0) + i)
                        linear(pe, bank[2 * u][:, :], s, 0, range(KT), hi, lo)
                        linear(pe, bank[2 * u + 1][:, :], s, KT * P, range(KT), hi, lo).then_inc(chunk_used.sem, 1)

                    def rg_gates(k):
                        pe.wait_ge(loads_done, loads.at(16))
                        pe.wait_ge(u_ready.sem, u_ready.at(k + 1))
                        pe.wait_ge(gates_ready.sem, gates_ready.at(k - 1))
                        for x in range(2):
                            mm = pe.matmul(bank[4 + 2 * (k % 2) + x][:, :], wab[:, 4 * x + k, :], U[:, k, :], start=True, stop=True)
                        mm.then_inc(psum_ready.sem, 1)

                    def turn_v():
                        pe.wait_ge(bank_free[0].sem, bank_free[0].at(4))
                        pe.wait_ge(gates_ready.sem, gates_ready.at(4))
                        for st in range(NS):
                            for h in range(4):
                                mm = pe.transpose(bank[4 + st][:, h * P:(h + 1) * P], V[:, h, st * P:(st + 1) * P], ident)
                            mm.then_inc(vt_psum.sem, 1)

                    def turn_u():
                        pe.wait_ge(frame_ready.sem, frame_ready.at(1))
                        pe.wait_ge(vt_ready.sem, vt_ready.at(1))
                        for st in range(NS):
                            mm = pe.transpose(bank[4][:, st * 4:st * 4 + 4], fr[:, 2, st * P:(st + 1) * P], ident[0:4, 0:4])
                        mm.then_inc(vt_psum.sem, 1)

                    lead_tensor(pe, n0)
                    chunk(0, 1)
                    for j in range(2, n):
                        chunk(j // 2, j % 2)
                        if j == GATES or j == GATES + 1:
                            rg_gates(2 * (j - GATES))
                            rg_gates(2 * (j - GATES) + 1)
                        elif j == QKK:
                            turn_v()
                        elif j == QKK + 1:
                            turn_u()

                @block.scalar
                def _(act):
                    ch = Chain(act, act_chain)
                    split = ahead(split_hi, act, n0, n, 1)

                    def leave(j, out, k, f):
                        act.wait_ge(chunk_used.sem, PRIME + n0 + j + 1)
                        for v in range(2):
                            ins = act.activation(out[:, k + v, :], bank[2 * (j % 2) + v][:, :], f)
                        ins.then_inc(bank_free[j % 2].sem, 1)

                    def sigmoids(k):
                        act.wait_ge(psum_ready.sem, psum_ready.at(k + 1))
                        b = 4 + 2 * (k % 2)
                        act.activation(R[:, k, :], bank[b][:, :], ACT.Sigmoid, bias=col("rg_ba", k))
                        act.activation(I[:, k, :], bank[b + 1][:, :], ACT.Sigmoid, bias=col("rg_bx", k)).then_inc(gates_ready.sem, 1)

                    def silu(k):
                        act.wait_ge(qk_ready.sem, qk_ready.at(k + 1))
                        act.activation(QK[:, k, :], QK[:, k, :], ACT.Silu)

                    split(0, 0)
                    lead_scalar(act)
                    for j in range(n):
                        if j:
                            split(j // 2, j % 2)
                        if j == 0:
                            lam = cols[:, col_at["rg_lambda"]:col_at["rg_lambda"] + 4]
                            ch.add(act.activation(rate[:, 0:4], lam, ACT.Abs))
                            ch.wait()
                            ch.add(act.activation(rate[:, 0:4], rate[:, 0:4], ACT.Exp, scale=-1.0))
                            ch.wait()
                            act.activation(rate[:, 0:4], rate[:, 0:4], ACT.Ln, bias=1.0).then_inc(decay_ready.sem, 1)
                        elif j == GATES:
                            act.wait_ge(chunk_used.sem, PRIME + n0 + j + 1)
                            for v, bias in enumerate(("ml_i_bias", "ml_f_bias")):
                                ins = act.activation(rows[:, v, :], bank[2 * (j % 2) + v][0:4, :], ACT.Identity, bias=col(bias)[0:4])
                            ins.then_inc(bank_free[j % 2].sem, 1)
                            act.wait_ge(bank_free[j % 2].sem, bank_free[j % 2].at(j // 2 + 1))
                            ch.add(act.activation(fr[:, 0, :], rows[:, 1, :], ACT.Abs))
                            ch.wait()
                            ch.add(act.activation(fr[:, 0, :], fr[:, 0, :], ACT.Exp, scale=-1.0))
                            ch.wait()
                            act.activation(fr[:, 0, :], fr[:, 0, :], ACT.Ln, bias=1.0).then_inc(rows_ready.sem, 1)
                            sigmoids(0)
                            sigmoids(1)
                        elif j == RGG:
                            leave(j, RG, 0, ACT.Gelu_apprx_tanh)
                            sigmoids(2)
                            sigmoids(3)
                        elif j == RGG + 1:
                            leave(j, RG, 2, ACT.Gelu_apprx_tanh)
                            act.wait_ge(gates_ready.sem, gates_ready.at(4))
                            act.wait_ge(inflow_ready.sem, inflow_ready.at(1))
                            for k in range(4):
                                act.activation(TH[:, k, :], R[:, k, :], ACT.Tanh, scale=rate[:, k:k + 1]).then_inc(gates_ready.sem, 1)
                        elif j == VV:
                            leave(j, V, 0, ACT.Copy)
                            for k in range(4):
                                act.activation(E[:, k, :], R[:, k, :], ACT.Exp, scale=rate[:, 4 + k:5 + k]).then_inc(gates_ready.sem, 1)
                        elif j == VV + 1:
                            leave(j, V, 2, ACT.Copy)
                            act.wait_ge(gates_ready.sem, gates_ready.at(12))
                            for k in range(4):
                                act.activation(R[:, k, :], TH[:, k, :], ACT.Sqrt).then_inc(gates_ready.sem, 1)
                        elif j == QKK + 1:
                            act.wait_ge(centred.sem, centred.at(1))
                            act.wait_ge(gates_ready.sem, gates_ready.at(16))
                            for st in range(NS):
                                act.wait_ge(vt_psum.sem, vt_psum.at(st + 1))
                                act.activation(VT[:, st, :], bank[4 + st][:, :], ACT.Copy).then_inc(vt_ready.sem, 1)
                            silu(0)
                            silu(1)
                        elif j == QKK + 2:
                            act.wait_ge(vt_psum.sem, vt_psum.at(NS + 1))
                            act.activation(ucol[:, :], bank[4][:, 0:4 * NS], ACT.Copy)
                            silu(2)
                            silu(3)
                        elif j == QKK + 3:
                            silu(4)
                            silu(5)
                        elif j >= OO:
                            if j == OO:
                                silu(6)
                                silu(7)
                                act.wait_ge(y_ready.sem, y_ready.at(4))
                            leave(j, O, 2 * (j - OO), ACT.Sigmoid)

                @block.vector
                def _(dve):
                    ch = Chain(dve, dve_chain)
                    split = ahead(split_lo, dve, n0, n, 1)

                    def causal_conv(j, out, k, name, tiles, done):
                        dve.wait_ge(chunk_used.sem, PRIME + n0 + j + 1)
                        b = lambda v: bank[2 * (j % 2) + v]
                        w = lambda v, i: col(f"{name}_w", i * tiles + k + v)
                        for v in range(2):
                            ch.add(dve.tensor_scalar(out[:, k + v, :], b(v)[:, :], w(v, 3), col(f"{name}_b", k + v), ALU.mult, ALU.add))
                        for i in (2, 1, 0):
                            d = 3 - i
                            for v in range(2):
                                ch.wait(ch.n - 1)
                                o = out[:, k + v, d:S]
                                ins = dve.scalar_tensor_tensor(out=o, in0=b(v)[:, 0:S - d], scalar=w(v, i), in1=o,
                                                               op0=ALU.mult, op1=ALU.add)
                                ch.add(ins)
                        ch.wait()
                        dve.sem_inc(done.sem, 2)
                        dve.sem_inc(bank_free[j % 2].sem, 1)

                    def rg_scan(k):
                        dve.wait_ge(gates_ready.sem, gates_ready.at(12 + k + 1))
                        ch.add(dve.tensor_scalar(E[:, k, :], E[:, k, :], -1.0, 1.0, ALU.mult, ALU.add))
                        ch.add(dve.tensor_tensor(I[:, k, :], I[:, k, :], R[:, k, :], ALU.mult))
                        ch.wait()
                        ch.add(dve.tensor_tensor_scan(U[:, k, :], E[:, k, :], I[:, k, :], 0.0, ALU.mult, ALU.add))
                        dve.wait_ge(bank_free[0].sem, bank_free[0].at(3))
                        ch.wait()
                        dve.tensor_tensor(U[:, k, :], U[:, k, :], RG[:, k, :], ALU.mult).then_inc(y_ready.sem, 1)

                    lead_vector(dve)
                    for j in range(n):
                        split(j // 2, j % 2)
                        if j < GATES:
                            causal_conv(j, U, 2 * j, "rg_conv", 4, u_ready)
                        if j == 1:
                            lam = cols[:, col_at["rg_lambda"]:col_at["rg_lambda"] + 4]
                            ch.add(dve.tensor_scalar(rate[:, 4:8], lam, -1.0, 0.0, ALU.mult, ALU.max))
                            dve.wait_ge(decay_ready.sem, decay_ready.at(1))
                            ch.wait()
                            ch.add(dve.tensor_tensor(rate[:, 0:4], rate[:, 0:4], rate[:, 4:8], ALU.add))
                            ch.wait()
                            ch.add(dve.tensor_scalar(rate[:, 4:8], rate[:, 0:4], -8.0, None, ALU.mult))
                            ch.wait()
                            dve.tensor_scalar(rate[:, 0:4], rate[:, 0:4], 4.0, None, ALU.mult).then_inc(inflow_ready.sem, 1)
                        elif j == RGG:
                            ch.add(dve.memset(fr[:, 5, :], 1.0))
                            dve.wait_ge(rows_ready.sem, rows_ready.at(1))
                            ch.add(dve.tensor_scalar(rows[:, 1, :], rows[:, 1, :], 0.0, None, ALU.min))
                            ch.wait()
                            ch.add(dve.tensor_tensor(fr[:, 0, :], rows[:, 1, :], fr[:, 0, :], ALU.subtract))
                            ch.wait()
                            ch.add(dve.tensor_tensor_scan(fr[:, 1, :], fr[:, 5, :], fr[:, 0, :], 0.0, ALU.mult, ALU.add))
                            ch.wait()
                            dve.tensor_tensor(fr[:, 2, :], rows[:, 0, :], fr[:, 1, :], ALU.subtract).then_inc(frame_ready.sem, 1)
                            dve.wait_ge(frame_ready.sem, frame_ready.at(1))
                            ch.add(dve.tensor_tensor_scan(fr[:, 3, :], fr[:, 2, :], fr[:, 2, :], 0.0, ALU.max, ALU.max))
                            ch.wait()
                            ch.add(dve.tensor_tensor(fr[:, 4, :], fr[:, 1, :], fr[:, 3, :], ALU.add))
                        elif j == VV:
                            dve.wait_ge(gates_ready.sem, gates_ready.at(4))
                            for k in range(4):
                                ch.add(dve.tensor_tensor(I[:, k, :], I[:, k, :], U[:, k, :], ALU.mult))
                        elif j == VV + 1:
                            dve.wait_ge(gates_ready.sem, gates_ready.at(12))
                            for k in range(4):
                                ch.add(dve.tensor_scalar(E[:, k, :], E[:, k, :], 1.0, None, ALU.add))
                            ch.wait()
                            for k in range(4):
                                ch.add(dve.tensor_tensor(I[:, k, :], I[:, k, :], E[:, k, :], ALU.mult))
                            for k in range(4):
                                ins = dve.tensor_tensor(E[:, k, :], TH[:, k, :], E[:, k, :], ALU.mult)
                            ins.then_inc(centred.sem, 1)
                            dve.wait_ge(centred.sem, centred.at(1))
                        if QKK <= j < OO:
                            causal_conv(j, QK, 2 * (j - QKK), "ml_conv", 8, qk_ready)
                            if j < QKK + 2:
                                rg_scan(2 * (j - QKK))
                                rg_scan(2 * (j - QKK) + 1)

                @block.gpsimd
                def _(pool):
                    lead_pool(pool)
            loads.advance(16)
            end_stage(bank_free0=7, bank_free1=6, psum_ready=4, act_chain=4, decay_ready=1, gates_ready=16, inflow_ready=1,
                      y_ready=4, u_ready=4, qk_ready=8, rows_ready=1, frame_ready=1, centred=1, vt_psum=NS + 1, vt_ready=NS,
                      dve_chain=6 * 8 + 3 + 6 + 4 + 8 + 4 * 3, **lead_counts())

        def mlstm(at, U, QK, O, VT, fr, ucol):
            H4, ST = 4, S // P
            scale = float(P) ** -0.5
            W = [at(56 + 8 * m, ST, S) for m in range(2)]
            EM = at(88, 2, S)
            H = at(8, 2, S)
            sq, rs = at(32, 2, S), at(36, 2, S)

            def span(st):
                return slice(st * P, S)

            def score_at(st):
                return bank[min(st, 2)][:, span(st)] if st < 3 else bank[2][:, 0:P]

            with nc.Block() as block:
                @block.tensor
                def _(pe):
                    def frame(h):
                        pe.wait_ge(weight_arg.sem, weight_arg.at(h))
                        pe.wait_ge(floor_ready.sem, floor_ready.at(h))
                        pe.matmul(bank[6][:, :], const[f"pick{h}"][0:4], fr[:, 3, :], start=True, stop=True)
                        pe.matmul(bank[7][:, :], const[f"pick{h}"][0:4], fr[:, 4, :], start=True, stop=True)\
                            .then_inc(psum_ready.sem, 1)

                    def scores(h):
                        pe.wait_ge(inflow_ready.sem, inflow_ready.at(ST * h))
                        for st in range(ST):
                            mm = pe.matmul(score_at(st), QK[:, 4 + h, st * P:(st + 1) * P], QK[:, h, span(st)],
                                           start=True, stop=True)
                        mm.then_inc(score_ready.sem, 1)

                    def sums(h):
                        pe.wait_ge(h_ready.sem, h_ready.at(h))
                        for st in range(ST):
                            pe.wait_ge(masked.sem, masked.at(ST * h + st + 1))
                            pe.matmul(bank[4][:, span(st)], VT[:, st, h * P:(h + 1) * P], W[h % 2][:, st, span(st)],
                                      start=st == 0, stop=st == ST - 1)
                            mm = pe.matmul(bank[5][:, span(st)], const["ones"], W[h % 2][:, st, span(st)],
                                           start=st == 0, stop=st == ST - 1)
                        mm.then_inc(attended.sem, 1)

                    def mean(h):
                        pe.wait_ge(h_ready.sem, h_ready.at(h + 1))
                        pe.wait_ge(scale_ready.sem, scale_ready.at(2 * h - 1))
                        pe.matmul(bank[3][:, :], const["mean_p"], H[:, h % 2, :], start=True, stop=True).then_inc(mean_ready.sem, 1)

                    def variance(h):
                        pe.wait_ge(square_ready.sem, square_ready.at(h + 1))
                        pe.matmul(bank[3][:, :], const["mean_p"], sq[:, h % 2, :], start=True, stop=True).then_inc(square_used.sem, 1)

                    frame(0)
                    scores(0)
                    for h in range(H4 + 1):
                        if h:
                            mean(h - 1)
                        if h + 1 < H4:
                            frame(h + 1)
                        if h < H4:
                            sums(h)
                        if h:
                            variance(h - 1)
                        if h + 1 < H4:
                            scores(h + 1)

                @block.scalar
                def _(act):
                    def weights(h):
                        act.wait_ge(psum_ready.sem, psum_ready.at(h + 1))
                        act.wait_ge(h_ready.sem, h_ready.at(h - 1))
                        act.activation(EM[:, h % 2, :], bank[7][:, :], ACT.Exp, scale=-1.0).then_inc(floor_ready.sem, 1)
                        act.wait_ge(weight_arg.sem, weight_arg.at(h + 1))
                        for st in range(ST):
                            w = W[h % 2][:, st, span(st)]
                            ins = act.activation(w, w, ACT.Exp, scale=-1.0)
                        ins.then_inc(weight_ready.sem, 1)

                    def over_den(h):
                        e = EM[:, h % 2, :]
                        act.wait_ge(gates_ready.sem, gates_ready.at(h + 1))
                        act.activation(e, e, ACT.Ln).then_inc(decay_ready.sem, 1)
                        act.wait_ge(decay_ready.sem, decay_ready.at(2 * h + 1))
                        act.activation(e, e, ACT.Exp, scale=-1.0).then_inc(decay_ready.sem, 1)

                    def square(h):
                        act.wait_ge(centred.sem, centred.at(h + 1))
                        act.wait_ge(square_used.sem, square_used.at(h - 1))
                        act.activation(sq[:, h % 2, :], H[:, h % 2, :], ACT.Square).then_inc(square_ready.sem, 1)

                    def factor(h):
                        r = rs[:, h % 2, :]
                        act.wait_ge(square_used.sem, square_used.at(h + 1))
                        act.wait_ge(y_ready.sem, y_ready.at(h - 1))
                        act.activation(r, bank[3][:, :], ACT.Ln, bias=col("eps_ml")).then_inc(scale_ready.sem, 1)
                        act.wait_ge(scale_ready.sem, scale_ready.at(2 * h + 1))
                        act.activation(r, r, ACT.Exp, scale=-0.5).then_inc(scale_ready.sem, 1)

                    def round_y(h):
                        act.wait_ge(y_ready.sem, y_ready.at(h + 1))
                        act.activation(x_hi[:, 4 + h, :], H[:, h % 2, :], ACT.Copy).then_inc(rounded.sem, 1)

                    act.preload_act_table_set(LOG_EXP)
                    weights(0)
                    for k in range(4):
                        act.activation(x_hi[:, k, :], U[:, k, :], ACT.Copy).then_inc(x_ready.sem, 1)
                    for h in range(H4 + 1):
                        if h:
                            square(h - 1)
                        if h + 1 < H4:
                            weights(h + 1)
                        if h < H4:
                            over_den(h)
                        if h:
                            factor(h - 1)
                            round_y(h - 1)

                @block.vector
                def _(dve):
                    ch = Chain(dve, dve_chain)

                    def weight_args(h):
                        dve.wait_ge(psum_ready.sem, psum_ready.at(h + 1))
                        dve.wait_ge(attended.sem, attended.at(h - 1))
                        for st in range(ST):
                            ins = dve.tensor_scalar(W[h % 2][:, st, span(st)], bank[6][:, span(st)],
                                                    ucol[:, st * 4 + h:st * 4 + h + 1], 0.0, ALU.subtract, ALU.max)
                        ins.then_inc(weight_arg.sem, 1)

                    def weigh(h):
                        dve.wait_ge(score_ready.sem, score_ready.at(h + 1))
                        dve.wait_ge(weight_ready.sem, weight_ready.at(h + 1))
                        for st in range(ST):
                            w = W[h % 2][:, st, span(st)]
                            dve.scalar_tensor_tensor(out=w, in0=score_at(st), scalar=scale, in1=w, op0=ALU.mult, op1=ALU.mult)\
                                .then_inc(inflow_ready.sem, 1)

                    def denominator(h):
                        e = EM[:, h % 2, :]
                        dve.wait_ge(attended.sem, attended.at(h + 1))
                        dve.wait_ge(floor_ready.sem, floor_ready.at(h + 1))
                        ch.add(dve.tensor_tensor(e, bank[5][:, :], e, ALU.max))
                        ch.wait()
                        dve.scalar_tensor_tensor(out=e, in0=bank[5][:, :], scalar=-1.0, in1=e, op0=ALU.mult,
                                                 op1=ALU.max).then_inc(gates_ready.sem, 1)

                    def divide(h):
                        dve.wait_ge(decay_ready.sem, decay_ready.at(2 * h + 2))
                        dve.wait_ge(rest_ready.sem, rest_ready.at(h - 1))
                        dve.tensor_tensor(H[:, h % 2, :], bank[4][:, :], EM[:, h % 2, :], ALU.mult).then_inc(h_ready.sem, 1)

                    def centre(h):
                        hb = H[:, h % 2, :]
                        dve.wait_ge(mean_ready.sem, mean_ready.at(h + 1))
                        dve.tensor_tensor(hb, hb, bank[3][:, :], ALU.subtract).then_inc(centred.sem, 1)

                    def gate(h):
                        hb = H[:, h % 2, :]
                        dve.wait_ge(scale_ready.sem, scale_ready.at(2 * h + 2))
                        ch.add(dve.scalar_tensor_tensor(out=hb, in0=hb, scalar=col("ml_norm_g", h), in1=rs[:, h % 2, :],
                                                        op0=ALU.mult, op1=ALU.mult))
                        ch.wait()
                        dve.tensor_tensor(hb, hb, O[:, h, :], ALU.mult).then_inc(y_ready.sem, 1)

                    weight_args(0)
                    for h in range(H4 + 1):
                        if h < H4:
                            weigh(h)
                        if h:
                            centre(h - 1)
                        if h + 1 < H4:
                            weight_args(h + 1)
                        if h < H4:
                            denominator(h)
                        if h:
                            gate(h - 1)
                        if h < H4:
                            divide(h)

                @block.gpsimd
                def _(pool):
                    for h in range(H4 + 1):
                        if h < H4:
                            for st in range(ST):
                                pool.wait_ge(inflow_ready.sem, inflow_ready.at(ST * h + st + 1))
                                d = W[h % 2][:, st, st * P:(st + 1) * P]
                                pool.affine_select(out=d, in_=d, pattern=[[1, P]], compare_op=ALU.is_ge, fill=0.0,
                                                   base=0, channel_multiplier=-1).then_inc(masked.sem, 1)
                            pool.wait_ge(x_ready.sem, x_ready.at(h + 1))
                            pool.tensor_tensor(x_lo[:, h, :], U[:, h, :], x_hi[:, h, :].bitcast(F32), ALU.subtract)
                        if h:
                            pool.wait_ge(rounded.sem, rounded.at(h))
                            pool.tensor_tensor(x_lo[:, 3 + h, :], H[:, (h - 1) % 2, :], x_hi[:, 3 + h, :].bitcast(F32),
                                               ALU.subtract).then_inc(rest_ready.sem, 1)
            end_stage(psum_ready=H4, score_ready=H4, weight_arg=H4, weight_ready=H4, inflow_ready=ST * H4, floor_ready=H4,
                      masked=ST * H4, attended=H4, gates_ready=H4, decay_ready=2 * H4, h_ready=H4, mean_ready=H4, centred=H4,
                      square_ready=H4, square_used=H4, scale_ready=2 * H4, y_ready=H4, rounded=H4, x_ready=4, rest_ready=H4,
                      dve_chain=2 * H4)


        def odd_mixer(l):
            n0 = c_next[0]
            c_next[0] = n0 + ODD_TILES // 2
            with ExitStack() as scope:
                arena = sb("odd_arena", [P, 99 * 256], F32, scope)

                def at(kb, *shape, rows=P):
                    n = int(np.prod(shape))
                    ap = arena[0:rows, int(kb * 256):int(kb * 256) + n]
                    return ap if len(shape) == 1 else ap.rearrange("p (a b) -> p a b", b=shape[1])

                RK = at(0, 13, S)
                one_less = sb("rk_one_less", [P, 17], F32, scope)
                OG = at(56, 4, S)
                GO = at(64, 4, S)
                lora, scan_reset = stats[:, 0, :], stats[:, 1, :]
                gla(n0, at, RK, one_less, OG, GO, lora, scan_reset)
                rwkv(at, RK, one_less, OG, GO, lora, scan_reset)
            mixer_out(l)

        def gla(n0, at, RK, one_less, OG, GO, lora, scan_reset):
            n = ODD_TILES // 2
            C, NB, H4 = 64, S // P, 4
            NC = S // C
            tau = 1.0 / 16.0
            GQ, GK, GV = at(26, 2, S), at(30, 2, S), at(34, 4, S)
            GD = at(42, S, rows=16)
            Z, CUM = at(44, 2, S), at(48, 2, S)
            E1, E2 = OG[:, 0:2, :], OG[:, 2:4, :]
            K2 = at(52, 2, S)
            VT = at(72, NB, S)
            K2T = at(80, 2, S)
            ST = at(84, NC + 1, 2 * P)
            reset, gB, mask = at(93, S), at(95, 2 * P, rows=16), at(96, P)
            dec = at(97, 2, NC)
            AT = GV
            ident = const["identity"]
            hi, lo = x_parts()
            dest = [(GQ, 0), (GQ, 1), (GK, 0), (GK, 1)] + [(GV, k) for k in range(4)] + [(GD, None)]
            dest += [(GO, k) for k in range(4)] + [(RK, 12)] + [(RK, k) for k in range(12)]

            with nc.Block() as block:
                @block.sync
                def _(sp):
                    sp.dma_start(gB[:, :], t["gla_gB"]).then_inc(loads_done, 16)
                    sp.dma_start(reset[:, :], t["masks"][:, S:2 * S]).then_inc(loads_done, 16)
                    sp.dma_start(mask[:, :], t["masks"][:, 2 * S + 2 * P:2 * S + 3 * P]).then_inc(loads_done, 16)
                    for_chunks(sp, n, ahead(fetch, sp, n0, n, 2))
                    sp.wait_ge(lead_shifted.sem, lead_shifted.at(KT))
                    sp.dma_start(lora[:, :], t["rk_lora"]).then_inc(loads_done, 16)
                    sp.dma_start(scan_reset[:, :], t["masks"][:, 0:S]).then_inc(loads_done, 16)

                @block.tensor
                def _(pe):
                    def chunk(i, u):
                        s = (n0 + u) % 2
                        pe.wait_ge(lo_ready.sem, i * 2 + (PRIME + n0 + u + 1))
                        pe.wait_ge(bank_free[u].sem, bank_free[u].at(0) + i)
                        linear(pe, bank[2 * u][:, :], s, 0, range(KT), hi, lo)
                        linear(pe, bank[2 * u + 1][:, :], s, KT * P, range(KT), hi, lo).then_inc(chunk_used.sem, 1)

                    def gates():
                        pe.wait_ge(loads_done, loads.at(48))
                        pe.wait_ge(bank_free[0].sem, bank_free[0].at(3))
                        for k in range(2):
                            mm = pe.matmul(bank[4 + k][:, :], gB[:, k * P:(k + 1) * P], GD[:, :], start=True, stop=True)
                        mm.then_inc(psum_ready.sem, 1)

                    def turn_v(b):
                        if b >= 2:
                            pe.wait_ge(gates_ready.sem, gates_ready.at(1))
                        pe.wait_ge(bank_free[1].sem, bank_free[1].at(2))
                        for h in range(H4):
                            mm = pe.transpose(bank[(6, 7, 4, 5)[b]][:, h * P:(h + 1) * P], GV[:, h, b * P:(b + 1) * P], ident)
                        mm.then_inc(vt_psum.sem, 1)

                    def turn_k():
                        pe.wait_ge(decay_ready.sem, decay_ready.at(3))
                        pe.wait_ge(vt_ready.sem, vt_ready.at(NB))
                        for b in range(NB):
                            for k in range(2):
                                to = 256 * (b % 2) + P * k
                                mm = pe.transpose(bank[4 + b // 2][:, to:to + P], K2[:, k, b * P:(b + 1) * P], ident)
                            if b % 2:
                                mm.then_inc(vt_psum.sem, 1)

                    def scores(bb):
                        if bb:
                            pe.wait_ge(masked.sem, masked.at(1))
                        for b in (2 * bb, 2 * bb + 1):
                            for h in range(H4):
                                f, k, tok = slice(64 * (h % 2), 64 * (h % 2) + 64), h // 2, slice(b * P, (b + 1) * P)
                                to = 256 * (b % 2) + P * k
                                mm = pe.matmul(bank[6 + h % 2][:, to:to + P], GK[f, k, tok], GQ[f, k, tok],
                                               start=True, stop=True)
                        mm.then_inc(score_ready.sem, 1)

                    def key_values(bb):
                        pe.wait_ge(vt_ready.sem, vt_ready.at(NB + 2))
                        if bb:
                            pe.wait_ge(masked.sem, masked.at(2))
                        for b in (2 * bb, 2 * bb + 1):
                            for c in range(2):
                                tok = slice(C * c, C * c + C)
                                for h in range(H4):
                                    f, k = slice(64 * (h % 2), 64 * (h % 2) + 64), h // 2
                                    src = 256 * (b % 2) + P * k + 64 * (h % 2)
                                    to = 256 * (b % 2) + P * k
                                    mm = pe.matmul(bank[4 + 2 * bb + c][f, to:to + P], K2T[tok, b // 2, src:src + 64],
                                                   VT[tok, b, h * P:(h + 1) * P], start=True, stop=True)
                        mm.then_inc(qk_ready.sem, 1)

                    def head(h):
                        pe.wait_ge(masked.sem, masked.at(2))
                        pe.wait_ge(state_ready.sem, state_ready.at(2 * NC))
                        f, k = slice(64 * (h % 2), 64 * (h % 2) + 64), h // 2
                        o = bank[4 + h]
                        for b in range(NB):
                            pe.matmul(o[:, b * P:(b + 1) * P], VT[:, b, h * P:(h + 1) * P],
                                      AT[:, b, h * P:(h + 1) * P], start=True, stop=False, skip_group_check=True)
                            for c in (2 * b, 2 * b + 1):
                                mm = pe.matmul(o[:, c * C:(c + 1) * C], ST[f, c, k * P:(k + 1) * P],
                                               GQ[f, k, c * C:(c + 1) * C], start=False, stop=c % 2 == 1,
                                               skip_group_check=True)
                        mm.then_inc(attended.sem, 1)

                    lead_tensor(pe, n0)
                    chunk(0, 1)
                    with pe.Fori(1, 3) as i:
                        for u in range(2):
                            chunk(i, u)
                    for j in range(6, n + 1):
                        if j == 6:
                            gates()
                            turn_v(0)
                            turn_v(1)
                        elif j == 7:
                            turn_v(2)
                            turn_v(3)
                        elif j == 9:
                            turn_k()
                            scores(0)
                        elif j == 10:
                            scores(1)
                            key_values(0)
                        elif j == 11:
                            key_values(1)
                        elif j == 12:
                            head(0)
                            head(1)
                        if j < n:
                            chunk(j // 2, j % 2)
                    head(2)
                    head(3)

                @block.scalar
                def _(act):
                    ch = Chain(act, act_chain)
                    split = ahead(split_hi, act, n0, n, 1)

                    def leave(j):
                        act.wait_ge(chunk_used.sem, PRIME + n0 + j + 1)
                        for v in range(2):
                            out, k = dest[2 * j + v]
                            b = bank[2 * (j % 2) + v]
                            if out is RK:
                                act.wait_ge(product_ready.sem, product_ready.at(1))
                            elif out is GD:
                                ins = act.activation(GD[:, :], b[0:16, :], ACT.Copy)
                            else:
                                ins = act.activation(out[:, k, :], b[:, :], ACT.Silu if out is GO else ACT.Copy)
                        ins.then_inc(bank_free[j % 2].sem, 1)

                    def copy_v(b):
                        act.wait_ge(vt_psum.sem, vt_psum.at(b + 1))
                        act.activation(VT[:, b, :], bank[(6, 7, 4, 5)[b]][:, :], ACT.Copy).then_inc(vt_ready.sem, 1)

                    def copy_head(h):
                        act.wait_ge(attended.sem, attended.at(h + 1))
                        act.activation(OG[:, h, :], bank[4 + h][:, :], ACT.Copy)

                    split(0, 0)
                    lead_scalar(act)
                    for j in range(n):
                        if j:
                            split(j // 2, j % 2)
                        if j <= 6:
                            leave(j)
                        if j == 5:
                            act.wait_ge(psum_ready.sem, psum_ready.at(1))
                            for k in range(2):
                                ins = act.activation(Z[:, k, :], bank[4 + k][:, :], ACT.Identity, bias=col("gla_gb", k))
                            ins.then_inc(gates_ready.sem, 1)
                            act.wait_ge(gates_ready.sem, gates_ready.at(1))
                            ch.add(act.activation(E1[:, :, :], Z[:, :, :], ACT.Abs))
                            ch.wait()
                            ch.add(act.activation(E1[:, :, :], E1[:, :, :], ACT.Exp, scale=-1.0))
                            ch.wait()
                            act.activation(E1[:, :, :], E1[:, :, :], ACT.Ln, bias=1.0).then_inc(gates_ready.sem, 1)
                            copy_v(0)
                            copy_v(1)
                        elif j == 6:
                            copy_v(2)
                            copy_v(3)
                        elif j == 7:
                            act.wait_ge(frame_ready.sem, frame_ready.at(1))
                            act.activation(E1[:, :, :], CUM[:, :, :], ACT.Exp, scale=tau).then_inc(gates_ready.sem, 1)
                            act.activation(E2[:, :, :], CUM[:, :, :], ACT.Exp, scale=-tau).then_inc(gates_ready.sem, 1)
                            act.activation(dec[:, :, :], CUM[:, :, C - 1::C], ACT.Exp, scale=tau)
                            act.wait_ge(frame_ready.sem, frame_ready.at(2))
                            act.activation(K2[:, :, :], Z[:, :, :], ACT.Exp, scale=tau).then_inc(gates_ready.sem, 1)
                        elif j == 8:
                            for m in range(2):
                                act.wait_ge(vt_psum.sem, vt_psum.at(NB + m + 1))
                                act.activation(K2T[:, m, :], bank[4 + m][:, :], ACT.Copy).then_inc(vt_ready.sem, 1)
                        elif j == 11:
                            copy_head(0)
                            copy_head(1)
                    copy_head(2)
                    copy_head(3)

                @block.vector
                def _(dve):
                    ch = Chain(dve, dve_chain)
                    split = ahead(split_lo, dve, n0, n, 1)
                    mu = cols[:, col_at["rk_mu"]:col_at["rk_mu"] + 13]
                    ka = cols[:, col_at["rk_k_a"]:col_at["rk_k_a"] + 4]
                    lead_vector(dve)
                    ch.add(dve.tensor_scalar(one_less[:, 0:13], mu, -1.0, 1.0, ALU.mult, ALU.add))
                    ch.add(dve.tensor_scalar(one_less[:, 13:17], ka, -1.0, 1.0, ALU.mult, ALU.add))
                    ch.wait()

                    def shift(j):
                        dve.wait_ge(chunk_used.sem, PRIME + n0 + j + 1)
                        for v in range(2):
                            out, k = dest[2 * j + v]
                            b = bank[2 * (j % 2) + v]
                            if out is not RK:
                                continue
                            ch.add(dve.tensor_scalar(RK[:, k, :], b[:, :], one_less[:, k:k + 1], None, ALU.mult))
                            ch.wait()
                            last = dve.scalar_tensor_tensor(
                                out=RK[:, k, 1:S], in0=b[:, 0:S - 1], scalar=col("rk_mu", k), in1=RK[:, k, 1:S],
                                op0=ALU.mult, op1=ALU.add)
                        last.then_inc((bank_free[j % 2] if j > 6 else product_ready).sem, 1)

                    def mask_scores(bb):
                        m = mask[:, :].bitcast(mybir.dt.uint32).unsqueeze(1).broadcast_to([P, 2, P])
                        dve.wait_ge(score_ready.sem, score_ready.at(bb + 1))
                        for b in (2 * bb, 2 * bb + 1):
                            for r in range(2):
                                src = bank[6 + r][:, 256 * (b % 2):256 * (b % 2) + 256]
                                ins = dve.copy_predicated(AT[:, b, :].rearrange("p (k r s) -> p k r s", k=2, r=2)[:, :, r, :],
                                                          m, src.rearrange("p (k s) -> p k s", k=2))
                        ins.then_inc(masked.sem, 1)

                    def states(bb):
                        dve.wait_ge(qk_ready.sem, qk_ready.at(bb + 1))
                        for c in range(4 * bb, 4 * bb + 4):
                            if c:
                                dve.wait_ge(state_ready.sem, state_ready.at(2 * c))
                            for k in range(2):
                                src = 256 * (c // 2 % 2) + P * k
                                dve.scalar_tensor_tensor(
                                    out=ST[:, c + 1, k * P:(k + 1) * P], in0=ST[:, c, k * P:(k + 1) * P],
                                    scalar=dec[:, k, c:c + 1], in1=bank[4 + 2 * bb + c % 2][:, src:src + P],
                                    op0=ALU.mult, op1=ALU.add).then_inc(state_ready.sem, 1)

                    for j in range(n):
                        split(j // 2, j % 2)
                        if j >= 6:
                            shift(j)
                        if j == 5:
                            dve.wait_ge(loads_done, loads.at(48))
                            dve.wait_ge(gates_ready.sem, gates_ready.at(2))
                            ch.add(dve.scalar_tensor_tensor(out=Z[:, :, :], in0=Z[:, :, :], scalar=0.0, in1=E1[:, :, :],
                                                            op0=ALU.min, op1=ALU.subtract))
                            ch.wait()
                            for k in range(2):
                                ins = dve.tensor_tensor_scan(CUM[:, k, :], reset[:, :], Z[:, k, :], 0.0, ALU.mult, ALU.add)
                            ins.then_inc(frame_ready.sem, 1)
                            dve.wait_ge(frame_ready.sem, frame_ready.at(1))
                            for k in range(2):
                                cum = CUM[:, k, :].rearrange("p (c s) -> p c s", s=C)
                                ins = dve.tensor_tensor(Z[:, k, :].rearrange("p (c s) -> p c s", s=C),
                                                        cum[:, :, C - 1:C].broadcast_to([P, NC, C]), cum, ALU.subtract)
                            ins.then_inc(frame_ready.sem, 1)
                        elif j == 7:
                            dve.wait_ge(gates_ready.sem, gates_ready.at(4))
                            dve.scalar_tensor_tensor(out=GQ[:, :, :], in0=GQ[:, :, :], scalar=0.125, in1=E1[:, :, :],
                                                     op0=ALU.mult, op1=ALU.mult).then_inc(decay_ready.sem, 1)
                            dve.wait_ge(gates_ready.sem, gates_ready.at(5))
                            dve.tensor_tensor(K2[:, :, :], K2[:, :, :], GK[:, :, :], ALU.mult).then_inc(decay_ready.sem, 1)
                            dve.wait_ge(decay_ready.sem, decay_ready.at(2))
                            dve.tensor_tensor(GK[:, :, :], E2[:, :, :], GK[:, :, :], ALU.mult).then_inc(decay_ready.sem, 1)
                            dve.wait_ge(vt_psum.sem, vt_psum.at(NB))
                            ch.add(dve.memset(AT[:, :, :], 0.0))
                            ch.add(dve.memset(ST[:, 0, :], 0.0))
                            ch.wait()
                        elif j == 8:
                            mask_scores(0)
                        elif j == 9:
                            mask_scores(1)
                            states(0)
                        elif j == 10:
                            states(1)

                @block.gpsimd
                def _(pool):
                    lead_pool(pool)
            loads.advance(48)
            end_stage(bank_free0=7, bank_free1=6, product_ready=1, psum_ready=1, vt_psum=NB + 2, decay_ready=3,
                      vt_ready=NB + 2, score_ready=2, qk_ready=2, masked=2, state_ready=2 * NC, attended=H4, act_chain=2,
                      gates_ready=5, frame_ready=2, dve_chain=2 + 13 + 3, **lead_counts())

        def rwkv(at, RK, one_less, OG, GO, lora, reset):
            C, NB, H8 = 32, S // P, 8
            NC = S // C
            kappa = float(np.exp(-0.5))
            ident = const["identity"]

            KD, BI = at(26, 4, S), at(34, 4, S)
            BV = at(42, 4, S)
            TT = at(50, C, 32)
            last = at(54, 4, NC)
            masks = at(54.25, 2 * P + C)
            strict, incl, low = masks[:, 0:P], masks[:, P:2 * P], masks[:, 2 * P:2 * P + C]
            rwkv_features(at, RK, one_less, KD, BI, BV, last, masks, kappa, lora, reset)
            rwkv_solve(at, KD, BI, TT, low, OG, GO)
            rwkv_chunks(at, RK, KD, BI, TT, last, strict, incl)
            rwkv_output(at, RK, KD, BV, lora)

        def rwkv_features(at, RK, one_less, KD, BI, BV, last, masks, kappa, lora, reset):
            C = 32
            A, CUM, SQ, CE = at(72, 4, S), at(80, 4, S), at(88, 2, S), at(92, 2, S)
            CP = BV
            LW, RN = BV, KD
            CI = CUM
            NORM_BANK = (2, 3, 6, 7)

            with nc.Block() as block:
                @block.sync
                def _(sp):
                    sp.wait_ge(loads_done, loads.at(32))
                    sp.dma_start(masks[:, 0:2 * P], t["masks"][:, 2 * S:2 * S + 2 * P]).then_inc(loads_done, 16)
                    sp.dma_start(masks[:, 2 * P:], t["masks"][:, 2 * S + 3 * P:]).then_inc(loads_done, 16)

                @block.tensor
                def _(pe):
                    def low_rank(k):
                        w = slice(k * P, (k + 1) * P)
                        pe.wait_ge(gates_ready.sem, gates_ready.at(k - 1))
                        pe.matmul(bank[4 * (k % 2)][:, :], lora[0:32, w], RK[0:32, 12, :], start=True, stop=True)
                        pe.matmul(bank[4 * (k % 2) + 1][:, :], lora[32:64, w], RK[32:64, 12, :], start=True, stop=True)\
                            .then_inc(psum_ready.sem, 1)

                    def key_norm(k):
                        pe.wait_ge(square_ready.sem, square_ready.at(k + 1))
                        pe.matmul(bank[NORM_BANK[k]][:, :], const["half_ones"], RN[:, k, :], start=True, stop=True)\
                            .then_inc(square_used.sem, 1)

                    def bonus(k):
                        pe.wait_ge(scaled.sem, scaled.at(k + 1))
                        pe.wait_ge(product_ready.sem, product_ready.at(k + 1))
                        pe.matmul(bank[NORM_BANK[k]][:, :], const["half_ones"], SQ[:, k % 2, :], start=True, stop=True)\
                            .then_inc(attended.sem, 1)

                    pe.wait_ge(loads_done, loads.at(32))
                    pe.wait_ge(rows_ready.sem, rows_ready.at(1))
                    for k in range(4):
                        low_rank(k)
                        key_norm(k)
                        if k >= 2:
                            bonus(k - 2)
                    bonus(2)
                    bonus(3)
                    pe.wait_ge(gates_ready.sem, gates_ready.at(4))
                    warm(pe, 0, 16)

                @block.scalar
                def _(act):
                    ch = Chain(act, act_chain)

                    def gates(k):
                        act.wait_ge(psum_ready.sem, psum_ready.at(k + 1))
                        act.activation(LW[:, k, :], bank[4 * (k % 2)][:, :], ACT.Sigmoid, bias=col("rk_w0", k))
                        act.activation(A[:, k, :], bank[4 * (k % 2) + 1][:, :], ACT.Sigmoid, bias=col("rk_a0", k))\
                            .then_inc(gates_ready.sem, 1)

                    def decays(k):
                        cum, cp = CUM[:, k, :], CP[:, k, :]
                        act.wait_ge(frame_ready.sem, frame_ready.at(k + 1))
                        act.wait_ge(r_scaled.sem, r_scaled.at(k - 1))
                        ch.add(act.activation(CE[:, k % 2, :], cum, ACT.Exp, scale=-kappa))
                        ch.add(act.activation(last[:, k, :], cum[:, C - 1::C], ACT.Exp, scale=-kappa))
                        act.activation(cp, cp, ACT.Exp, scale=-kappa)
                        ch.wait()
                        act.activation(cum, cum, ACT.Exp, scale=kappa).then_inc(decay_ready.sem, 1)

                    act.activation(RK[0:32, 12, :], RK[0:32, 12, :], ACT.Tanh).then_inc(rows_ready.sem, 1)
                    for k in range(4):
                        act.activation(RN[:, k, :], RK[:, 4 + k, :], ACT.Square, scale=col("rk_k_k", k))\
                            .then_inc(square_ready.sem, 1)
                        if k == 0:
                            act.activation(RK[64:P, 12, :], RK[64:P, 12, :], ACT.Sigmoid)
                        gates(k)
                    act.preload_act_table(ACT.Ln)
                    for k in range(4):
                        act.wait_ge(scaled.sem, scaled.at(k + 1))
                        act.activation(RN[:, k, :], RN[:, k, :], ACT.Ln).then_inc(scale_ready.sem, 1)
                    for k in range(4):
                        act.wait_ge(scale_ready.sem, scale_ready.at(k + 1))
                        act.activation(RN[:, k, :], RN[:, k, :], ACT.Exp, scale=-0.5).then_inc(scale_ready.sem, 1)
                        decays(k)

                @block.vector
                def _(dve):
                    ch = Chain(dve, dve_chain)

                    def early(k):
                        r, key, sq = RK[:, k, :], RK[:, 4 + k, :], SQ[:, k % 2, :]
                        dve.wait_ge(square_used.sem, square_used.at(k + 1))
                        dve.tensor_scalar(RN[:, k, :], bank[NORM_BANK[k]][:, :], 1e-24, None, ALU.max).then_inc(scaled.sem, 1)
                        ch.add(dve.tensor_scalar(BI[:, k, :], key, col("rk_k_k", k), None, ALU.mult))
                        dve.wait_ge(gates_ready.sem, gates_ready.at(k + 1))
                        ch.add(dve.tensor_tensor_scan(CUM[:, k, :], reset[:, :], LW[:, k, :], 0.0, ALU.mult, ALU.add))
                        summed = ch.n
                        dve.wait_ge(attended.sem, attended.at(k - 1))
                        ch.add(dve.tensor_scalar(sq, A[:, k, :], col("rk_k_a", k), one_less[:, 13 + k:14 + k], ALU.mult, ALU.add))
                        ch.wait(summed)
                        dve.tensor_tensor(CP[:, k, :], CUM[:, k, :], LW[:, k, :], ALU.subtract).then_inc(frame_ready.sem, 1)
                        ch.wait()
                        ch.add(dve.tensor_tensor(key, key, sq, ALU.mult))
                        ch.wait()
                        dve.scalar_tensor_tensor(out=sq, in0=r, scalar=col("rk_r_k", k), in1=key,
                                                 op0=ALU.mult, op1=ALU.mult).then_inc(product_ready.sem, 1)

                    def bonus(k):
                        dve.wait_ge(attended.sem, attended.at(k + 1))
                        dve.wait_ge(rest_ready.sem, rest_ready.at(k + 1))
                        dve.tensor_tensor(BV[:, k, :], bank[NORM_BANK[k]][:, :], RK[:, 8 + k, :], ALU.mult)

                    def keys(k):
                        dve.wait_ge(scale_ready.sem, scale_ready.at(4 + k + 1))
                        dve.wait_ge(product_ready.sem, product_ready.at(k + 1))
                        ch.add(dve.tensor_tensor(KD[:, k, :], RN[:, k, :], BI[:, k, :], ALU.mult))
                        ch.wait()
                        dve.tensor_tensor(BI[:, k, :], KD[:, k, :], A[:, k, :], ALU.mult).then_inc(h_ready.sem, 1)

                    def factors(k):
                        key, ci = RK[:, 4 + k, :], CI[:, k, :]
                        dve.wait_ge(decay_ready.sem, decay_ready.at(k + 1))
                        dve.tensor_tensor(key, key, ci, ALU.mult)
                        dve.wait_ge(h_ready.sem, h_ready.at(k + 1))
                        dve.tensor_tensor(BI[:, k, :], BI[:, k, :], ci, ALU.mult)

                    dve.wait_ge(loads_done, loads.at(32))
                    for k in range(4):
                        early(k)
                    for k in range(6):
                        if k < 4:
                            keys(k)
                        if 1 <= k < 5:
                            factors(k - 1)
                        if k >= 2:
                            bonus(k - 2)
                    dve.wait_ge(loads_done, loads.at(64))

                @block.gpsimd
                def _(pool):
                    for k in range(4):
                        r = RK[:, k, :]
                        pool.wait_ge(product_ready.sem, product_ready.at(k + 1))
                        pool.wait_ge(decay_ready.sem, decay_ready.at(k + 1))
                        pool.tensor_tensor(r, r, CE[:, k % 2, :], ALU.mult).then_inc(r_scaled.sem, 1)
                        pool.wait_ge(h_ready.sem, h_ready.at(k + 1))
                        pool.tensor_tensor(KD[:, k, :], KD[:, k, :], CP[:, k, :], ALU.mult).then_inc(rest_ready.sem, 1)
            loads.advance(64)
            end_stage(rows_ready=1, gates_ready=4, psum_ready=4, square_ready=4, square_used=4, product_ready=4,
                      attended=4, h_ready=4, scale_ready=8, scaled=4, frame_ready=4, decay_ready=4, r_scaled=4, rest_ready=4, dve_chain=4 * 5, act_chain=4 * 2)

        def rwkv_solve(at, KD, BI, TT, low, OG, GO):
            C, NB, H8 = 32, S // P, 8
            LT = at(72, 32, C)
            LS = at(76, C, C)
            T = at(80, C, C)
            prod = at(84, C * C)
            sq, rs = at(88, 2, S), at(92, 2, S)
            H4 = 4
            with nc.Block() as block:
                @block.tensor
                def _(pe):
                    for b in range(NB):
                        tok = slice(b * P, (b + 1) * P)
                        pe.wait_ge(masked.sem, masked.at(2 * b - 2))
                        for k in range(4):
                            for r in range(2):
                                f = slice(64 * r, 64 * r + 64)
                                mm = pe.matmul(bank[2 * (b % 2) + r][:, k * P:(k + 1) * P], KD[f, k, tok], BI[f, k, tok],
                                               start=True, stop=True)
                                if k == 3:
                                    mm.then_inc(score_ready.sem, 1)
                    for h in range(H4 + 1):
                        if h < H4:
                            pe.wait_ge(centred.sem, centred.at(h - 1))
                            pe.matmul(bank[4 + h % 2][:, :], const["centre_p"], OG[:, h, :], start=True, stop=True)\
                                .then_inc(mean_ready.sem, 1)
                        if h:
                            pe.wait_ge(square_ready.sem, square_ready.at(h))
                            pe.wait_ge(scale_ready.sem, scale_ready.at(2 * h - 4))
                            pe.matmul(bank[6 + (h - 1) % 2][:, :], const["mean_p"], sq[:, (h - 1) % 2, :], start=True, stop=True)\
                                .then_inc(square_used.sem, 1)
                    pe.wait_ge(masked.sem, masked.at(2 * NB))
                    warm(pe, 0, 27)

                @block.scalar
                def _(act):
                    def centre(h):
                        act.wait_ge(mean_ready.sem, mean_ready.at(h + 1))
                        act.wait_ge(square_used.sem, square_used.at(h - 1))
                        act.activation(sq[:, h % 2, :], bank[4 + h % 2][:, :], ACT.Square).then_inc(square_ready.sem, 1)
                        act.activation(OG[:, h, :], bank[4 + h % 2][:, :], ACT.Copy).then_inc(centred.sem, 1)

                    def factor(h):
                        r = rs[:, h % 2, :]
                        act.wait_ge(square_used.sem, square_used.at(h + 1))
                        act.wait_ge(y_ready.sem, y_ready.at(h - 1))
                        act.activation(r, bank[6 + h % 2][:, :], ACT.Ln, bias=col("eps_gla")).then_inc(scale_ready.sem, 1)
                        act.wait_ge(scale_ready.sem, scale_ready.at(2 * h + 1))
                        act.activation(r, r, ACT.Exp, scale=-0.5).then_inc(scale_ready.sem, 1)

                    def gain(h):
                        act.wait_ge(y_ready.sem, y_ready.at(h + 1))
                        act.activation(OG[:, h, :], OG[:, h, :], ACT.Copy, scale=col("gla_norm_g", h)).then_inc(h_ready.sem, 1)
                        act.wait_ge(h_ready.sem, h_ready.at(h + 1))
                        act.activation(x_hi[:, 4 + h, :], OG[:, h, :], ACT.Copy).then_inc(rounded.sem, 1)

                    for h in range(H4 + 2):
                        if h < H4:
                            centre(h)
                        if 1 <= h <= H4:
                            factor(h - 1)
                        if h >= 2:
                            gain(h - 2)

                @block.gpsimd
                def _(pool):
                    for h in range(H4 + 1):
                        if h < H4:
                            pool.wait_ge(scale_ready.sem, scale_ready.at(2 * h + 2))
                            pool.tensor_tensor(OG[:, h, :], OG[:, h, :], rs[:, h % 2, :], ALU.mult).then_inc(rest_ready.sem, 1)
                            pool.wait_ge(rest_ready.sem, rest_ready.at(h + 1))
                            pool.tensor_tensor(OG[:, h, :], OG[:, h, :], GO[:, h, :], ALU.mult).then_inc(y_ready.sem, 1)
                        if h:
                            pool.wait_ge(rounded.sem, rounded.at(h))
                            pool.tensor_tensor(x_lo[:, 3 + h, :], OG[:, h - 1, :], x_hi[:, 3 + h, :].bitcast(F32), ALU.subtract)

                @block.vector
                def _(dve):
                    ch = Chain(dve, dve_chain)
                    for g in range(2 * NB):
                        dve.wait_ge(score_ready.sem, score_ready.at(g + 1))
                        for c in range(4):
                            p = slice(C * c, C * c + C)
                            src = bank[g % 4][p, :].rearrange("p (h s) -> p h s", h=4)[:, :, C * c:C * c + C]
                            ins = dve.tensor_tensor(LT[p, 4 * g:4 * g + 4, :], src,
                                                    low[p, :].unsqueeze(1).broadcast_to([C, 4, C]), ALU.mult)
                        ins.then_inc(masked.sem, 1)
                    ch.add(dve.memset(T[:, :, :], 0.0))
                    ch.wait()
                    ch.add(dve.memset(T[:, :, :].rearrange("p s t -> p (s t)")[:, 0::C + 1], 1.0))
                    dve.wait_ge(masked.sem, masked.at(2 * NB))
                    ch.add(dve.transpose(LS[:, :, :], LT[:, :, :].rearrange("p h s -> p s h")))
                    ch.wait()
                    for i in range(1, C):
                        pr = prod[:, 0:i * i].rearrange("p (j s) -> p j s", s=i)
                        row = LS[:, 0:i, i:i + 1].rearrange("p s o -> p o s").broadcast_to([P, i, i])
                        ch.add(dve.tensor_tensor(pr, T[:, 0:i, 0:i], row, ALU.mult))
                        ch.wait()
                        ch.add(dve.tensor_reduce(T[:, 0:i, i:i + 1], pr, AX_X, ALU.add, negate=True))
                        ch.wait()
                    dve.transpose(TT[:, :, :], T[:, :, :].rearrange("p s t -> p t s"))
            end_stage(masked=2 * NB, score_ready=2 * NB, dve_chain=3 + 2 * (C - 1), mean_ready=H4, centred=H4,
                      square_ready=H4, square_used=H4, scale_ready=2 * H4, y_ready=H4, h_ready=H4, rounded=H4, rest_ready=H4)

        def rwkv_chunks(at, RK, KD, BI, TT, last, strict, incl):
            C, NB, H8 = 32, S // P, 8
            ident = const["identity"]
            M, A1, A2, BD = (at(56 + 4 * n, H8, P) for n in range(4))
            KDT, VT, BT, KT2, U, U1, SA = (at(72 + 2 * n, S) for n in range(7))
            B2, K2, W1 = (at(86 + 2 * n, 4, P) for n in range(3))
            ST = at(92, 5, 4 * 64)
            DS = at(97, 4 * 64)

            def heads(h):
                return slice(64 * (h // 4), 64 * (h // 4) + 64), h % 4

            def cells(h):
                at = P * (h % 4) + 64 * (h // 4)
                return slice(at, at + 64)

            with nc.Block() as block:
                @block.tensor
                def _(pe):
                    def scores(b, x):
                        tok = slice(b * P, (b + 1) * P)
                        lhs, lk, rhs, rk = ((RK, 4, KD, 0), (BI, 0, RK, 0), (RK, 4, RK, 0))[x]
                        for h in range(H8):
                            f, k = heads(h)
                            mm = pe.matmul(bank[2 * x + h // 4][:, (h % 4) * P:(h % 4) * P + P],
                                           lhs[f, lk + k, tok], rhs[f, rk + k, tok], start=True, stop=True)
                        mm.then_inc(score_ready.sem, 1)

                    def turn(b, x):
                        tok = slice(b * P, (b + 1) * P)
                        src = (lambda k: KD[:, k, tok], lambda k: B2[:, k, :], lambda k: K2[:, k, :], lambda k: RK[:, 8 + k, tok])[x]
                        if 1 <= x <= 2:
                            pe.wait_ge(decay_ready.sem, decay_ready.at(2 * b + x))
                        pe.wait_ge(vt_ready.sem, vt_ready.at(4 * b + x - 1))
                        for k in range(4):
                            mm = pe.transpose(bank[6 + x % 2][:, k * P:(k + 1) * P], src(k), ident)
                        mm.then_inc(vt_psum.sem, 1)

                    def before(b):
                        pe.wait_ge(h_ready.sem, h_ready.at(4 * b))
                        scores(b, 0)
                        for x in range(3):
                            turn(b, x)

                    def front(b):
                        turn(b, 3)
                        scores(b, 1)
                        pe.wait_ge(y_ready.sem, y_ready.at(b))
                        pe.wait_ge(state_ready.sem, state_ready.at(4 * b + 1))
                        scores(b, 2)
                        pe.wait_ge(masked.sem, masked.at(3 * b + 1))
                        pe.wait_ge(vt_ready.sem, vt_ready.at(4 * b + 4))
                        for h in range(H8):
                            mm = pe.matmul(bank[0][:, cells(h)], M[:, h, :], VT[:, cells(h)], start=True, stop=True)
                        mm.then_inc(attended.sem, 1)
                        pe.wait_ge(frame_ready.sem, frame_ready.at(b + 1))
                        for h in range(H8):
                            f, k = heads(h)
                            mm = pe.matmul(bank[1][f, k * P:(k + 1) * P], KDT[:, cells(h)], BD[:, h, :],
                                           start=True, stop=True)
                        mm.then_inc(attended.sem, 1)
                        pe.wait_ge(masked.sem, masked.at(3 * b + 2))
                        pe.wait_ge(u_ready.sem, u_ready.at(3 * b + 1))
                        for h in range(H8):
                            mm = pe.matmul(bank[2][:, cells(h)], BD[:, h, :], U[:, cells(h)], start=True, stop=True)
                        mm.then_inc(attended.sem, 1)
                        pe.wait_ge(u_ready.sem, u_ready.at(3 * b + 3))
                        pe.wait_ge(masked.sem, masked.at(3 * b + 3))

                    def steps(b):
                        for c in range(4):
                            g = 4 * b + c
                            p = slice(C * c, C * c + C)
                            pe.wait_ge(state_ready.sem, state_ready.at(g + 1))
                            for h in range(H8):
                                f, k = heads(h)
                                mm = pe.matmul(bank[3 - 3 * (h // 4)][p, k * 64:k * 64 + 64], W1[f, k, p],
                                               ST[f, g % 5, k * 64:k * 64 + 64], start=True, stop=True)
                            mm.then_inc(qk_ready.sem, 1)
                            for h in range(H8):
                                f, k = heads(h)
                                pe.matmul(bank[4][f, k * 64:k * 64 + 64], KT2[p, cells(h)], VT[p, cells(h)], start=k == 0,
                                          stop=False, skip_group_check=True)
                            pe.wait_ge(h_ready.sem, h_ready.at(g + 1))
                            for h in range(H8):
                                f, k = heads(h)
                                mm = pe.matmul(bank[4][f, k * 64:k * 64 + 64], BT[p, cells(h)], SA[p, cells(h)], start=False,
                                               stop=True, skip_group_check=True)
                            mm.then_inc(psum_ready.sem, 1)

                    def output(b):
                        for h in range(H8):
                            f, k = heads(h)
                            o = bank[5]
                            pe.matmul(o[f, k * P:(k + 1) * P], VT[:, cells(h)], A2[:, h, :], start=True, stop=False,
                                      skip_group_check=True)
                            pe.matmul(o[f, k * P:(k + 1) * P], SA[:, cells(h)], A1[:, h, :], start=False, stop=False,
                                      skip_group_check=True)
                            for c in range(4):
                                at_ = b * P + C * c
                                mm = pe.matmul(o[f, k * P + C * c:k * P + C * c + C],
                                               ST[f, (4 * b + c) % 5, k * 64:k * 64 + 64], RK[f, k, at_:at_ + C],
                                               start=False, stop=c == 3, skip_group_check=True)
                        mm.then_inc(pair_ready.sem, 1)

                    before(0)
                    for b in range(NB):
                        front(b)
                        steps(b)
                        if b + 1 < NB:
                            before(b + 1)
                        output(b)

                @block.scalar
                def _(act):
                    def turned(b, x):
                        out, bk = ((KDT, 6), (BT, 7), (KT2, 6), (VT, 7))[x]
                        act.wait_ge(vt_psum.sem, vt_psum.at(4 * b + x + 1))
                        act.activation(out[:, :], bank[bk][:, :], ACT.Copy).then_inc(vt_ready.sem, 1)

                    for b in range(NB):
                        for x in range(3 if b else 4):
                            turned(b, x)
                        if b:
                            act.wait_ge(pair_ready.sem, pair_ready.at(b))
                            act.activation(KD[:, :, (b - 1) * P:b * P], bank[5][:, :].rearrange("p (k t) -> p k t", k=4),
                                           ACT.Copy).then_inc(y_ready.sem, 1)
                            turned(b, 3)
                        for x, (out, bk) in enumerate(((U[:, :], 0), (W1[:, :, :], 1), (U1[:, :], 2))):
                            act.wait_ge(attended.sem, attended.at(3 * b + x + 1))
                            src = bank[bk][:, :]
                            if bk == 1:
                                src = src.rearrange("p (k t) -> p k t", k=4)
                            act.activation(out, src, ACT.Copy).then_inc(u_ready.sem, 1)
                    act.wait_ge(pair_ready.sem, pair_ready.at(NB))
                    act.activation(KD[:, :, (NB - 1) * P:], bank[5][:, :].rearrange("p (k t) -> p k t", k=4),
                                   ACT.Copy).then_inc(y_ready.sem, 1)

                @block.gpsimd
                def _(pool):
                    pool.memset(BD[:, :, :], 0.0).then_inc(pool_zero.sem, 1)
                    def ends(b):
                        tok = slice(b * P, (b + 1) * P)
                        if b:
                            pool.wait_ge(vt_psum.sem, vt_psum.at(4 * b - 1))
                        for out, src, off in ((B2, BI, 0), (K2, RK, 4)):
                            for k in range(4):
                                o = out[:, k, :].rearrange("p (c s) -> p c s", s=C)
                                i = src[:, off + k, tok].rearrange("p (c s) -> p c s", s=C)
                                e = last[:, k, 4 * b:4 * b + 4].unsqueeze(2).broadcast_to([P, 4, C])
                                ins = pool.tensor_tensor(o, i, e, ALU.mult)
                            ins.then_inc(decay_ready.sem, 1)

                    ends(0)
                    for b in range(NB):
                        if b + 1 < NB:
                            ends(b + 1)
                        for c in range(4):
                            g = 4 * b + c
                            pool.wait_ge(state_ready.sem, state_ready.at(g + 1))
                            e = last[:, :, g:g + 1].broadcast_to([P, 4, 64])
                            pool.tensor_tensor(DS[:, :].rearrange("p (k i) -> p k i", k=4),
                                               ST[:, g % 5, :].rearrange("p (k i) -> p k i", k=4), e, ALU.mult)\
                                .then_inc(rest_ready.sem, 1)

                @block.vector
                def _(dve):
                    dve.memset(ST[:, 0, :], 0.0).then_inc(state_ready.sem, 1)
                    dve.wait_ge(pool_zero.sem, pool_zero.at(1))
                    def mask_scores(b, x):
                        out, m = ((M, strict), (A1, incl), (A2, incl))[x]
                        dve.wait_ge(score_ready.sem, score_ready.at(3 * b + x + 1))
                        for v in range(2):
                            ins = dve.tensor_tensor(out[:, 4 * v:4 * v + 4, :],
                                                    bank[2 * x + v][:, :].rearrange("p (h t) -> p h t", h=4),
                                                    m.unsqueeze(1).broadcast_to([P, 4, P]), ALU.mult)
                        ins.then_inc(masked.sem, 1)

                    for b in range(NB):
                        for c in range(4):
                            p = slice(C * c, C * c + C)
                            ins = dve.tensor_copy(BD[p, :, p],
                                                  TT[p, :, 8 * b:8 * b + 8].rearrange("p t h -> p h t"))
                        ins.then_inc(frame_ready.sem, 1)
                        mask_scores(b, 0)
                        if b:
                            dve.wait_ge(pair_ready.sem, pair_ready.at(b))
                        mask_scores(b, 1)
                        mask_scores(b, 2)
                        dve.wait_ge(u_ready.sem, u_ready.at(3 * b + 3))
                        for c in range(4):
                            g = 4 * b + c
                            p = slice(C * c, C * c + C)
                            dve.wait_ge(qk_ready.sem, qk_ready.at(g + 1))
                            for r in range(2):
                                out, u1 = (a[p, :].rearrange("p (k r i) -> p k r i", k=4, r=2)[:, :, r, :] for a in (SA, U1))
                                ins = dve.scalar_tensor_tensor(
                                    out=out, in0=bank[3 - 3 * r][p, 0:256].rearrange("p (k i) -> p k i", k=4),
                                    scalar=-1.0, in1=u1, op0=ALU.mult, op1=ALU.subtract)
                            ins.then_inc(h_ready.sem, 1)
                            dve.wait_ge(psum_ready.sem, psum_ready.at(g + 1))
                            dve.wait_ge(rest_ready.sem, rest_ready.at(g + 1))
                            dve.tensor_tensor(ST[:, (g + 1) % 5, :], bank[4][:, 0:256], DS[:, :], ALU.add)\
                                .then_inc(state_ready.sem, 1)
            end_stage(y_ready=NB, score_ready=3 * NB, vt_psum=4 * NB, decay_ready=2 * NB, vt_ready=4 * NB,
                      masked=3 * NB, attended=3 * NB, frame_ready=NB, u_ready=3 * NB, state_ready=4 * NB + 1,
                      qk_ready=4 * NB, h_ready=4 * NB, psum_ready=4 * NB, pair_ready=NB, pool_zero=1,
                      rest_ready=4 * NB)

        def rwkv_output(at, RK, Y, BV, lora):
            sq, rs = at(56, 4, S), at(64, 4, S)
            with nc.Block() as block:
                @block.tensor
                def _(pe):
                    for k in range(4):
                        pe.matmul(bank[4 + k][:, :], const["half_mean"], Y[:, k, :], start=True, stop=True)\
                            .then_inc(mean_ready.sem, 1)
                    for k in range(4):
                        pe.matmul(bank[k][:, :], lora[64:P, k * P:(k + 1) * P], RK[64:P, 12, :], start=True, stop=True)\
                            .then_inc(gates_ready.sem, 1)
                        pe.wait_ge(square_ready.sem, square_ready.at(k + 1))
                        pe.matmul(bank[4 + k][:, :], const["half_mean"], sq[:, k, :], start=True, stop=True)\
                            .then_inc(square_used.sem, 1)

                @block.scalar
                def _(act):
                    for k in range(4):
                        act.wait_ge(centred.sem, centred.at(k + 1))
                        act.activation(sq[:, k, :], Y[:, k, :], ACT.Square).then_inc(square_ready.sem, 1)
                    for k in range(4):
                        act.wait_ge(square_used.sem, square_used.at(k + 1))
                        act.activation(rs[:, k, :], bank[4 + k][:, :], ACT.Ln, bias=col("eps_rk")).then_inc(scale_ready.sem, 1)
                    for k in range(4):
                        act.wait_ge(scale_ready.sem, scale_ready.at(k + 1))
                        act.activation(rs[:, k, :], rs[:, k, :], ACT.Exp, scale=-0.5).then_inc(scale_ready.sem, 1)
                    for k in range(4):
                        act.wait_ge(y_ready.sem, y_ready.at(k + 1))
                        act.activation(x_hi[:, k, :], Y[:, k, :], ACT.Copy).then_inc(rounded.sem, 1)

                @block.vector
                def _(dve):
                    ch = Chain(dve, dve_chain)
                    for k in range(4):
                        y = Y[:, k, :]
                        dve.wait_ge(mean_ready.sem, mean_ready.at(k + 1))
                        dve.tensor_tensor(y, y, bank[4 + k][:, :], ALU.subtract).then_inc(centred.sem, 1)
                    for k in range(4):
                        y = Y[:, k, :]
                        dve.wait_ge(square_ready.sem, square_ready.at(k + 1))
                        dve.wait_ge(scale_ready.sem, scale_ready.at(4 + k + 1))
                        ch.add(dve.scalar_tensor_tensor(out=y, in0=y, scalar=col("rk_ln_g", k), in1=rs[:, k, :],
                                                        op0=ALU.mult, op1=ALU.mult))
                        ch.wait()
                        ch.add(dve.scalar_tensor_tensor(out=y, in0=y, scalar=col("rk_ln_b", k), in1=BV[:, k, :],
                                                        op0=ALU.add, op1=ALU.add))
                        ch.wait()
                        dve.wait_ge(gates_ready.sem, gates_ready.at(k + 1))
                        dve.tensor_tensor(y, y, bank[k][:, :], ALU.mult).then_inc(y_ready.sem, 1)

                @block.gpsimd
                def _(pool):
                    for k in range(4):
                        pool.wait_ge(rounded.sem, rounded.at(k + 1))
                        pool.tensor_tensor(x_lo[:, k, :], Y[:, k, :], x_hi[:, k, :].bitcast(F32), ALU.subtract)
            end_stage(mean_ready=4, gates_ready=4, square_ready=4, square_used=4, centred=4, scale_ready=8, y_ready=4, rounded=4,
                      dve_chain=8)


        sum_tile, FACTOR = stats[:, 0, :], stats[:, 1, :]

        def start_vector(dve, work, post, acc):
            last = {"ln": 1}.get(post[0], 0)
            SUM = 4 + last
            for n in range(KT + (SUM if acc is not None else 1)):
                if n < KT:
                    if post[0] == "ln":
                        dve.tensor_tensor(X[:, n, :], X[:, n, :], stats[:, 0, :], ALU.mult).then_inc(lead_scaled.sem, 1)
                    else:
                        dve.scalar_tensor_tensor(out=work[:, n, :], in0=work[:, n, :], scalar=col(post[0], post[1] * KT + n),
                                                 in1=FACTOR, op0=ALU.mult, op1=ALU.mult).then_inc(y_ready.sem, 1)
                if 1 <= n <= KT:
                    k = n - 1
                    if post[0] == "ln":
                        dve.wait_ge(lead_scaled.sem, lead_scaled.at(k + 1))
                        dve.tensor_tensor(X[:, k, :], X[:, k, :], stats[:, 1, :], ALU.subtract).then_inc(lead_shifted.sem, 1)
                    else:
                        dve.wait_ge(y_ready.sem, y_ready.at(k + 1))
                        dve.tensor_tensor(X[:, k, :], X[:, k, :], work[:, k, :], ALU.add).then_inc(x_ready.sem, 1)
                k = n - SUM
                if k >= 1 and acc is not None:
                    dve.wait_ge(square_ready.sem, square_ready.at(k + 1))
                    dve.wait_ge(square_used.sem, square_used.at(k - 1))
                    dve.tensor_tensor(acc, acc, work[:, k - 1, :], ALU.add).then_inc(square_used.sem, 1)

        def start_scalar(act, work, post, acc, gain, l):
            for k in range(KT + 1):
                if k < KT:
                    if post[0] == "ln":
                        lead_gain(act, k)
                    else:
                        act.wait_ge(x_ready.sem, x_ready.at(k + 1))
                    act.activation(work[:, k, :], X[:, k, :], ACT.Copy, scale=col(gain, l * KT + k)).then_inc(scaled.sem, 1)
                if k:
                    if k > 1:
                        act.wait_ge(split_ready.sem, split_ready.at(k - 1))
                    act.activation(work[:, k - 2, :] if k > 1 else acc, X[:, k - 1, :], ACT.Square)\
                        .then_inc(square_ready.sem, 1)
                if k < KT:
                    act.wait_ge(scaled.sem, scaled.at(k + 1))
                    act.activation(x_hi[:, k, :], work[:, k, :], ACT.Copy).then_inc(rounded.sem, 1)

        def start_pool(pool, work):
            for k in range(KT):
                pool.wait_ge(rounded.sem, rounded.at(k + 1))
                pool.tensor_tensor(x_lo[:, k, :], work[:, k, :], x_hi[:, k, :].bitcast(F32),
                                   ALU.subtract).then_inc(split_ready.sem, 1)

        def start_tensor(pe, acc, n0):
            lead_tensor(pe, n0)
            pe.wait_ge(square_used.sem, square_used.at(KT - 1))
            pe.matmul(bank[7][:, :], const["mean_d"], acc, start=True, stop=True).then_inc(mean_ready.sem, 1)

        def factor_scalar(act, out, mean, n=1):
            act.preload_act_table_set(LOG_EXP)
            act.wait_ge(mean_ready.sem, mean_ready.at(n))
            act.activation(out, mean, ACT.Ln, bias=col("eps_rms")).then_inc(scale_ready.sem, 1)
            act.wait_ge(scale_ready.sem, scale_ready.at(2 * n - 1))
            act.activation(out, out, ACT.Exp, scale=-0.5).then_inc(scale_ready.sem, 1)

        def start_counts(post):
            first = dict(lead_scaled=KT, lead_shifted=KT) if post[0] == "ln" else dict(y_ready=KT)
            return dict(x_ready=KT, scaled=KT, rounded=KT, split_ready=KT, square_ready=KT, square_used=KT - 1,
                        mean_ready=1, scale_ready=2, **first)

        def finish_scalar(act, work, n, b, after=0):
            if n:
                act.wait_ge(square_used.sem, square_used.at(after * (KT - 1) + n - 1))
            act.activation(FACTOR if n else sum_tile, b[:, :], ACT.Square).then_inc(square_ready.sem, 1)
            act.activation(work[:, n, :], b[:, :], ACT.Copy).then_inc(z_ready.sem, 1)

        def finish_pool(pool, work, after=0):
            for n in range(1, KT - 1):
                pool.wait_ge(square_ready.sem, square_ready.at(after * KT + n + 1))
                pool.wait_ge(square_used.sem, square_used.at(after * (KT - 1) + n - 1))
                pool.tensor_tensor(sum_tile, sum_tile, FACTOR,
                                   ALU.add).then_inc(square_used.sem, 1)

        def finish_tensor(pe, work, after=0):
            pe.wait_ge(square_used.sem, square_used.at(after * (KT - 1) + KT - 2))
            pe.matmul(bank[7][:, :], const["mean_d"], sum_tile, start=True, stop=False)
            pe.wait_ge(square_ready.sem, square_ready.at(after * KT + KT))
            pe.matmul(bank[7][:, :], const["mean_d"], FACTOR, start=False, stop=True)\
                .then_inc(mean_ready.sem, 1)

        FINISH = dict(square_ready=KT, square_used=KT - 2, z_ready=KT, mean_ready=1, scale_ready=2)


        QA, KA, QB, KB, QM, VALUES_A, VALUES_B = 0, 3, 6, 9, 12, 14, 17
        M = 256
        SCALE = 64.0 ** -0.5

        def attention(l, work, post):
            n0 = c_next[0]
            NQ, NKV = 10, 2
            outer = ExitStack()
            with outer:
                o_hi = sb(f"o{l}_hi", [P, 6, S], F32R, outer)
                o_lo = sb(f"o{l}_lo", [P, 6, S], F32R, outer)
                factor = sb(f"a{l}_factor", [P, S], F32, outer)
                inner = ExitStack()
                with inner:
                    KM = sb(f"a{l}_km", [P, 2, M], F32, inner)
                    VM = sb(f"a{l}_vm", [P, 2, M], F32, inner)
                    Q = sb(f"a{l}_qkv", [P, 20, S], F32, inner)
                    c_next[0] = n0 + NQ + NKV
                    project_qkv(l, n0, NQ, NKV, Q, KM, VM, o_hi, o_lo, work, factor, post)
                    attend(l, Q, KM, VM, o_hi, o_lo, work)
                gated_merge(l, o_hi, o_lo, work, factor)

        def project_qkv(l, n0, n, nkv, Q, KM, VM, o_hi, o_lo, work, factor, post):
            with ExitStack() as scope:
                mem = sb(f"m{l}_mem", [P, KT, M], F32, scope)
                msq = sb(f"m{l}_squares", [P, KT, M], F32, scope)
                mfac = sb(f"m{l}_factor", [P, M], F32, scope)
                m_hi, m_lo = (o[:, :, :].rearrange("p a (b m) -> p (a b) m", m=M) for o in (o_hi, o_lo))
                vf = mem[:, 0:2, :]
                hi, lo = x_parts()
                acc = factor[:, :]
                by_column = [*range(QA, QA + 3), *range(KA, KA + 3), *range(VALUES_A, VALUES_A + 3)]
                SUM, APPLY = 7, 8

                with nc.Block() as block:
                    @block.sync
                    def _(sp):
                        sp.dma_start(mem[:, :, :], t["mem"]).then_inc(loads_done, 16)
                        for j in range(n + nkv):
                            ahead(fetch, sp, n0, n + nkv, 2)(j // 2, j % 2)

                    @block.tensor
                    def _(pe):
                        def chunk(i, u):
                            s = (n0 + u) % 2
                            pe.wait_ge(lo_ready.sem, i * 2 + (PRIME + n0 + u + 1))
                            pe.wait_ge(bank_free[u].sem, bank_free[u].at(0) + i)
                            linear(pe, bank[2 * u][:, :], s, 0, range(KT), hi, lo)
                            linear(pe, bank[2 * u + 1][:, :], s, KT * P, range(KT), hi, lo).then_inc(chunk_used.sem, 1)

                        start_tensor(pe, acc, n0)
                        chunk(0, 1)
                        with pe.Fori(1, SUM // 2 + 1) as i:
                            chunk(i, 0)
                            chunk(i, 1)
                        pe.wait_ge(part_ready.sem, part_ready.at(KT - 1))
                        pe.matmul(bank[7][:, 0:M], const["mean_d"], msq[:, 0, :], start=True, stop=True)\
                            .then_inc(mean_ready.sem, 1)
                        for j in range(SUM + 1, n):
                            chunk(j // 2, j % 2)
                        pe.wait_ge(part_free.sem, part_free.at(KT))
                        for j in range(nkv):
                            c = n0 + n + j
                            pe.wait_ge(lo_ready.sem, PRIME + c + 1)
                            for k in range(2):
                                mm = linear(pe, bank[4 + j][:, k * M:(k + 1) * M], c % 2, k * KT * P, range(KT),
                                            lambda i: m_hi[:, i, :], lambda i: m_lo[:, i, :])
                            mm.then_inc(chunk_used.sem, 1)
                        pe.wait_ge(vt_ready.sem, vt_ready.at(1))
                        for m in range(2):
                            for k in range(2):
                                mm = pe.transpose(bank[6][:, m * M + k * P:m * M + (k + 1) * P],
                                                  vf[:, k, m * P:(m + 1) * P], const["identity"])
                        mm.then_inc(vt_psum.sem, 1)

                    @block.scalar
                    def _(act):
                        split = ahead(split_hi, act, n0, n + nkv, 1)
                        split(0, 0)
                        start_scalar(act, work, post, acc, "g_pre_mix_2", l)
                        for j in range(n + nkv):
                            if j:
                                split(j // 2, j % 2)
                            if j == 0:
                                factor_scalar(act, factor[:, :], bank[7][:, :])
                                act.wait_ge(loads_done, loads.at(16))
                            elif j <= KT // 2:
                                for k in range(2 * j - 2, 2 * j):
                                    act.activation(msq[:, k, :], mem[:, k, :], ACT.Square).then_inc(weight_arg.sem, 1)
                            elif j == APPLY - 1:
                                factor_scalar(act, mfac[:, :], bank[7][:, 0:M], 2)
                            elif j == APPLY:
                                for k in range(KT):
                                    act.wait_ge(weight_ready.sem, weight_ready.at(k + 1))
                                    act.activation(m_hi[:, k, :], msq[:, k, :], ACT.Copy).then_inc(floor_ready.sem, 1)
                            elif j >= n:
                                act.wait_ge(chunk_used.sem, PRIME + n0 + j + 1)
                                ins = act.activation((KM, vf)[j - n][:, :, :],
                                                     bank[4 + j - n][:, :].rearrange("p (k m) -> p k m", k=2), ACT.Copy)
                        ins.then_inc(vt_ready.sem, 1)
                        act.wait_ge(vt_psum.sem, vt_psum.at(1))
                        act.activation(VM[:, :, :], bank[6][:, :].rearrange("p (m f) -> p m f", m=2), ACT.Copy)

                    @block.vector
                    def _(dve):
                        split = ahead(split_lo, dve, n0, n + nkv, 1)
                        start_vector(dve, work, post, acc)
                        for j in range(n + nkv):
                            split(j // 2, j % 2)
                            if j == 0:
                                dve.wait_ge(scale_ready.sem, scale_ready.at(2))
                            if j < n:
                                dve.wait_ge(chunk_used.sem, PRIME + n0 + j + 1)
                                for v in range(2):
                                    out, b, f = Q[:, 2 * j + v, :], bank[2 * (j % 2) + v][:, :], factor[:, :]
                                    if 2 * j + v in by_column:
                                        out = out.rearrange("p (c r) -> p r c", r=8)
                                        b, f = (ap.rearrange("p (r c) -> p r c", r=8) for ap in (b, f))
                                    ins = dve.tensor_tensor(out, b, f, ALU.mult)
                                ins.then_inc(bank_free[j % 2].sem, 1)
                            if j == APPLY - 1:
                                dve.wait_ge(scale_ready.sem, scale_ready.at(4))
                                for k in range(KT):
                                    dve.scalar_tensor_tensor(out=msq[:, k, :], in0=mem[:, k, :], scalar=col("mem_norm_g_2", k),
                                                             in1=mfac[:, :], op0=ALU.mult, op1=ALU.mult)\
                                        .then_inc(weight_ready.sem, 1)

                    @block.gpsimd
                    def _(pool):
                        start_pool(pool, work)
                        for k in range(1, KT):
                            pool.wait_ge(weight_arg.sem, weight_arg.at(k + 1))
                            pool.wait_ge(part_ready.sem, part_ready.at(k - 1))
                            pool.tensor_tensor(msq[:, 0, :], msq[:, 0, :], msq[:, k, :], ALU.add).then_inc(part_ready.sem, 1)
                        for k in range(KT):
                            pool.wait_ge(floor_ready.sem, floor_ready.at(k + 1))
                            pool.tensor_tensor(m_lo[:, k, :], msq[:, k, :], m_hi[:, k, :].bitcast(F32),
                                               ALU.subtract).then_inc(part_free.sem, 1)
                loads.advance(16)
                counts = start_counts(post)
                counts["mean_ready"] += 1
                counts["scale_ready"] += 2
                end_stage(bank_free0=(n + 1) // 2, bank_free1=n // 2, weight_arg=KT, part_ready=KT - 1, weight_ready=KT,
                          floor_ready=KT, part_free=KT, vt_ready=1, vt_psum=1, **counts)

        def attend(l, Q, KM, VM, o_hi, o_lo, work):
            items = []
            for hh in range(2):
                items += [("n", hh, r) for r in range(4)] + [("d", hh, 1), ("d", hh, 2)]
            items += [("a", h, b) for h in range(6) for b in range(2)]
            items += [("m", h, b) for h in range(4) for b in range(2)]
            NI, NB, NA = len(items), 12, 12
            parts = {"a": 2, "m": 2, "n": 1, "d": 4}
            biased = range(NB + NA)
            first_col = (0, 8, 24, 32)
            ident = const["identity"]
            RING = 3
            finals = {NB + 1: 3, 17: 0, 21: 1, 25: 2, 29: 4, NI + 1: 5}
            turned = (7, 4, 5, 2, 3, 0, 1, 6, 7)
            final_no = {k: n for n, k in enumerate(finals.values())}

            with ExitStack() as scope:
                VB = sb(f"t{l}_vb", [P, 3, 4, P], F32, scope)
                VA = sb(f"t{l}_va", [P, 8, 384], F32, scope)
                O = Q[:, VALUES_A:VALUES_A + 5, :].rearrange("p a b -> p (a b)").rearrange("p (t f) -> p t f", f=640)
                OB = Q[:, VALUES_B + 2, :].rearrange("p (r f) -> p r f", r=4)
                SC, PT, bias = work[:, 0:3, :], work[:, 3:5, :], work[:, 5:8, :]
                groups = stats[:, :, :].rearrange("p a b -> p (a b)")[:, 0:768].rearrange("p (g f) -> p g f", f=64)
                small = stats[:, :, :].rearrange("p a b -> p (a b)")[:, 768:928]

                def rows(h):
                    return slice(64 * (h % 2), 64 * (h % 2) + 64)

                def sums_of(x):
                    kind, h, y = items[x]
                    G = parts[kind]
                    if x < NB:
                        at = 48 * h + (y if kind == "n" else 4 * y)
                        return small[:, at:at + G], small[:, at + 12:at + 12 + G]
                    at = 96 + 8 * (x % 4)
                    return small[:, at:at + G], small[:, at + 2:at + 2 + G]

                with nc.Block() as block:
                    @block.sync
                    def _(sp):
                        for x in biased:
                            kind, h, y = items[x]
                            if x >= RING:
                                sp.wait_ge(score_ready.sem, score_ready.at(x - RING + 1))
                            src = t["rpb"][l, h, y] if kind == "a" else t["dilated"][x]
                            sp.dma_start(bias[:, x % RING, :], src).then_inc(bias_loaded[x % RING].sem, 16)

                    @block.tensor
                    def _(pe):
                        def turn_values(n):
                            if n == 8:
                                pe.wait_ge(vt_ready.sem, vt_ready.at(1))
                            for j in range(4):
                                if n < 3:
                                    src = Q[:, VALUES_B, j * P:(j + 1) * P] if n == 0 else Q[:, VALUES_B + n, j::4]
                                else:
                                    tt = 4 * ((n - 3) % 2) + j
                                    at = 8 * first_col[tt // 2] + P * (tt % 2)
                                    src = Q[:, VALUES_A + (n - 3) // 2, at:at + P]
                                mm = pe.transpose(bank[turned[n]][:, j * P:(j + 1) * P], src, ident)
                            mm.then_inc(vt_psum.sem, 1)

                        def scores(x):
                            kind, h, y = items[x]
                            b, f = bank[(0, 1, 6)[x % 3]], rows(h)
                            if x < 3:
                                pe.wait_ge(vt_ready.sem, vt_ready.at(6 + x))
                            else:
                                pe.wait_ge(score_ready.sem, score_ready.at(x - 2))
                            if kind == "n":
                                mm = pe.matmul(b[:, :], Q[f, QB, y::4], Q[f, KB, :], start=True, stop=True)
                            elif kind == "d":
                                for r in range(4):
                                    mm = pe.matmul(b[:, r * P:(r + 1) * P], Q[f, QB + y, r::4], Q[f, KB + y, r::4],
                                                   start=True, stop=True)
                            elif kind == "a":
                                for v in range(2):
                                    n = 2 * y + v
                                    k = 8 * first_col[n]
                                    mm = pe.matmul(b[:, v * 256:(v + 1) * 256], Q[f, QA + h // 2, n * P:(n + 1) * P],
                                                   Q[f, KA + h // 2, k:k + 256], start=True, stop=True)
                            else:
                                for v in range(2):
                                    q = (2 * y + v) * P
                                    mm = pe.matmul(b[:, v * M:(v + 1) * M], Q[f, QM + h // 2, q:q + P], KM[f, h // 2, :],
                                                   start=True, stop=True)
                            mm.then_inc(psum_ready.sem, 1)

                        def turn(x):
                            pe.wait_ge(weight_ready.sem, weight_ready.at(x + 1))
                            pe.wait_ge(u_ready.sem, u_ready.at(x - 1))
                            for j in range(4):
                                mm = pe.transpose(bank[2 + x % 2][:, j * P:(j + 1) * P], SC[:, x % RING, j * P:(j + 1) * P], ident)
                            mm.then_inc(masked.sem, 1)

                        def values(x):
                            kind, h, y = items[x]
                            pe.wait_ge(u_ready.sem, u_ready.at(x + 1))
                            pe.wait_ge(vt_ready.sem, vt_ready.at(9))
                            pe.wait_ge(h_ready.sem, h_ready.at(x - 1))
                            o, p = bank[4 + x % 2], lambda j: PT[:, x % 2, j * P:(j + 1) * P]
                            at = 64 * h
                            for j in range(4):
                                if kind == "n":
                                    out, v, first, last = 0, VB[:, 0, j, at:at + 64], j == 0, j == 3
                                elif kind == "d":
                                    out, v, first, last = j, VB[:, y, j, at:at + 64], True, True
                                else:
                                    src = VA[:, 4 * y + j, :] if kind == "a" else VM[:, j % 2, :]
                                    out, v, first, last = j // 2, src[:, at:at + 64], j % 2 == 0, j % 2 == 1
                                mm = pe.matmul(o[:, 64 * out:64 * out + 64], p(j), v, start=first, stop=last)
                            mm.then_inc(attended.sem, 1)

                        def final(k):
                            pe.wait_ge(z_ready.sem, z_ready.at(final_no[k]))
                            if k == 3:
                                pe.wait_ge(y_ready.sem, y_ready.at(2))
                            else:
                                x = NB + 4 * k + 3 if k < 3 else NB + NA + 4 * (k - 4) + 3
                                pe.wait_ge(h_ready.sem, h_ready.at(x + 1))
                            for n in range(4):
                                if k == 3:
                                    out, src = bank[7][:, n::4], OB[:, n, :]
                                elif k < 3:
                                    out = bank[7][:, :].rearrange("p (r c) -> p c r", r=8)[:, 16 * n:16 * n + 16, :]
                                    src = O[:, n, k * P:(k + 1) * P]
                                else:
                                    out, src = bank[7][:, n * P:(n + 1) * P], O[:, n, (k - 1) * P:k * P]
                                mm = pe.transpose(out, src, ident)
                            mm.then_inc(pair_ready.sem, 1)

                        for n in range(9):
                            turn_values(n)
                        for x in range(-2, NI + 2):
                            if x + 2 < NI:
                                scores(x + 2)
                            if 0 <= x < NI:
                                turn(x)
                            if 0 <= x - 1 < NI:
                                values(x - 1)
                            if x in finals:
                                final(finals[x])

                    @block.scalar
                    def _(act):
                        def bank_copy(n):
                            act.wait_ge(vt_psum.sem, vt_psum.at(n + 1))
                            src = bank[turned[n]][:, :].rearrange("p (j f) -> p j f", j=4)
                            f = n - 3
                            out = VB[:, n, :, :] if n < 3 else VA[:, 4 * (f % 2):4 * (f % 2) + 4, f // 2 * P:(f // 2 + 1) * P]
                            act.activation(out, src, ACT.Copy).then_inc(vt_ready.sem, 1)

                        def exps(x):
                            G = parts[items[x][0]]
                            w = S // G
                            neg, den = sums_of(x)
                            act.wait_ge(frame_ready.sem, frame_ready.at(x + 1))
                            for g in range(G):
                                sc = SC[:, x % RING, g * w:(g + 1) * w]
                                ins = act.activation(sc, sc, ACT.Exp, bias=neg[:, g:g + 1], accum_out=den[:, g:g + 1])
                            ins.then_inc(weight_ready.sem, 1)

                        def copy(x):
                            act.wait_ge(masked.sem, masked.at(x + 1))
                            act.wait_ge(attended.sem, attended.at(x - 1))
                            act.activation(PT[:, x % 2, :], bank[2 + x % 2][:, :], ACT.Copy).then_inc(u_ready.sem, 1)

                        for n in range(9):
                            bank_copy(n)
                        for x in range(-2, NI + 2):
                            if 0 <= x + 1 < NI:
                                exps(x + 1)
                            if 0 <= x < NI:
                                copy(x)
                            for hh in range(2):
                                if x == 6 * hh + 5:
                                    act.wait_ge(weight_arg.sem, weight_arg.at(hh + 1))
                                    arg = small[:, 48 * hh + 24:48 * hh + 36]
                                    act.activation(arg, arg, ACT.Exp).then_inc(decay_ready.sem, 1)
                            if x in finals:
                                k = finals[x]
                                act.wait_ge(pair_ready.sem, pair_ready.at(final_no[k] + 1))
                                act.activation(o_hi[:, k, :], bank[7][:, :], ACT.Copy).then_inc(rounded.sem, 1)

                    @block.vector
                    def _(dve):
                        ch = Chain(dve, dve_chain)

                        def top(x):
                            kind, h, y = items[x]
                            G = parts[kind]
                            sc, b = SC[:, x % RING, :], bank[(0, 1, 6)[x % 3]][:, :]
                            by_part = lambda ap: ap.rearrange("p (g s) -> p g s", g=G)
                            dve.wait_ge(psum_ready.sem, psum_ready.at(x + 1))
                            dve.wait_ge(masked.sem, masked.at(x - RING + 1))
                            if x in biased:
                                bs = bias_loaded[x % RING]
                                dve.wait_ge(bs.sem, bs.at(16 * (x // RING + 1)))
                                ins = dve.scalar_tensor_tensor(out=sc, in0=b, scalar=SCALE, in1=bias[:, x % RING, :],
                                                               op0=ALU.mult, op1=ALU.add)
                            else:
                                ins = dve.tensor_scalar(sc, b, SCALE, None, ALU.mult)
                            ins.then_inc(score_ready.sem, 1)
                            dve.wait_ge(score_ready.sem, score_ready.at(x + 1))
                            dve.tensor_reduce(sums_of(x)[0], by_part(sc), AX_X, ALU.max, negate=True).then_inc(frame_ready.sem, 1)

                        def out(x):
                            kind, h, y = items[x]
                            o = bank[4 + x % 2]
                            if x < NB:
                                dve.wait_ge(attended.sem, attended.at(x + 1))
                                at, w = (y, 1) if kind == "n" else (4 * y, 4)
                                dve.tensor_scalar(groups[:, at:at + w, :], o[:, 0:64 * w].rearrange("p (g f) -> p g f", f=64),
                                                  1.0, None, ALU.mult).then_inc(h_ready.sem, 1)
                                return
                            den = sums_of(x)[1]
                            dve.wait_ge(weight_ready.sem, weight_ready.at(x + 1))
                            ch.add(dve.reciprocal(den, den))
                            ch.wait()
                            dve.wait_ge(attended.sem, attended.at(x + 1))
                            f = 64 * h if kind == "a" else 384 + 64 * h
                            dve.tensor_tensor(O[:, 2 * y:2 * y + 2, f:f + 64], o[:, 0:P].rearrange("p (v f) -> p v f", f=64),
                                              den.unsqueeze(2).broadcast_to([P, 2, 64]), ALU.mult).then_inc(h_ready.sem, 1)

                        def group_frame(hh):
                            neg, arg = small[:, 48 * hh:48 * hh + 12], small[:, 48 * hh + 24:48 * hh + 36]
                            low = small[:, 48 * hh + 36:48 * hh + 40]
                            dve.wait_ge(frame_ready.sem, frame_ready.at(6 * hh + 6))
                            ch.add(dve.tensor_tensor(low, neg[:, 0:4], neg[:, 4:8], ALU.min))
                            ch.wait()
                            ch.add(dve.tensor_tensor(low, low, neg[:, 8:12], ALU.min))
                            ch.wait()
                            dve.tensor_tensor(arg.rearrange("p (g r) -> p g r", g=3), low.unsqueeze(1).broadcast_to([P, 3, 4]),
                                              neg.rearrange("p (g r) -> p g r", g=3), ALU.subtract).then_inc(weight_arg.sem, 1)

                        def group_merge(hh):
                            den, arg = small[:, 48 * hh + 12:48 * hh + 24], small[:, 48 * hh + 24:48 * hh + 36]
                            z = small[:, 48 * hh + 40:48 * hh + 44]
                            by_group = lambda ap: ap.rearrange("p (g r) -> p g r", g=3)
                            dve.wait_ge(decay_ready.sem, decay_ready.at(hh + 1))
                            dve.wait_ge(weight_ready.sem, weight_ready.at(6 * hh + 6))
                            ch.add(dve.tensor_tensor(den, den, arg, ALU.mult))
                            ch.wait()
                            ch.add(dve.tensor_reduce(z, den.rearrange("p (g r) -> p r g", g=3), AX_X, ALU.add))
                            ch.wait()
                            ch.add(dve.reciprocal(z, z))
                            ch.wait()
                            ch.add(dve.tensor_tensor(by_group(arg), by_group(arg), z.unsqueeze(1).broadcast_to([P, 3, 4]), ALU.mult))
                            ch.wait()
                            dve.wait_ge(h_ready.sem, h_ready.at(6 * hh + 6))
                            ch.add(dve.tensor_tensor(groups[:, :, :], groups[:, :, :], arg.unsqueeze(2).broadcast_to([P, 12, 64]), ALU.mult))
                            ch.wait()
                            ob = OB[:, :, 64 * hh:64 * hh + 64]
                            ch.add(dve.tensor_tensor(ob, groups[:, 0:4, :], groups[:, 4:8, :], ALU.add))
                            ch.wait()
                            dve.tensor_tensor(ob, ob, groups[:, 8:12, :], ALU.add).then_inc(y_ready.sem, 1)

                        for x in range(-2, NI + 3):
                            if x + 2 < NI:
                                top(x + 2)
                            if 0 <= x - 1 < NI:
                                out(x - 1)
                            for hh in range(2):
                                if x == 6 * hh + 4:
                                    group_frame(hh)
                                if x == 6 * hh + 6:
                                    group_merge(hh)
                            if x - 1 in finals:
                                k = finals[x - 1]
                                dve.wait_ge(rounded.sem, rounded.at(final_no[k] + 1))
                                dve.tensor_tensor(o_lo[:, k, :], bank[7][:, :], o_hi[:, k, :].bitcast(F32),
                                                  ALU.subtract).then_inc(z_ready.sem, 1)
                for x in biased:
                    bias_loaded[x % RING].advance(16)
                end_stage(vt_psum=9, vt_ready=9, score_ready=NI, psum_ready=NI, u_ready=NI, masked=NI, attended=NI, h_ready=NI,
                          frame_ready=NI, weight_ready=NI, weight_arg=2, decay_ready=2, y_ready=2, pair_ready=6, rounded=6,
                          z_ready=6, dve_chain=(NI - NB) + 2 * 8)

        def gated_merge(l, o_hi, o_lo, work, factor):
            n0 = c_next[0]
            NP = KT // 2
            n1 = n0 + 4 * NP
            c_next[0] = n1 + NP
            with ExitStack() as scope:
                GR = 12
                G = sb(f"g{l}_gates", [P, GR, S], F32, scope)
                y_hi = sb(f"g{l}_y_hi", [P, KT, S], F32R, scope)
                y_lo = sb(f"g{l}_y_lo", [P, KT, S], F32R, scope)
                mg, part = work[:, 0:2, :], work[:, 2:4, :]
                hi, lo = x_parts()
                branch_banks = ((4, 5, 6), (7, 2, 3))
                branch_tiles = (range(0, 3), range(3, 4), range(4, 6))
                chunks = 5 * NP

                with nc.Block() as block:
                    @block.sync
                    def _(sp):
                        for j in range(chunks):
                            ahead(fetch, sp, n0, chunks, 2)(j // 2, j % 2)

                    @block.tensor
                    def _(pe):
                        for j in range(NP):
                            for g in range(3):
                                c = n0 + 4 * j + g
                                pe.wait_ge(lo_ready.sem, PRIME + c + 1)
                                pe.wait_ge(gates_ready.sem, gates_ready.at(3 * j + (0, -1, 1)[g]))
                                if g == 1:
                                    pe.wait_ge(y_ready.sem, y_ready.at(2 * j))
                                b = 2 * (g % 2)
                                linear(pe, bank[b][:, :], c % 2, 0, range(KT), hi, lo)
                                linear(pe, bank[b + 1][:, :], c % 2, KT * P, range(KT), hi, lo).then_inc(chunk_used.sem, 1)
                            c = n0 + 4 * j + 3
                            pe.wait_ge(lo_ready.sem, PRIME + c + 1)
                            for v in range(2):
                                pe.wait_ge(y_ready.sem, y_ready.at(2 * j + v - 1))
                                if v:
                                    pe.wait_ge(gates_ready.sem, gates_ready.at(3 * j + 2))
                                for x, ks in enumerate(branch_tiles):
                                    mm = linear(pe, bank[branch_banks[v][x]][:, :], c % 2, (6 * v + ks[0]) * P, ks,
                                                lambda k: o_hi[:, k, :], lambda k: o_lo[:, k, :])
                                mm.then_inc((psum_ready if v == 0 else chunk_used).sem, 1)
                        for j in range(NP):
                            c = n1 + j
                            u = j % 2
                            pe.wait_ge(lo_ready.sem, PRIME + c + 1)
                            if j == 0:
                                pe.wait_ge(gates_ready.sem, gates_ready.at(3 * NP))
                                for k in range(KT):
                                    pe.wait_ge(split_ready.sem, split_ready.at(k + 1))
                                    for v in range(2):
                                        mm = linear(pe, bank[v][:, :], c % 2, (v * KT + k) * P, [k], lambda i: y_hi[:, i, :],
                                                    lambda i: y_lo[:, i, :], first=k == 0, last=k == KT - 1)
                                        if k == KT - 1:
                                            mm.then_inc((frame_ready if v == 0 else chunk_used).sem, 1)
                                continue
                            if j >= 2:
                                pe.wait_ge(z_ready.sem, z_ready.at(2 * j - 2))
                            for v in range(2):
                                mm = linear(pe, bank[2 * u + v][:, :], c % 2, v * KT * P, range(KT),
                                            lambda k: y_hi[:, k, :], lambda k: y_lo[:, k, :])
                                mm.then_inc((frame_ready if v == 0 else chunk_used).sem, 1)
                        finish_tensor(pe, work)

                    @block.scalar
                    def _(act):
                        split = ahead(split_hi, act, n0, chunks, 1)

                        def round_(n):
                            act.wait_ge(y_ready.sem, y_ready.at(n + 1))
                            act.activation(y_hi[:, n, :], mg[:, n % 2, :], ACT.Copy).then_inc(rounded.sem, 1)

                        for j in range(NP):
                            for g in range(3):
                                i = 4 * j + g
                                split(i // 2, i % 2)
                                act.wait_ge(gates_ready.sem, gates_ready.at(3 * j + g + 1))
                                for v in range(2):
                                    k = 6 * j + 2 * g + v
                                    ins = act.activation(G[:, k % GR, :], G[:, k % GR, :], ACT.Sigmoid,
                                                         bias=col("b_gate_2", l * 24 + k % 3 * KT + k // 3))
                                ins.then_inc(act_ready.sem, 1)
                                if j and g < 2:
                                    round_(2 * j - 2 + g)
                            i = 4 * j + 3
                            split(i // 2, i % 2)
                        for n in range(KT - 2, KT):
                            round_(n)
                        for j in range(NP):
                            i = 4 * NP + j
                            split(i // 2, i % 2)
                            for v in range(2):
                                if v == 0:
                                    act.wait_ge(frame_ready.sem, frame_ready.at(j + 1))
                                else:
                                    act.wait_ge(chunk_used.sem, PRIME + n1 + j + 1)
                                finish_scalar(act, work, 2 * j + v, bank[2 * (j % 2) + v])
                        factor_scalar(act, FACTOR, bank[7][:, :])

                    @block.vector
                    def _(dve):
                        ch = Chain(dve, dve_chain)
                        split = ahead(split_lo, dve, n0, chunks, 1)
                        for j in range(NP):
                            for g in range(4):
                                i = 4 * j + g
                                split(i // 2, i % 2)
                                if g == 3:
                                    break
                                dve.wait_ge(chunk_used.sem, PRIME + n0 + i + 1)
                                if j >= 2:
                                    dve.wait_ge(y_ready.sem, y_ready.at(2 * j - 2))
                                for v in range(2):
                                    ins = dve.tensor_tensor(G[:, (6 * j + 2 * g + v) % GR, :], bank[2 * (g % 2) + v][:, :],
                                                            factor[:, :], ALU.mult)
                                ins.then_inc(gates_ready.sem, 1)
                            dve.wait_ge(act_ready.sem, act_ready.at(3 * j + 3))
                            for v in range(2):
                                n = 2 * j + v
                                if v == 0:
                                    dve.wait_ge(psum_ready.sem, psum_ready.at(j + 1))
                                else:
                                    dve.wait_ge(chunk_used.sem, PRIME + n0 + 4 * j + 4)
                                dve.wait_ge(split_ready.sem, split_ready.at(n - 1))
                                m, q = mg[:, v, :], part[:, v, :]
                                b = [bank[x][:, :] for x in branch_banks[v]]
                                gate = [G[:, (3 * n + x) % GR, :] for x in range(3)]
                                ch.add(dve.tensor_tensor(m, b[0], gate[0], ALU.mult))
                                ch.add(dve.tensor_tensor(q, b[1], gate[1], ALU.mult))
                                ch.wait()
                                ch.add(dve.tensor_tensor(m, m, q, ALU.add))
                                ch.wait()
                                ch.add(dve.tensor_tensor(q, b[2], gate[2], ALU.mult))
                                ch.wait()
                                dve.tensor_tensor(m, m, q, ALU.add).then_inc(y_ready.sem, 1)
                        for j in range(NP):
                            i = 4 * NP + j
                            split(i // 2, i % 2)

                    @block.gpsimd
                    def _(pool):
                        for n in range(KT):
                            pool.wait_ge(rounded.sem, rounded.at(n + 1))
                            pool.tensor_tensor(y_lo[:, n, :], mg[:, n % 2, :], y_hi[:, n, :].bitcast(F32),
                                               ALU.subtract).then_inc(split_ready.sem, 1)
                        finish_pool(pool, work)
                end_stage(act_ready=3 * NP, gates_ready=3 * NP, psum_ready=NP, y_ready=KT, rounded=KT, split_ready=KT, frame_ready=NP,
                          dve_chain=4 * KT, **FINISH)


        def conv_ffn(l, work, post):
            n0 = c_next[0]
            n1 = n0 + FT
            c_next[0] = n1 + 2 * KT
            with ExitStack() as scope:
                g_hi = sb(f"c{l}_g_hi", [P, FT, S], F32R, scope)
                g_lo = sb(f"c{l}_g_lo", [P, FT, S], F32R, scope)
                ca, cb, prod = (work[:, 2 * n:2 * n + 2, :] for n in range(3))
                factor, acc = FACTOR, sum_tile
                hi, lo = x_parts()

                def ccol(name, n):
                    at = col_at[name] + n
                    return cols[:, bass.ds(at, 1)]

                with nc.Block() as block:
                    @block.sync
                    def _(sp):
                        for_chunks(sp, FT, ahead(fetch, sp, n0, FT, 2))
                        for_chunks(sp, 2 * KT, ahead(fetch, sp, n1, 2 * KT, 2))

                    @block.tensor
                    def _(pe):
                        def g_tile(g, n):
                            def tile(k):
                                if n == 0 and k == FT - 1:
                                    pe.wait_ge(rest_ready.sem, rest_ready.at(FT))
                                return g[:, k, :]
                            return tile

                        def up(i, u):
                            s, j = (n0 + u) % 2, i * 2 + u
                            pe.wait_ge(lo_ready.sem, j + (PRIME + n0 + 1))
                            pe.wait_ge(frame_ready.sem, frame_ready.at(-1) + j)
                            linear(pe, bank[2 * u][:, :], s, 0, range(KT), hi, lo)
                            linear(pe, bank[2 * u + 1][:, :], s, KT * P, range(KT), hi, lo)\
                                .then_inc(chunk_used.sem, 1)

                        start_tensor(pe, acc, n0)
                        up(0, 1)
                        with pe.Fori(1, FT // 2) as i:
                            up(i, 0)
                            up(i, 1)
                        for n in range(KT):
                            for u in range(2):
                                c = n1 + 2 * n + u
                                pe.wait_ge(lo_ready.sem, PRIME + c + 1)
                                if n >= 2 and u == 0:
                                    pe.wait_ge(z_ready.sem, z_ready.at(n - 1))
                                if n == 0:
                                    pe.wait_ge(rest_ready.sem, rest_ready.at(FH if u == 0 else FT - 1))
                                mm = linear(pe, bank[4 + n % 2][:, :], c % 2, 0, range(FH * u, FH * u + FH), g_tile(g_hi, n),
                                            g_tile(g_lo, n), first=u == 0, last=u == 1)
                                mm.then_inc(chunk_used.sem, 1)
                        finish_tensor(pe, work, 1)

                    @block.scalar
                    def _(act):
                        split = ahead(split_hi, act, n0, FT, 1)

                        def taps(i, u):
                            j = i * 2 + u
                            for n, (out, off, signal_) in enumerate(((ca, 0, conv_a), (cb, FT, conv_b))):
                                act.wait_ge(signal_.sem, signal_.at(1) + j * 2)
                                act.activation(out[:, u, :], bank[2 * u + n][:, :], ACT.Identity,
                                               bias=ccol("conv_b_2", l * 2 * FT + off + j),
                                               scale=ccol("conv_w_2", (l * 3 + 1) * 2 * FT + off + j)).then_inc(signal_.sem, 1)
                            act.wait_ge(frame_ready.sem, frame_ready.at(1) + j)
                            act.activation(ca[:, u, :], ca[:, u, :], ACT.Gelu_apprx_tanh).then_inc(act_ready.sem, 1)

                        def round_(i, u):
                            j = i * 2 + u
                            act.wait_ge(product_ready.sem, product_ready.at(1) + j)
                            act.activation(g_hi[:, j, :], prod[:, u, :], ACT.Copy).then_inc(rounded.sem, 1)

                        def body(i, u):
                            split(i, u)
                            taps(i, u)
                            round_(i + u - 1, 1 - u)

                        split(0, 0)
                        start_scalar(act, work, post, acc, "g_pre_ffn_2", l)
                        factor_scalar(act, factor, bank[7][:, :])
                        taps(0, 0)
                        body(0, 1)
                        with act.Fori(1, FT // 2 - 1) as i:
                            body(i, 0)
                            body(i, 1)
                        for u in range(2):
                            body(FT // 2 - 1, u)
                        round_(FT // 2 - 1, 1)
                        for n in range(KT):
                            for u in range(2):
                                ahead(split_hi, act, n1, 2 * KT, 1)(n, u)
                            act.wait_ge(chunk_used.sem, PRIME + n1 + 2 * n + 2)
                            finish_scalar(act, work, n, bank[4 + n % 2], 1)
                        factor_scalar(act, factor, bank[7][:, :], 2)

                    @block.vector
                    def _(dve):
                        split = ahead(split_lo, dve, n0, FT, 1)

                        def factors(i, u):
                            j = i * 2 + u
                            halves = ((ca, 2 * u, 0, conv_a), (cb, 2 * u + 1, FT, conv_b))
                            dve.wait_ge(chunk_used.sem, j + (PRIME + n0 + 1))
                            dve.wait_ge(product_ready.sem, product_ready.at(-1) + j)
                            for out, b, off, signal_ in halves:
                                dve.tensor_tensor(bank[b][:, :], bank[b][:, :], factor, ALU.mult).then_inc(signal_.sem, 1)

                        def outer(i, u):
                            j = i * 2 + u
                            halves = ((ca, 2 * u, 0, conv_a), (cb, 2 * u + 1, FT, conv_b))
                            for out, b, off, signal_ in halves:
                                o, p = out[:, u, :], bank[b]
                                dve.wait_ge(signal_.sem, signal_.at(2) + j * 2)
                                dve.scalar_tensor_tensor(out=o[:, 1:S], in0=p[:, 0:S - 1], in1=o[:, 1:S], op0=ALU.mult,
                                                         scalar=ccol("conv_w_2", (l * 3) * 2 * FT + off + j),
                                                         op1=ALU.add).then_inc(part_ready.sem, 1)
                            for n, (out, b, off, signal_) in enumerate(halves):
                                o, p = out[:, u, :], bank[b]
                                dve.wait_ge(part_ready.sem, part_ready.at(1 + n) + j * 2)
                                ins = dve.scalar_tensor_tensor(out=o[:, 0:S - 1], in0=p[:, 1:S], in1=o[:, 0:S - 1],
                                                               scalar=ccol("conv_w_2", (l * 3 + 2) * 2 * FT + off + j),
                                                               op0=ALU.mult, op1=ALU.add)
                            ins.then_inc(frame_ready.sem, 1)

                        def product(i, u):
                            j = i * 2 + u
                            dve.wait_ge(act_ready.sem, act_ready.at(1) + j)
                            dve.wait_ge(rest_ready.sem, rest_ready.at(-1) + j)
                            dve.tensor_tensor(prod[:, u, :], ca[:, u, :], cb[:, u, :], ALU.mult)\
                                .then_inc(product_ready.sem, 1)

                        def body(i, u):
                            split(i, u)
                            factors(i, u)
                            product(i + u - 1, 1 - u)
                            outer(i, u)

                        start_vector(dve, work, post, acc)
                        split(0, 0)
                        dve.wait_ge(scale_ready.sem, scale_ready.at(2))
                        factors(0, 0)
                        outer(0, 0)
                        body(0, 1)
                        with dve.Fori(1, FT // 2 - 1) as i:
                            body(i, 0)
                            body(i, 1)
                        for u in range(2):
                            body(FT // 2 - 1, u)
                        product(FT // 2 - 1, 1)
                        for_chunks(dve, 2 * KT, ahead(split_lo, dve, n1, 2 * KT, 1))

                    @block.gpsimd
                    def _(pool):
                        start_pool(pool, work)
                        def body(i, u):
                            j = i * 2 + u
                            pool.wait_ge(rounded.sem, rounded.at(KT + 1) + j)
                            pool.tensor_tensor(g_lo[:, j, :], prod[:, u, :], g_hi[:, j, :].bitcast(F32),
                                               ALU.subtract).then_inc(rest_ready.sem, 1)

                        for_chunks(pool, FT, body)
                        finish_pool(pool, work, 1)
            counts = {name: start_counts(post).get(name, 0) + FINISH.get(name, 0) for name in {**start_counts(post), **FINISH}}
            counts["rounded"] += FT
            end_stage(frame_ready=FT, act_ready=FT, product_ready=FT, rest_ready=FT, conv_a=2 * FT, conv_b=2 * FT, part_ready=2 * FT, **counts)

        def finish(work, post):
            with nc.Block() as block:
                @block.vector
                def _(dve):
                    start_vector(dve, work, post, None)

                @block.sync
                def _(sp):
                    for k in range(KT):
                        sp.wait_ge(x_ready.sem, x_ready.at(k + 1))
                        sp.dma_start(t["out"][:, k, :], X[:, k, :]).then_inc(stores_done, 16)
                    sp.wait_ge(stores_done, 16 * KT)


        stages = []
        for l in range(DEPTH):
            stages.append(lambda l=l: swiglu(l, 0))
            stages.append(lambda l=l: even_mixer(l) if l % 2 == 0 else odd_mixer(l))
            stages.append(lambda l=l: swiglu(l, 2))
        for st in stages:
            st()
        first_block.close()
        work = sb("work", [P, KT, S])
        post = ("ln", None)
        layers = []
        for l in range(DEPTH):
            layers.append((attention, l, "g_post_mix_2"))
            layers.append((conv_ffn, l, "g_post_ffn_2"))
        for layer, l, gain in layers:
            layer(l, work, post)
            post = (gain, l)
        finish(work, post)


def block_diagonal(w):
    out = np.zeros((P, 4, P), np.float32)
    for b in range(8):
        at = 64 * (b % 2)
        out[at:at + 64, b // 2, at:at + 64] = w[b]
    return out


MASKED = -1e30


def lay_out_rpb(rpb):
    tile, first = np.arange(4), np.array([0, 8, 24, 32])
    c, r, kc, kr = np.ogrid[:16, :8, :32, :8]
    parts = []
    for n in tile:
        col, key = 16 * n + c, first[n] + kc
        start = np.clip(col - 8, 0, 48)
        seen = np.broadcast_to((key >= start) & (key < start + 16), (16, 8, 32, 8))
        at = np.broadcast_to(kr - r + 7, seen.shape), np.where(seen, key - col + 15, 0)
        part = np.where(seen, rpb[:, :, at[0], at[1]], np.float32(MASKED)).astype(rpb.dtype)
        parts.append(part.reshape(DEPTH, 6, P, 256))
    out = np.stack(parts, 2).reshape(DEPTH, 6, 2, 2, P, 256)
    return np.ascontiguousarray(out.transpose(0, 1, 2, 4, 3, 5)).reshape(DEPTH, 6, 2, P, 512)


def slopes():
    return (2.0 ** (-8.0 * np.arange(1, 7, dtype=np.float32) / 6)).astype(np.float32)


def dilated_bias():
    key, n = np.arange(S), np.arange(P)
    apart = np.abs(n[:, None] - n[None, :])
    out = []
    for h in range(2):
        for r in range(4):
            far = np.abs(key[None, :] - (4 * n + r)[:, None])
            out.append(np.where(far <= 64, -slopes()[h] * far, MASKED))
        for g, seen in ((1, apart <= 64), (2, apart % 4 == 0)):
            out.append(np.tile(np.where(seen, -slopes()[2 * g + h] * 4 * apart, MASKED), (1, 4)))
    return np.stack(out).astype(np.float32)


def lay_out(i):
    return {"weights": lay_out_weights(i), "cols": lay_out_columns(i),
            "consts": np.ascontiguousarray(np.stack(list(constants().values()), 1)),
            "x": np.ascontiguousarray(np.asarray(i["x"])[0].T.reshape(KT, P, S).transpose(1, 0, 2)),
            "rg_w": np.concatenate([block_diagonal(i["rg_wa"][0]), block_diagonal(i["rg_wx"][0])], 1),
            "masks": odd_masks(), "gla_gB": i["gla_gB"][0],
            "mem": np.ascontiguousarray(np.asarray(i["mem_2"])[0].T.reshape(KT, P, 256).transpose(1, 0, 2)),
            "rpb": lay_out_rpb(np.asarray(i["rpb_na_2"])), "dilated": dilated_bias(),
            "rk_lora": np.concatenate([i["rk_wB"][0], i["rk_aB"][0], i["rk_gB"][0]], 0)}


def kernel(**inputs):
    from concourse import bacc
    from concourse.bass_utils import run_bass_kernel_spmd

    arrays = lay_out({name: np.asarray(a) for name, a in inputs.items()})
    nc = bacc.Bacc("TRN2", target_bir_lowering=False, num_devices=1)
    t = {}
    for name, a in arrays.items():
        t[name] = nc.dram_tensor(f"in_{name}", a.shape, mybir.dt.from_np(a.dtype), kind="ExternalInput").ap()
    t["out"] = nc.dram_tensor("out_x", (P, KT, S), F32, kind="ExternalOutput").ap()
    program(nc, t)
    got = run_bass_kernel_spmd(nc, [{f"in_{name}": a for name, a in arrays.items()}], core_ids=[0])
    x = np.asarray(got.results[0]["out_x"])
    return np.ascontiguousarray(x.transpose(1, 0, 2).reshape(D, S).T[None])
```
